# Optimizing a Trainium2 kernel written in Bass

```python
import math
import jax, jax.numpy as jnp
from jax import lax
import numpy as np

D_MODEL = 1024
BATCH = 1
SEQ = 1024
DEPTH = 1
DEC_BATCH = 1
DEC_SEQ = 32
PAST_LEN = 1024

CHUNK = 64
EPS = 1e-6
D_CONV = D_MODEL
CONV_W = 3
N_HEADS = 8
HEAD_DIM = 64
V_DIM = 2 * HEAD_DIM
QK_WIDTH = N_HEADS * 2 * HEAD_DIM
ATTN_WIDTH = N_HEADS * V_DIM
ROPE_THETA = 10000.0
Q_BLOCK = 128
IN_SPLITS = [D_CONV, 2 * D_CONV, 3 * D_CONV,
             3 * D_CONV + QK_WIDTH,
             3 * D_CONV + 2 * QK_WIDTH,
             3 * D_CONV + 2 * QK_WIDTH + ATTN_WIDTH]
IN_WIDTH = 3 * D_CONV + 2 * QK_WIDTH + ATTN_WIDTH + 2 * D_MODEL
N_KEYS = 128
N_EXPERTS = N_KEYS * N_KEYS
PEER_HEADS = 8
PEER_TOPK = 16
D_KEY = 256
PEER_BLOCK = 128

kernel_name = 'hybrid_conv_diffattn_peer_stream_step'

def lambda_init(layer_idx):
    return 0.8 - 0.6 * math.exp(-0.3 * layer_idx)

def rmsnorm(x, g):
    xf = x.astype(jnp.float32)
    r = lax.rsqrt(jnp.mean(xf * xf, axis=-1, keepdims=True) + EPS)
    return (xf * r).astype(x.dtype) * g

def rope(x, pos):
    half = HEAD_DIM // 2
    inv = ROPE_THETA ** (-jnp.arange(half, dtype=jnp.float32) / half)
    ang = pos.astype(jnp.float32)[:, None] * inv[None, :]
    cos = jnp.cos(ang)[:, None, None, :].astype(x.dtype)
    sin = jnp.sin(ang)[:, None, None, :].astype(x.dtype)
    x1, x2 = x[..., :half], x[..., half:]
    return jnp.concatenate([x1 * cos - x2 * sin, x2 * cos + x1 * sin], axis=-1)

def conv_branch(bg, cg, hh, conv_w, conv_state):
    u = cg * hh
    up = jnp.concatenate([conv_state, u], axis=1)
    T = u.shape[1]
    y = sum(conv_w[j] * up[:, j:j + T] for j in range(CONV_W))
    return bg * y, up[:, -(CONV_W - 1):]

def diff_attn_block(q, k, v, q_pos, k_pos, lam):
    s = jnp.einsum('bqhcd,bkhcd->bhcqk', q, k).astype(jnp.float32) * (HEAD_DIM ** -0.5)
    visible = k_pos[None, :] < (q_pos[:, None] // CHUNK + 1) * CHUNK
    s = jnp.where(visible, s, -jnp.inf)
    p = jax.nn.softmax(s, axis=-1)
    a = p[:, :, 0] - lam * p[:, :, 1]
    return jnp.einsum('bhqk,bkhe->bqhe', a.astype(v.dtype), v)

def peer_ffn(xt, wq, q_g, subkeys, u, v):
    n = xt.shape[0]
    q = rmsnorm((xt @ wq).reshape(n, PEER_HEADS, D_KEY), q_g)
    q = q.reshape(n, PEER_HEADS, 2, D_KEY // 2)
    s = jnp.einsum('nhcd,ckd->nhck', q, subkeys).astype(jnp.float32)
    s_top, i_top = lax.top_k(s, PEER_TOPK)
    cand = s_top[:, :, 0, :, None] + s_top[:, :, 1, None, :]
    cand_idx = i_top[:, :, 0, :, None] * N_KEYS + i_top[:, :, 1, None, :]
    best, sel = lax.top_k(cand.reshape(n, PEER_HEADS, PEER_TOPK * PEER_TOPK), PEER_TOPK)
    experts = jnp.take_along_axis(cand_idx.reshape(n, PEER_HEADS, -1), sel, axis=-1)
    g = jax.nn.softmax(best, axis=-1).reshape(n, -1)
    e = experts.reshape(n, -1)
    ue = jnp.take(u, e, axis=0)
    h = jax.nn.gelu(jnp.einsum('nkd,nd->nk', ue, xt), approximate=False)
    ve = jnp.take(v, e, axis=0)
    return jnp.einsum('nk,nkd->nd', (g * h).astype(xt.dtype), ve)

def trunk_layer(x, pos, conv_state, k_past, v_past, w, lam_init):
    (norm1_g, w_in, b_gate, conv_w, q_norm_g, k_norm_g, lam_q1, lam_k1, lam_q2, lam_k2,
     subln_g, w_conv_out, w_attn_out, w_o, norm2_g, peer_wq, peer_q_g, peer_subkeys,
     peer_u, peer_v) = w
    B, T, _ = x.shape
    xn = rmsnorm(x, norm1_g)
    z = xn @ w_in
    hb, hc, hh, q, k, v, gz = jnp.split(z, IN_SPLITS, axis=-1)
    conv_y, new_conv = conv_branch(hb, hc, hh, conv_w, conv_state)
    q = rope(rmsnorm(q.reshape(B, T, N_HEADS, 2, HEAD_DIM), q_norm_g), pos)
    k = rope(rmsnorm(k.reshape(B, T, N_HEADS, 2, HEAD_DIM), k_norm_g), pos)
    v = v.reshape(B, T, N_HEADS, V_DIM)
    lam = (jnp.exp(jnp.sum(lam_q1.astype(jnp.float32) * lam_k1.astype(jnp.float32)))
           - jnp.exp(jnp.sum(lam_q2.astype(jnp.float32) * lam_k2.astype(jnp.float32)))
           + lam_init)
    if k_past is None:
        k_pos = pos
        nb = T // Q_BLOCK
        qb = jnp.moveaxis(q.reshape(B, nb, Q_BLOCK, N_HEADS, 2, HEAD_DIM), 1, 0)
        pb = pos.reshape(nb, Q_BLOCK)
        o = lax.map(lambda a: diff_attn_block(a[0], k, v, a[1], k_pos, lam), (qb, pb))
        o = jnp.moveaxis(o, 0, 1).reshape(B, T, N_HEADS, V_DIM)
    else:
        k_all = jnp.concatenate([k_past, k], axis=1)
        v_all = jnp.concatenate([v_past, v], axis=1)
        k_pos = jnp.arange(k_all.shape[1], dtype=jnp.int32)
        o = diff_attn_block(q, k_all, v_all, pos, k_pos, lam)
    o = (rmsnorm(o, subln_g) * (1.0 - lam_init)).reshape(B, T, ATTN_WIDTH)
    gates = jax.nn.sigmoid(gz.reshape(B, T, 2, D_MODEL) + b_gate)
    mix = gates[:, :, 0] * (conv_y @ w_conv_out) + gates[:, :, 1] * (o @ w_attn_out)
    x = x + mix @ w_o
    xn2 = rmsnorm(x, norm2_g)
    if k_past is None:
        blocks = xn2.reshape(-1, PEER_BLOCK, D_MODEL)
        f = lax.map(lambda t: peer_ffn(t, peer_wq, peer_q_g, peer_subkeys, peer_u, peer_v), blocks)
    else:
        f = peer_ffn(xn2.reshape(-1, D_MODEL), peer_wq, peer_q_g, peer_subkeys, peer_u, peer_v)
    x = x + f.reshape(B, T, D_MODEL)
    return x, k, v, new_conv

def setup_inputs(seed: int = 0) -> dict:
    key = jax.random.key(seed)
    ks = jax.random.split(key, 24)
    L = DEPTH
    nrm = lambda k, shape, scale: jax.random.normal(k, shape, jnp.float32) * scale
    return {
        'x_prompt': nrm(ks[0], (BATCH, SEQ, D_MODEL), 1.0),
        'x_sample': nrm(ks[1], (DEC_BATCH, DEC_SEQ, D_MODEL), 1.0),
        'cache_k': nrm(ks[2], (L, DEC_BATCH, PAST_LEN, N_HEADS, 2, HEAD_DIM), 1.0),
        'cache_v': nrm(ks[3], (L, DEC_BATCH, PAST_LEN, N_HEADS, V_DIM), 1.0),
        'state_conv': nrm(ks[4], (L, DEC_BATCH, CONV_W - 1, D_CONV), 1.0),
        'norm1_g': 1.0 + nrm(ks[5], (L, D_MODEL), 0.02),
        'w_in': nrm(ks[6], (L, D_MODEL, IN_WIDTH), D_MODEL ** -0.5),
        'b_gate': nrm(ks[7], (L, 2, D_MODEL), 0.02),
        'conv_w': nrm(ks[8], (L, CONV_W, D_CONV), CONV_W ** -0.5),
        'q_norm_g': 1.0 + nrm(ks[9], (L, HEAD_DIM), 0.02),
        'k_norm_g': 1.0 + nrm(ks[10], (L, HEAD_DIM), 0.02),
        'lam_q1': nrm(ks[11], (L, HEAD_DIM), 0.1),
        'lam_k1': nrm(ks[12], (L, HEAD_DIM), 0.1),
        'lam_q2': nrm(ks[13], (L, HEAD_DIM), 0.1),
        'lam_k2': nrm(ks[14], (L, HEAD_DIM), 0.1),
        'subln_g': 1.0 + nrm(ks[15], (L, V_DIM), 0.02),
        'w_conv_out': nrm(ks[16], (L, D_CONV, D_MODEL), D_CONV ** -0.5),
        'w_attn_out': nrm(ks[17], (L, ATTN_WIDTH, D_MODEL), ATTN_WIDTH ** -0.5),
        'w_o': nrm(ks[18], (L, D_MODEL, D_MODEL), D_MODEL ** -0.5),
        'norm2_g': 1.0 + nrm(ks[19], (L, D_MODEL), 0.02),
        'peer_wq': nrm(ks[20], (L, D_MODEL, PEER_HEADS * D_KEY), D_MODEL ** -0.5),
        'peer_q_g': 1.0 + nrm(ks[21], (L, D_KEY), 0.02),
        'peer_subkeys': nrm(ks[22], (L, 2, N_KEYS, D_KEY // 2), (D_KEY // 2) ** -0.5),
        'peer_u': nrm(jax.random.fold_in(ks[23], 0), (L, N_EXPERTS, D_MODEL), D_MODEL ** -0.5),
        'peer_v': nrm(jax.random.fold_in(ks[23], 1), (L, N_EXPERTS, D_MODEL), PEER_HEADS ** -0.5),
    }

def reference(x_prompt, x_sample, cache_k, cache_v, state_conv, norm1_g, w_in, b_gate, conv_w,
              q_norm_g, k_norm_g, lam_q1, lam_k1, lam_q2, lam_k2, subln_g, w_conv_out,
              w_attn_out, w_o, norm2_g, peer_wq, peer_q_g, peer_subkeys, peer_u, peer_v):
    y_p, y_s = x_prompt, x_sample
    past_len = cache_k.shape[2]
    pos_p = jnp.arange(x_prompt.shape[1], dtype=jnp.int32)
    pos_s = past_len + jnp.arange(x_sample.shape[1], dtype=jnp.int32)
    kp, vp, cp, ksm, vsm, csm = [], [], [], [], [], []
    for l in range(DEPTH):
        w = (norm1_g[l], w_in[l], b_gate[l], conv_w[l], q_norm_g[l], k_norm_g[l], lam_q1[l],
             lam_k1[l], lam_q2[l], lam_k2[l], subln_g[l], w_conv_out[l], w_attn_out[l], w_o[l],
             norm2_g[l], peer_wq[l], peer_q_g[l], peer_subkeys[l], peer_u[l], peer_v[l])
        lam0 = lambda_init(l)
        zero_conv = jnp.zeros((x_prompt.shape[0], CONV_W - 1, D_CONV), x_prompt.dtype)
        y_p, k_new, v_new, c_new = trunk_layer(y_p, pos_p, zero_conv, None, None, w, lam0)
        kp.append(k_new); vp.append(v_new); cp.append(c_new)
        y_s, k_new, v_new, c_new = trunk_layer(y_s, pos_s, state_conv[l], cache_k[l], cache_v[l], w, lam0)
        ksm.append(k_new); vsm.append(v_new); csm.append(c_new)
    return (y_p, y_s, jnp.stack(kp), jnp.stack(vp), jnp.stack(cp),
            jnp.stack(ksm), jnp.stack(vsm), jnp.stack(csm))


_drawn_inputs = setup_inputs


def setup_inputs(seed=0):
    import zlib

    import numpy as np

    out = dict(_drawn_inputs(seed))
    spreads = {}
    factors = {'b_gate': 4.938, 'q_norm_g': 3.45, 'subln_g': 9.822, 'norm2_g': 4.022, 'peer_q_g': 11.8}
    for name, (base, spread) in spreads.items():
        noise = np.random.default_rng([zlib.crc32(name.encode()), seed]).standard_normal(out[name].shape)
        drawn = base * np.exp(spread * noise) if base else spread * noise
        out[name] = __import__('jax').numpy.asarray(drawn.astype(out[name].dtype))
    for name, factor in factors.items():
        out[name] = (out[name] * factor).astype(out[name].dtype)
    return out
```

```python
from contextlib import ExitStack

import numpy as np
import concourse.bass as bass
from concourse import mybir

F32 = mybir.dt.float32
U32 = mybir.dt.uint32
ALU = mybir.AluOpType
ACT = mybir.ActivationFunctionType
AX = mybir.AxisListType
ds = bass.ds

P = 128
D = 1024
DC = D // P
SEQ, DEC = 1024, 32
ROWS = SEQ + DEC
NT = SEQ // P
PAST = 1024
HEADS = 8
HD = 64
VD = 128
GROUPS = 4
GW = 2 * VD
CHUNK = 64
EPS = 1e-6
LAM0 = 0.8 - 0.6
QKS = HD ** -0.5
LOW = -3.0e38
PART = ROWS // 3
QCOL, KCOL, VCOL = 3 * D, 4 * D, 5 * D
GACOL, GBCOL = 6 * D, 7 * D
TOPK = 16
NKEYS = 128
PH = 8
PQ = 2048
SLOTS = PH * TOPK
RING = 16


def rows_of(t):
    return DEC if isinstance(t, int) and t == NT else P


def hold(eng, sem, value, passed):
    eng.wait_ge(sem, value)
    if not isinstance(value, int):
        eng.sem_inc(passed, 1)


def semaphores(ctx, nc, block, names):
    return {n: ctx.enter_context(nc.semaphore(f"{block}_{n}")) for n in names.split()}


def build_norm1(nc, A, keep):
    with ExitStack() as ctx:
        def sb(name, shape, dt=F32):
            return ctx.enter_context(nc.sbuf_tensor("n1_" + name, shape, dt))

        s = semaphores(ctx, nc, "n1", "consts x_in0 x_in1 sq_done r_done xn_done tr_done cpa cpd passed_pool ident_done "
                 "lam_d lam_e tab_done sp_ok passed_pe passed_act passed_dve")
        x_in = [s["x_in0"], s["x_in1"]]
        xt = sb("xt", [P, 2, D])
        xn = sb("xn", [P, 2, D])
        junk = sb("junk", [P, D])
        g1b = sb("g1b", [P, D])
        ss = sb("ss", [P, 2])
        rr = sb("rr", [P, 2])
        cosd = sb("cosd", [P, NT + 1, HD])
        sind = sb("sind", [P, NT + 1, HD])
        gains = sb("gains", [P, 4, HD])
        lamv = sb("lamv", [P, 4, HD])
        lamp = sb("lamp", [P, 2, HD])
        lamd = sb("lamd", [P, 2])
        lame = sb("lame", [P, 2])
        ps = [ctx.enter_context(nc.psum_tensor(f"n1_ps{b}", [P, 2, 512], F32)) for b in range(2)]
        block = ctx.enter_context(nc.Block())
        N_CONST = 1 + 2 + 6 + 4 + 1

        def x_rows(t):
            if isinstance(t, int) and t == NT:
                return A["x_sample"][0]
            return A["x_prompt"][0, ds(t * P, P), :]

        @block.sync
        def _(sp):
            def load(t, b):
                sp.wait_ge(s["xn_done"], t + 1)
                sp.dma_start(xt[:rows_of(t), b, :], x_rows(t)).then_inc(x_in[b], 16)

            with sp.Fori(0, NT // 2) as pair:
                for b in range(2):
                    load(pair * 2 + b, b)
            load(NT, 0)

        @block.scalar
        def _(act):
            act.dma_start(g1b[:], A["norm1_g"].to_broadcast([P, D])).then_inc(s["consts"], 16)
            act.dma_start(cosd[:], A["rope_cos"]).then_inc(s["consts"], 16)
            act.dma_start(sind[:], A["rope_sin"]).then_inc(s["consts"], 16)
            h = HD // 2
            for k, name in enumerate(("q_norm_g", "k_norm_g")):
                g = A[name]
                act.dma_start(gains[:, 2 * k, :], g.to_broadcast([P, HD])).then_inc(s["consts"], 16)
                act.dma_start(gains[:, 2 * k + 1, 0:h], g[:, h:HD].to_broadcast([P, h])).then_inc(s["consts"], 16)
                act.dma_start(gains[:, 2 * k + 1, h:HD], g[:, 0:h].to_broadcast([P, h])).then_inc(s["consts"], 16)
            for k, name in enumerate(("lam_q1", "lam_k1", "lam_q2", "lam_k2")):
                act.dma_start(lamv[:, k, :], A[name].to_broadcast([P, HD])).then_inc(s["consts"], 16)
            act.dma_start(keep["subg"][:], A["subln_g"].to_broadcast([P, VD])).then_inc(s["consts"], 16)

            def tile(t, b, turn):
                n = rows_of(t)
                act.wait_ge(x_in[b], 16 * turn)
                nc.scalar.activation(junk[:n, :], xt[:n, b, :], ACT.Square, scale=D ** -0.5,
                                     accum_out=ss[:n, b:b + 1]).then_inc(s["sq_done"], 1)
                hold(act, s["tr_done"], t + 3, s["passed_act"])
                nc.scalar.copy(keep["xnT"][:, 0:4, ds(t * P, n)],
                               ps[b][:, 0, :].rearrange("p (c r) -> p c r", c=4)[:, :, 0:n]).then_inc(s["cpa"], 1)

            act.sem_inc(s["cpa"], 2)
            with act.Fori(0, NT // 2) as pair:
                for b in range(2):
                    tile(pair * 2 + b, b, pair + 1)
            tile(NT, 0, NT // 2 + 1)
            act.wait_ge(s["lam_d"], 1)
            nc.scalar.activation(lame[:], lamd[:], ACT.Exp).then_inc(s["lam_e"], 1)

        @block.gpsimd
        def _(pool):
            ident = keep["ident"]
            nc.gpsimd.memset(ident[:], 0.0)
            nc.gpsimd.memset(keep["mhalf"][:], -0.5)
            pool.drain()
            nc.gpsimd.affine_select(out=ident[:], in_=ident[:], compare_op=ALU.not_equal, fill=1.0, base=0,
                                    pattern=[[-1, P]], channel_multiplier=1).then_inc(s["ident_done"], 1)

            def tile(t, b):
                n = rows_of(t)
                hold(pool, s["sq_done"], t + 1, s["passed_pool"])
                nc.gpsimd.tensor_scalar(rr[:n, b:b + 1], ss[:n, b:b + 1], EPS, None, ALU.add)
                pool.drain()
                nc.gpsimd.tensor_tensor(rr[:n, b:b + 1], rr[:n, b:b + 1], keep["mhalf"][:n, 0:1],
                                        ALU.pow).then_inc(s["r_done"], 1)

            with pool.Fori(0, NT // 2) as pair:
                for b in range(2):
                    tile(pair * 2 + b, b)
            tile(NT, 0)

        @block.vector
        def _(dve):
            dve.sem_inc(s["xn_done"], 2)
            dve.sem_inc(s["cpd"], 2)
            dve.wait_ge(s["consts"], 16 * N_CONST)

            def tile(t, b):
                n = rows_of(t)
                dve.wait_ge(s["tr_done"], t + 1)
                dve.wait_ge(s["r_done"], t + 1)
                nc.vector.scalar_tensor_tensor(out=xn[:n, b, :], in0=xt[:n, b, :], scalar=rr[:n, b:b + 1],
                                               in1=g1b[:n, :], op0=ALU.mult, op1=ALU.mult).then_inc(s["xn_done"], 1)
                hold(dve, s["tr_done"], t + 3, s["passed_dve"])
                nc.vector.tensor_copy(keep["xnT"][:, 4:8, ds(t * P, n)],
                                      ps[b][:, 1, :].rearrange("p (c r) -> p c r", c=4)[:, :, 0:n]).then_inc(s["cpd"], 1)

            with dve.Fori(0, NT // 2) as pair:
                for b in range(2):
                    tile(pair * 2 + b, b)
            tile(NT, 0)

            for k, (ta, tb) in enumerate(((keep["qa"], keep["qb"]), (keep["ka"], keep["kb"]))):
                ga = gains[:, 2 * k:2 * k + 1, :].to_broadcast([P, NT + 1, HD])
                gb = gains[:, 2 * k + 1:2 * k + 2, :].to_broadcast([P, NT + 1, HD])
                nc.vector.tensor_tensor(ta[:], cosd[:], ga, ALU.mult)
                nc.vector.tensor_tensor(tb[:], sind[:], gb, ALU.mult)
            nc.vector.tensor_scalar(keep["subg"][:], keep["subg"][:], 1.0 - LAM0, None, ALU.mult)
            lv = lamv[:].rearrange("p (a b) d -> p a b d", b=2)
            nc.vector.tensor_tensor(lamp[:], lv[:, :, 0, :], lv[:, :, 1, :], ALU.mult)
            dve.drain()
            nc.vector.tensor_reduce(lamd[:], lamp[:], AX.X, ALU.add).then_inc(s["lam_d"], 1)
            dve.wait_ge(s["lam_e"], 1)
            nc.vector.tensor_tensor(keep["neglam"][:], lame[:, 1:2], lame[:, 0:1], ALU.subtract)
            dve.drain()
            nc.vector.tensor_scalar(keep["neglam"][:], keep["neglam"][:], -LAM0, None, ALU.add)

        @block.tensor
        def _(pe):
            pe.sem_inc(s["tr_done"], 2)
            pe.wait_ge(s["ident_done"], 1)

            def tile(t, b):
                n = rows_of(t)
                hold(pe, s["cpa"], t + 1, s["passed_pe"])
                hold(pe, s["cpd"], t + 1, s["passed_pe"])
                hold(pe, s["xn_done"], t + 3, s["passed_pe"])
                for c in range(DC):
                    o = ps[b][:, c // 4, (c % 4) * P:(c % 4) * P + n]
                    last = nc.tensor.transpose(o, xn[:n, b, c * P:(c + 1) * P], keep["ident"][:n, :n])
                last.then_inc(s["tr_done"], 1)

            with pe.Fori(0, NT // 2) as pair:
                for b in range(2):
                    tile(pair * 2 + b, b)
            tile(NT, 0)


def build_attention(nc, A, keep):
    NU = 2 * (NT + 1)
    with ExitStack() as ctx:
        def sb(name, shape, dt=F32):
            return ctx.enter_context(nc.sbuf_tensor("at_" + name, shape, dt))

        s = semaphores(ctx, nc, "at", "w_in0 w_in1 w_in2 kc_in vc_in pj_done evq evv sq_done ss_done rr_done qf_done tr_done trc "
                 "kct_done kct_cp k_out v_out kv_free sc_done mx_done ex_done a_done at_a at_d tc_a tc_d pv_done "
                 "so_done ro_done on_done ot_done otc passed_pe passed_act passed_dve passed_pool passed_sp")
        w_in = [s["w_in0"], s["w_in1"], s["w_in2"]]
        w = [sb(f"w{k}", [P, DC, GW]) for k in range(3)]
        kc = sb("kc", [P, DC, GW])
        vc = sb("vc", [P, DC, GW])
        kcT = sb("kcT", [P, 2, PAST])
        qT = sb("qT", [P, 2, ROWS])
        kT = sb("kT", [P, 2, ROWS])
        kf = sb("kf", [P, NT + 1, GW])
        V = sb("V", [P, NT + 1, GW])
        sq = sb("sq", [P, 2, GW])
        qn = sb("qn", [P, GW])
        t1 = sb("t1", [P, GW])
        t2 = sb("t2", [P, GW])
        qf = sb("qf", [P, 4, GW])
        ss = sb("ss", [P, 2, 4])
        rr = sb("rr", [P, 2, 4])
        p = sb("p", [P, 2, 2, ROWS])
        aT = sb("aT", [P, 2, (NT + 1) * P])
        mx = sb("mx", [P, 2, 2])
        nb = sb("nb", [P, 2, 2])
        Z = sb("Z", [P, 2, 2])
        rz = sb("rz", [P, 2])
        rl = sb("rl", [P, 1])
        so = sb("so", [P, 2])
        ro = sb("ro", [P, 2])
        on = sb("on", [P, 2, VD])
        oj = sb("oj", [P, VD])
        S = ctx.enter_context(nc.psum_tensor("at_S", [P, 4, 512], F32))
        B = [ctx.enter_context(nc.psum_tensor(f"at_B{k}", [P, 512], F32)) for k in range(4)]
        T, O = B[0:2], B[2:4]
        ident, xnT, oT = keep["ident"], keep["xnT"], keep["oT"]
        block = ctx.enter_context(nc.Block())

        def wcols(kind, g):
            return A["w_in"][0, :, ds((QCOL, KCOL, VCOL)[kind] + g * GW, GW)].rearrange("(c p) n -> p c n", p=P)

        def cache(name, g):
            return A[name][:, ds(g * GW, GW)].rearrange("(c p) n -> p c n", p=P)

        def keys(t):
            return (t + 1) * P if t < NT else PAST + DEC

        def scores(c, t, n):
            first = 0 if t == NT else 2 * c
            banks = 3 if t == NT else 2
            return S[:n, first:first + banks, :].rearrange("p a b -> p (a b)")

        @block.sync
        def _(sp):
            def load_w(kind, g):
                sp.dma_start(w[kind][:], wcols(kind, g)).then_inc(w_in[kind], 16)

            def stores(g, then_load):
                if then_load:
                    sp.wait_ge(s["kct_done"], 4 * (g + 1))
                    sp.dma_start(kc[:], cache("cache_k", g + 1)).then_inc(s["kc_in"], 16)
                    for kind in range(2):
                        sp.wait_ge(s["pj_done"], 27 * g + 9 * (kind + 1))
                        load_w(kind, g + 1)
                sp.wait_ge(s["qf_done"], NU * (g + 1))
                sp.dma_start(A["k_prompt"][:, ds(g * GW, GW)].rearrange("(t p) n -> p t n", p=P),
                             kf[:, 0:NT, :]).then_inc(s["k_out"], 16)
                sp.dma_start(A["k_sample"][:, ds(g * GW, GW)], kf[:DEC, NT, :]).then_inc(s["k_out"], 16)
                if then_load:
                    sp.wait_ge(s["pj_done"], 27 * (g + 1))
                    load_w(2, g + 1)
                sp.wait_ge(s["evv"], 9 * (g + 2))
                sp.dma_start(A["v_prompt"][:, ds(g * GW, GW)].rearrange("(t p) n -> p t n", p=P),
                             V[:, 0:NT, :]).then_inc(s["v_out"], 16)
                sp.dma_start(A["v_sample"][:, ds(g * GW, GW)], V[:DEC, NT, :]).then_inc(s["v_out"], 16)
                sp.wait_ge(s["k_out"], 32 * (g + 1))
                hold(sp, s["v_out"], 32 * (g + 1), s["passed_sp"])
                sp.sem_inc(s["kv_free"], 1)
                if then_load:
                    sp.wait_ge(s["pv_done"], NU * (g + 1))
                    sp.dma_start(vc[:], cache("cache_v", g + 1)).then_inc(s["vc_in"], 16)

            sp.sem_inc(s["kv_free"], 1)
            sp.dma_start(kc[:], cache("cache_k", 0)).then_inc(s["kc_in"], 16)
            for kind in range(3):
                load_w(kind, 0)
            sp.dma_start(vc[:], cache("cache_v", 0)).then_inc(s["vc_in"], 16)
            with sp.Fori(0, GROUPS - 1) as g:
                stores(g, True)
            stores(GROUPS - 1, False)

        @block.tensor
        def _(pe):
            def cached_keys(g):
                pe.wait_ge(s["kc_in"], 16 * (g + 1))
                for m in range(4):
                    pe.wait_ge(s["kct_cp"], 4 * g + m + 1)
                    for k in range(4):
                        last = nc.tensor.transpose(S[:, 2 + m % 2, k * P:(k + 1) * P],
                                                   kc[:, 4 * (m % 2) + k, (m // 2) * P:(m // 2 + 1) * P], ident[:])
                    last.then_inc(s["kct_done"], 1)

            def project(g, u):
                kind, t = divmod(u, NT + 1)
                n = rows_of(t)
                if t == 0:
                    pe.wait_ge(w_in[kind], 16 * (g + 1))
                if u >= 4:
                    if u - 4 < NU:
                        hold(pe, s["evq"], NU * g + u - 3, s["passed_pe"])
                    else:
                        hold(pe, s["evv"], 9 * (g + 1) + u - 4 - NU + 1, s["passed_pe"])
                for c in range(DC):
                    last = nc.tensor.matmul(B[u % 4][:n, 0:GW], xnT[:, c, t * P:t * P + n], w[kind][:, c, :],
                                            start=(c == 0), stop=(c == DC - 1))
                last.then_inc(s["pj_done"], 1)

            def turn(g, u):
                kind, t = divmod(u, NT + 1)
                n = rows_of(t)
                hold(pe, s["trc"], NU * g + u + 1, s["passed_pe"])
                hold(pe, s["qf_done"], NU * g + u + 1, s["passed_pe"])
                for h in range(2):
                    src = qf[:n, u % 4, h * P:(h + 1) * P] if kind == 0 else kf[:n, t, h * P:(h + 1) * P]
                    last = nc.tensor.transpose(S[:, u % 2, h * P:h * P + n], src, ident[:n, :n])
                last.then_inc(s["tr_done"], 1)

            def score(g, i):
                h, t = divmod(i, NT + 1)
                n, nk = rows_of(t), keys(t)
                for c in range(2):
                    need = 2 * i + c if t == NT else (2 * i if t == 0 else 2 * i - 1 + c)
                    if i:
                        hold(pe, s["ex_done"], 4 * (NT + 1) * g + need, s["passed_pe"])
                    o = scores(c, t, n)
                    rows = slice(c * HD, (c + 1) * HD)
                    q = qT[rows, h, t * P:t * P + n]
                    if t < NT:
                        parts = [(k, kT[rows, h, k:min(k + 512, nk)]) for k in range(0, nk, 512)]
                    else:
                        parts = [(k, kcT[rows, h, k:k + 512]) for k in range(0, PAST, 512)]
                        parts.append((PAST, kT[rows, h, SEQ:ROWS]))
                    for k, keys_ap in parts:
                        last = nc.tensor.matmul(o[:, k:k + keys_ap.shape[1]], q, keys_ap, start=True, stop=True)
                    last.then_inc(s["sc_done"], 1)

            def turn_weights(g, i):
                h, t = divmod(i, NT + 1)
                n, nk = rows_of(t), keys(t)
                blocks = (nk + P - 1) // P
                hold(pe, s["tc_a"], NU * g + i + 1, s["passed_pe"])
                if t in range(4, NT):
                    hold(pe, s["tc_d"], 8 * g + 4 * h + t - 4 + 1, s["passed_pe"])
                hold(pe, s["a_done"], NU * g + i + 1, s["passed_pe"])
                for k in range(blocks):
                    m = min(P, nk - k * P)
                    o = T[0][:m, k * DEC:(k + 1) * DEC] if t == NT else T[k // 4][:, (k % 4) * P:(k % 4 + 1) * P]
                    last = nc.tensor.transpose(o, p[:n, i % 2, 0, k * P:k * P + m], ident[:n, :n])
                    if k == min(3, blocks - 1) and t < NT or t == NT and k == blocks - 1:
                        last.then_inc(s["at_a"], 1)
                    elif k == blocks - 1:
                        last.then_inc(s["at_d"], 1)

            def turn_out(g, i):
                n = rows_of(i % (NT + 1))
                hold(pe, s["on_done"], NU * g + i + 1, s["passed_pe"])
                nc.tensor.transpose(O[i % 2][:, P:P + n], on[:n, i % 2, :], ident[:n, :n]).then_inc(s["ot_done"], 1)

            def weigh(g, i):
                h, t = divmod(i, NT + 1)
                n, nk = rows_of(t), keys(t)
                blocks = (nk + P - 1) // P
                if i == NT:
                    hold(pe, s["vc_in"], 16 * (g + 1), s["passed_pe"])
                hold(pe, s["otc"], NU * g + i + 1, s["passed_pe"])
                hold(pe, s["tc_a"], NU * g + i + 2, s["passed_pe"])
                for k in range(blocks):
                    if t in range(4, NT) and k == 4:
                        hold(pe, s["tc_d"], 8 * g + 4 * h + t - 4 + 2, s["passed_pe"])
                    m = min(P, nk - k * P)
                    a = aT[:m, i % 2, k * n:(k + 1) * n]
                    v = (V[:m, k, h * P:(h + 1) * P] if t < NT or k == PAST // P
                         else vc[:, k, h * P:(h + 1) * P])
                    last = nc.tensor.matmul(O[i % 2][:n, 0:VD], a, v, start=(k == 0), stop=(k == blocks - 1))
                last.then_inc(s["pv_done"], 1)

            with pe.Fori(0, GROUPS) as g:
                hold(pe, s["otc"], NU * g + 2, s["passed_pe"])
                hold(pe, s["evv"], 9 * (g + 1), s["passed_pe"])
                cached_keys(g)
                for u in range(3 * (NT + 1)):
                    project(g, u)
                    if 0 <= u - 2 < NU:
                        turn(g, u - 2)
                hold(pe, s["evv"], 9 * (g + 2), s["passed_pe"])
                hold(pe, s["trc"], NU * (g + 1) + 2, s["passed_pe"])
                hold(pe, s["kct_cp"], 4 * (g + 1) + 2, s["passed_pe"])
                score(g, 0)
                for i in range(NU):
                    if i + 1 < NU:
                        score(g, i + 1)
                    turn_weights(g, i)
                    if i:
                        turn_out(g, i - 1)
                    weigh(g, i)
                turn_out(g, NU - 1)

        @block.scalar
        def _(act):
            def square(g, u):
                n = rows_of(u % (NT + 1))
                if u >= 2:
                    act.wait_ge(s["ss_done"], NU * g + u - 1)
                act.wait_ge(s["pj_done"], 27 * g + u + 1)
                nc.scalar.activation(sq[:n, u % 2, :], B[u % 4][:n, 0:GW], ACT.Square,
                                     scale=HD ** -0.5).then_inc(s["sq_done"], 1)

            def keep_turned(g, u):
                kind, t = divmod(u, NT + 1)
                n = rows_of(t)
                act.wait_ge(s["tr_done"], NU * g + u + 5)
                dst = (qT, kT)[kind]
                nc.scalar.copy(dst[:, :, t * P:t * P + n],
                               S[:, u % 2, 0:GW].rearrange("p (h r) -> p h r", h=2)[:, :, 0:n]).then_inc(s["trc"], 1)

            def keep_value(g, u):
                t = u - NU
                n = rows_of(t)
                if t == 0:
                    act.wait_ge(s["kv_free"], g + 1)
                act.wait_ge(s["pj_done"], 27 * g + u + 1)
                nc.scalar.copy(V[:n, t, :], B[u % 4][:n, 0:GW]).then_inc(s["evv"], 1)

            def exps(g, i):
                t = i % (NT + 1)
                n, nk = rows_of(t), keys(t)
                for c in range(2):
                    act.wait_ge(s["mx_done"], 2 * NU * g + 2 * i + c + 1)
                    nc.scalar.activation(p[:n, i % 2, c, 0:nk], scores(c, t, n)[:, 0:nk], ACT.Exp, scale=QKS,
                                         bias=nb[:n, i % 2, c:c + 1],
                                         accum_out=Z[:n, i % 2, c:c + 1]).then_inc(s["ex_done"], 1)

            def keep_weights(g, i):
                t = i % (NT + 1)
                cols = (NT + 1) * DEC if t == NT else min(t + 1, 4) * P
                act.wait_ge(s["at_a"], NU * g + i + 1)
                if t == NT:
                    last = PAST // P * DEC
                    nc.scalar.copy(aT[:, i % 2, 0:last], T[0][:, 0:last])
                    nc.scalar.copy(aT[:DEC, i % 2, last:cols], T[0][:DEC, last:cols]).then_inc(s["tc_a"], 1)
                else:
                    nc.scalar.copy(aT[:, i % 2, 0:cols], T[0][:, 0:cols]).then_inc(s["tc_a"], 1)

            def keep_out(g, i):
                h, t = divmod(i, NT + 1)
                n = rows_of(t)
                hold(act, s["ot_done"], NU * g + i + 3, s["passed_act"])
                nc.scalar.copy(oT[:, ds(g * 2 + h, 1), t * P:t * P + n],
                               O[i % 2][:, P:P + n].unsqueeze(1)).then_inc(s["otc"], 1)

            def square_out(g, i):
                n = rows_of(i % (NT + 1))
                act.wait_ge(s["pv_done"], NU * g + i + 1)
                nc.scalar.activation(oj[:n, :], O[i % 2][:n, 0:VD], ACT.Square, scale=VD ** -0.5,
                                     accum_out=so[:n, i % 2:i % 2 + 1]).then_inc(s["so_done"], 1)

            for sem, credit in ((s["evv"], 9), (s["trc"], 2), (s["kct_cp"], 2), (s["tc_a"], 1), (s["otc"], 2)):
                act.sem_inc(sem, credit)
            with act.Fori(0, GROUPS) as g:
                for m in range(4):
                    act.wait_ge(s["kct_done"], 4 * g + m + 1)
                    nc.scalar.copy(kcT[:, m // 2, 512 * (m % 2):512 * (m % 2 + 1)],
                                   S[:, 2 + m % 2, :]).then_inc(s["kct_cp"], 1)
                for u in range(3 * (NT + 1)):
                    if u < NU:
                        square(g, u)
                    else:
                        keep_value(g, u)
                    if 0 <= u - 2 < NU:
                        keep_turned(g, u - 2)
                exps(g, 0)
                for i in range(NU):
                    if i + 1 < NU:
                        exps(g, i + 1)
                    keep_weights(g, i)
                    if i:
                        keep_out(g, i - 1)
                    square_out(g, i)
                keep_out(g, NU - 1)

        @block.gpsimd
        def _(pool):
            def rsqrt(dst, src, done):
                nc.gpsimd.tensor_scalar(dst, src, EPS, None, ALU.add)
                pool.drain()
                nc.gpsimd.tensor_tensor(dst, dst, keep["mhalf"][:dst.shape[0], 0:dst.shape[1]],
                                        ALU.pow).then_inc(done, 1)

            with pool.Fori(0, GROUPS) as g:
                for u in range(NU):
                    n = rows_of(u % (NT + 1))
                    hold(pool, s["ss_done"], NU * g + u + 1, s["passed_pool"])
                    rsqrt(rr[:n, u % 2, :], ss[:n, u % 2, :], s["rr_done"])
                for i in range(NU):
                    n = rows_of(i % (NT + 1))
                    hold(pool, s["so_done"], NU * g + i + 1, s["passed_pool"])
                    rsqrt(ro[:n, i % 2:i % 2 + 1], so[:n, i % 2:i % 2 + 1], s["ro_done"])

        @block.vector
        def _(dve):
            def segs(ap):
                return ap.rearrange("p (a d) -> p a d", d=HD)

            def mean_square(g, u):
                n = rows_of(u % (NT + 1))
                dve.wait_ge(s["sq_done"], NU * g + u + 1)
                nc.vector.tensor_reduce(ss[:n, u % 2, :], segs(sq[:n, u % 2, :]), AX.X, ALU.add).then_inc(s["ss_done"], 1)

            def rotate(g, u):
                kind, t = divmod(u, NT + 1)
                n = rows_of(t)
                h = HD // 2
                ta, tb = ((keep["qa"], keep["qb"]), (keep["ka"], keep["kb"]))[kind]
                dve.wait_ge(s["rr_done"], NU * g + u + 1)
                nc.vector.tensor_tensor(segs(qn[:n, :]), segs(B[u % 4][:n, 0:GW]),
                                        rr[:n, u % 2, :].unsqueeze(2).to_broadcast([n, 4, HD]),
                                        ALU.mult).then_inc(s["evq"], 1)
                dve.drain()
                q3 = segs(qn[:n, :])
                nc.vector.tensor_tensor(segs(t1[:n, :]), q3, ta[:n, t:t + 1, :].to_broadcast([n, 4, HD]), ALU.mult)
                nc.vector.tensor_tensor(segs(t2[:n, :])[:, :, 0:h], q3[:, :, h:HD],
                                        tb[:n, t:t + 1, 0:h].to_broadcast([n, 4, h]), ALU.mult)
                nc.vector.tensor_tensor(segs(t2[:n, :])[:, :, h:HD], q3[:, :, 0:h],
                                        tb[:n, t:t + 1, h:HD].to_broadcast([n, 4, h]), ALU.mult)
                dve.drain()
                if kind == 0:
                    dve.wait_ge(s["tr_done"], NU * g + u + 1)
                    dst = qf[:n, u % 4, :]
                else:
                    if t == 0:
                        dve.wait_ge(s["kv_free"], g + 1)
                    dst = kf[:n, t, :]
                nc.vector.tensor_tensor(dst, t1[:n, :], t2[:n, :], ALU.add).then_inc(s["qf_done"], 1)

            def row_max(g, i):
                t = i % (NT + 1)
                n, nk = rows_of(t), keys(t)
                for c in range(2):
                    sc = scores(c, t, n)
                    dve.wait_ge(s["sc_done"], 2 * NU * g + 2 * i + c + 1)
                    if t < NT:
                        nc.vector.memset(sc[0:CHUNK, nk - CHUNK:nk], LOW)
                        dve.drain()
                    nc.vector.tensor_reduce(mx[:n, i % 2, c:c + 1], sc[:, 0:nk], AX.X, ALU.max)
                    dve.drain()
                    nc.vector.tensor_scalar(nb[:n, i % 2, c:c + 1], mx[:n, i % 2, c:c + 1], -QKS, None,
                                            ALU.mult).then_inc(s["mx_done"], 1)

            def difference(g, i):
                t = i % (NT + 1)
                n, nk = rows_of(t), keys(t)
                dve.wait_ge(s["ex_done"], 2 * NU * g + 2 * i + 2)
                nc.vector.reciprocal(rz[:n, :], Z[:n, i % 2, :])
                dve.drain()
                nc.vector.tensor_tensor(rl[:n, :], rz[:n, 1:2], keep["neglam"][:n, :], ALU.mult)
                dve.drain()
                nc.vector.tensor_scalar(p[:n, i % 2, 1, 0:nk], p[:n, i % 2, 1, 0:nk], rl[:n, 0:1], None, ALU.mult)
                dve.drain()
                nc.vector.scalar_tensor_tensor(out=p[:n, i % 2, 0, 0:nk], in0=p[:n, i % 2, 0, 0:nk],
                                               scalar=rz[:n, 0:1], in1=p[:n, i % 2, 1, 0:nk],
                                               op0=ALU.mult, op1=ALU.add).then_inc(s["a_done"], 1)

            def keep_weights(g, i):
                h, t = divmod(i, NT + 1)
                if t in range(4, NT):
                    cols = (t - 3) * P
                    dve.wait_ge(s["at_d"], 8 * g + 4 * h + t - 4 + 1)
                    nc.vector.tensor_copy(aT[:, i % 2, 4 * P:4 * P + cols], T[1][:, 0:cols]).then_inc(s["tc_d"], 1)

            def norm_out(g, i):
                n = rows_of(i % (NT + 1))
                dve.wait_ge(s["ot_done"], NU * g + i + 1)
                dve.wait_ge(s["ro_done"], NU * g + i + 1)
                nc.vector.scalar_tensor_tensor(out=on[:n, i % 2, :], in0=O[i % 2][:n, 0:VD],
                                               scalar=ro[:n, i % 2:i % 2 + 1], in1=keep["subg"][:n, :],
                                               op0=ALU.mult, op1=ALU.mult).then_inc(s["on_done"], 1)

            dve.sem_inc(s["tc_d"], 1)
            dve.sem_inc(s["tr_done"], 4)
            dve.sem_inc(s["ot_done"], 2)
            with dve.Fori(0, GROUPS) as g:
                for u in range(NU):
                    mean_square(g, u)
                    if u:
                        rotate(g, u - 1)
                rotate(g, NU - 1)
                row_max(g, 0)
                for i in range(NU):
                    difference(g, i)
                    if i + 1 < NU:
                        row_max(g, i + 1)
                    if i:
                        norm_out(g, i - 1)
                    keep_weights(g, i)
                norm_out(g, NU - 1)


def products(nc, pe, out, w, src, done):
    for part in range(3):
        for c in range(DC):
            last = nc.tensor.matmul(out[:, part, 0:PART], w[:, c, :], src[:, c, part * PART:(part + 1) * PART],
                                    start=(c == 0), stop=(c == DC - 1))
    last.then_inc(done, 1)


def thirds(ap):
    return ap.rearrange("p (a b) -> p a b", a=3)


def build_conv(nc, A, keep):
    with ExitStack() as ctx:
        def sb(name, shape, dt=F32):
            return ctx.enter_context(nc.sbuf_tensor("cv_" + name, shape, dt))

        s = semaphores(ctx, nc, "cv", "w_in0 w_in1 consts z_done c_done u_done y_done passed_dve passed_pe passed_act ready "
                 "tails out")
        w_in = [s["w_in0"], s["w_in1"]]
        w = sb("w", [P, 2, 3, DC, P])
        cw = sb("cw", [P, 3, DC])
        st = sb("st", [P, 2, DC])
        U = sb("U", [P, 2, ROWS + 4])
        Y = sb("Y", [P, 2, ROWS + 2])
        C = sb("C", [P, 2, ROWS])
        tail = sb("tail", [P, 4, DC])
        Z = [ctx.enter_context(nc.psum_tensor(f"cv_Z{b}", [P, 3, 512], F32)) for b in range(2)]
        cvT = keep["cvT"]
        block = ctx.enter_context(nc.Block())
        cols = (D, 2 * D, 0)
        cut = SEQ - 2 * PART

        def pieces(z, row, shift):
            return [(z[:, 0:2, 0:PART], row[:, 0:2 * PART].rearrange("p (a b) -> p a b", a=2)),
                    (z[:, 2, 0:cut], row[:, 2 * PART:SEQ]),
                    (z[:, 2, cut:PART], row[:, SEQ + shift:SEQ + shift + DEC])]

        @block.sync
        def _(sp):
            def load(cc, b):
                for k in range(3):
                    sp.dma_start(w[:, b, k, :, :], A["w_in"][0, :, ds(cols[k] + cc * P, P)]
                                 .rearrange("(c p) n -> p c n", p=P)).then_inc(w_in[b], 16)

            load(0, 0)
            load(1, 1)
            with sp.Fori(0, DC // 2 - 1) as pair:
                for b in range(2):
                    sp.wait_ge(s["z_done"], 6 * pair + 3 * (b + 1))
                    load(pair * 2 + 2 + b, b)
            sp.wait_ge(s["tails"], DC)
            with nc.allow_non_contiguous_dma(reason="two rows of state, channels in partitions"):
                for j in range(2):
                    for k, name in enumerate(("conv_prompt", "conv_sample")):
                        sp.dma_start(A[name][j].rearrange("(c p) -> p c", p=P), tail[:, 2 * k + j, :]).then_inc(s["out"], 16)
            sp.wait_ge(s["out"], 64)

        @block.gpsimd
        def _(pool):
            with nc.allow_non_contiguous_dma(reason="small vectors, channels in partitions"):
                for j in range(3):
                    pool.dma_start(cw[:, j, :], A["conv_w"][0, j].rearrange("(c p) -> p c", p=P)).then_inc(s["consts"], 16)
                for j in range(2):
                    pool.dma_start(st[:, j, :], A["state_conv"][0, 0, j].rearrange("(c p) -> p c", p=P)).then_inc(s["consts"], 16)

        @block.tensor
        def _(pe):
            def turn(pair, b):
                pe.wait_ge(w_in[b], 48 * (pair + 1))
                for k in range(3):
                    u = 3 * b + k
                    before = (u - 2) % 3
                    if before == 0:
                        pe.wait_ge(s["c_done"], 2 * pair + (u - 2) // 3 + 3)
                    elif before == 1:
                        pe.wait_ge(s["u_done"], 2 * pair + (u - 2) // 3 + 3)
                    else:
                        pe.wait_ge(s["y_done"], 2 * pair + (u - 2) // 3 + 3)
                    products(nc, pe, Z[u % 2], w[:, b, k], keep["xnT"], s["z_done"])

            with pe.Fori(0, DC // 2) as pair:
                for b in range(2):
                    turn(pair, b)

        @block.scalar
        def _(act):
            act.sem_inc(s["c_done"], 2)
            with act.Fori(0, DC // 2) as pair:
                for b in range(2):
                    act.wait_ge(s["u_done"], 2 * pair + b + 1)
                    act.wait_ge(s["z_done"], 6 * pair + 3 * b + 1)
                    nc.scalar.copy(thirds(C[:, b, :]), Z[(3 * b) % 2][:, :, 0:PART]).then_inc(s["c_done"], 1)

        @block.vector
        def _(dve):
            dve.sem_inc(s["u_done"], 2)
            dve.sem_inc(s["y_done"], 2)
            nc.vector.memset(U[:, :, 0:2], 0.0)
            dve.wait_ge(s["consts"], 80)

            def turn(pair, b):
                cc = pair * 2 + b
                nc.vector.tensor_copy(U[:, b, SEQ + 2:SEQ + 4], st[:, :, ds(cc, 1)].rearrange("p j c -> p (j c)"))
                dve.wait_ge(s["c_done"], 2 * pair + b + 3)
                hold(dve, s["z_done"], 6 * pair + 3 * b + 2, s["passed_dve"])
                z = Z[(3 * b + 1) % 2]
                for (zp, up), (_, cp) in zip(pieces(z, U[:, b, 2:], 2), pieces(z, C[:, b, :], 0)):
                    last = nc.vector.tensor_tensor(up, zp, cp, ALU.mult)
                last.then_inc(s["u_done"], 1)
                dve.drain()
                m = ROWS + 2
                nc.vector.tensor_scalar(Y[:, b, :], U[:, b, 0:m], cw[:, 0, ds(cc, 1)], None, ALU.mult)
                for j in (1, 2):
                    dve.drain()
                    nc.vector.scalar_tensor_tensor(out=Y[:, b, :], in0=U[:, b, j:j + m], scalar=cw[:, j, ds(cc, 1)],
                                                   in1=Y[:, b, :], op0=ALU.mult, op1=ALU.add)
                nc.vector.tensor_copy(tail[:, 0:2, ds(cc, 1)].rearrange("p j c -> p (j c)"), U[:, b, SEQ:SEQ + 2])
                nc.vector.tensor_copy(tail[:, 2:4, ds(cc, 1)].rearrange("p j c -> p (j c)"),
                                      U[:, b, SEQ + 2 + DEC:SEQ + 4 + DEC]).then_inc(s["tails"], 1)
                dve.drain()
                hold(dve, s["z_done"], 6 * pair + 3 * b + 3, s["passed_dve"])
                z = Z[(3 * b + 2) % 2]
                row = cvT[:, ds(cc, 1), :].rearrange("p c r -> p (c r)")
                for (zp, yp), (_, op) in zip(pieces(z, Y[:, b, :], 2), pieces(z, row, 0)):
                    last = nc.vector.tensor_tensor(op, zp, yp, ALU.mult)
                last.then_inc(s["y_done"], 1)

            with dve.Fori(0, DC // 2) as pair:
                for b in range(2):
                    turn(pair, b)


def build_merge(nc, A, keep):
    with ExitStack() as ctx:
        def sb(name, shape, dt=F32):
            return ctx.enter_context(nc.sbuf_tensor("mg_" + name, shape, dt))

        s = semaphores(ctx, nc, "mg", "w_in0 w_in1 consts z_done g_done m_done passed_dve passed_act mixed")
        w_in = [s["w_in0"], s["w_in1"]]
        w = sb("w", [P, 2, 4, DC, P])
        bg = sb("bg", [P, 2, DC])
        G = sb("G", [P, 2, ROWS])
        M = sb("M", [P, 2, ROWS])
        Z = [ctx.enter_context(nc.psum_tensor(f"mg_Z{b}", [P, 3, 512], F32)) for b in range(2)]
        mixT = keep["mixT"]
        block = ctx.enter_context(nc.Block())

        @block.sync
        def _(sp):
            def load(cc, b):
                srcs = (A["w_in"][0, :, ds(GACOL + cc * P, P)], A["w_conv_out"][0, :, ds(cc * P, P)],
                        A["w_in"][0, :, ds(GBCOL + cc * P, P)], A["w_attn_out"][0, :, ds(cc * P, P)])
                for k in range(4):
                    sp.dma_start(w[:, b, k, :, :], srcs[k].rearrange("(c p) n -> p c n", p=P)).then_inc(w_in[b], 16)

            load(0, 0)
            load(1, 1)
            with sp.Fori(0, DC // 2 - 1) as pair:
                for b in range(2):
                    sp.wait_ge(s["z_done"], 8 * pair + 4 * (b + 1))
                    load(pair * 2 + 2 + b, b)

        @block.gpsimd
        def _(pool):
            with nc.allow_non_contiguous_dma(reason="gate biases, channels in partitions"):
                for j in range(2):
                    pool.dma_start(bg[:, j, :], A["b_gate"][0, j].rearrange("(c p) -> p c", p=P)).then_inc(s["consts"], 16)

        @block.tensor
        def _(pe):
            with pe.Fori(0, DC // 2) as pair:
                for b in range(2):
                    pe.wait_ge(w_in[b], 64 * (pair + 1))
                    for k in range(4):
                        if k % 2 == 0:
                            pe.wait_ge(s["g_done"], 4 * pair + 2 * b + k // 2 + 1)
                        else:
                            pe.wait_ge(s["m_done"], 4 * pair + 2 * b + k // 2 + 1)
                        products(nc, pe, Z[k % 2], w[:, b, k], (keep["xnT"], keep["cvT"], keep["xnT"], keep["oT"])[k],
                                 s["z_done"])

        @block.scalar
        def _(act):
            act.sem_inc(s["g_done"], 1)
            act.wait_ge(s["consts"], 32)
            with act.Fori(0, DC // 2) as pair:
                for b in range(2):
                    for k in range(2):
                        act.wait_ge(s["m_done"], 4 * pair + max(2 * b + k, 1))
                        hold(act, s["z_done"], 8 * pair + 4 * b + 2 * k + 1, s["passed_act"])
                        nc.scalar.activation(thirds(G[:, k, :]), Z[0][:, :, 0:PART], ACT.Sigmoid,
                                             bias=bg[:, k, ds(pair * 2 + b, 1)]).then_inc(s["g_done"], 1)

        @block.vector
        def _(dve):
            dve.sem_inc(s["m_done"], 1)
            with dve.Fori(0, DC // 2) as pair:
                for b in range(2):
                    for k in range(2):
                        dve.wait_ge(s["g_done"], 4 * pair + 2 * b + k + 2)
                        dve.wait_ge(s["z_done"], 8 * pair + 4 * b + 2 * k + 2)
                        nc.vector.tensor_tensor(thirds(M[:, k, :]), Z[1][:, :, 0:PART], thirds(G[:, k, :]),
                                                ALU.mult).then_inc(s["m_done"], 1)
                    dve.drain()
                    nc.vector.tensor_tensor(mixT[:, ds(pair * 2 + b, 1), :], M[:, 0:1, :], M[:, 1:2, :], ALU.add)
                    dve.drain()


def build_out(nc, A, keep):
    with ExitStack() as ctx:
        def sb(name, shape, dt=F32):
            return ctx.enter_context(nc.sbuf_tensor("ou_" + name, shape, dt))

        s = semaphores(ctx, nc, "ou", "w_in0 w_in1 x_in0 x_in1 x_in2 z_done a_done out0 out1 out2")
        w_in = [s["w_in0"], s["w_in1"]]
        x_in = [s["x_in0"], s["x_in1"], s["x_in2"]]
        out = [s["out0"], s["out1"], s["out2"]]
        w = sb("w", [P, DC, D])
        xt = sb("xt", [P, 3, D])
        Z = [ctx.enter_context(nc.psum_tensor(f"ou_Z{b}", [P, 2, 512], F32)) for b in range(2)]
        mixT = keep["mixT"]
        x1 = A["x1"]
        block = ctx.enter_context(nc.Block())

        def load_x(eng, t):
            src = A["x_sample"][0] if t == NT else A["x_prompt"][0, t * P:(t + 1) * P, :]
            eng.dma_start(xt[:rows_of(t), t % 3, :], src).then_inc(x_in[t % 3], 16)

        @block.sync
        def _(sp):
            for h in range(2):
                sp.dma_start(w[:, :, h * 512:(h + 1) * 512],
                             A["w_o"][0, :, h * 512:(h + 1) * 512].rearrange("(c p) n -> p c n", p=P)).then_inc(w_in[h], 16)
            for t in range(3):
                load_x(sp, t)
            for t in range(NT + 1):
                sp.wait_ge(s["a_done"], t + 1)
                if t < NT:
                    sp.dma_start(x1[t * P:(t + 1) * P, :], xt[:, t % 3, :]).then_inc(out[t % 3], 16)
                else:
                    for q in range(4):
                        sp.dma_start(x1[SEQ + q * DEC:SEQ + (q + 1) * DEC, :], xt[:DEC, t % 3, :]).then_inc(out[t % 3], 16)
                if 1 <= t and t + 2 <= NT:
                    sp.wait_ge(out[(t - 1) % 3], 16 * ((t - 1) // 3 + 1))
                    load_x(sp, t + 2)
            for b in range(3):
                tiles = len(range(b, NT + 1, 3)) + (3 if NT % 3 == b else 0)
                sp.wait_ge(out[b], 16 * tiles)

        @block.tensor
        def _(pe):
            for t in range(NT + 1):
                n = rows_of(t)
                if t >= 2:
                    pe.wait_ge(s["a_done"], t - 1)
                for h in range(2):
                    if t == 0:
                        pe.wait_ge(w_in[h], 16)
                    for c in range(DC):
                        last = nc.tensor.matmul(Z[t % 2][:n, h, :], mixT[:, c, t * P:t * P + n],
                                                w[:, c, h * 512:(h + 1) * 512], start=(c == 0), stop=(c == DC - 1))
                last.then_inc(s["z_done"], 1)

        @block.vector
        def _(dve):
            for t in range(NT + 1):
                n = rows_of(t)
                dve.wait_ge(x_in[t % 3], 16 * (t // 3 + 1))
                dve.wait_ge(s["z_done"], t + 1)
                nc.vector.tensor_tensor(xt[:n, t % 3, :], Z[t % 2][:n, :, :].rearrange("p a b -> p (a b)"),
                                        xt[:n, t % 3, :], ALU.add).then_inc(s["a_done"], 1)


def build_peer(nc, A, keep):
    with ExitStack() as ctx:
        def sb(name, shape, dt=F32):
            return ctx.enter_context(nc.sbuf_tensor("pe_" + name, shape, dt))

        s = semaphores(ctx, nc, "pe", "wq_in consts setup sk_t x_in0 x_in1 y_out used idx_ready staged xsq r_done xn_done xt_done "
                 "xt_copied q_done qsq rq_done qn_done qt_done qt_copied s_done s_copied s_used dots_done gelu_done "
                 "acc_done gm_done ge_done fin_p fin_d passed_pool passed_dve passed_act passed_pe sel_done")
        landed = [ctx.enter_context(nc.semaphore(f"pe_landed{j}")) for j in range(RING)]
        x_in = [s["x_in0"], s["x_in1"]]
        wq = sb("wq", [P, DC, PQ])
        ring = sb("ring", [P, RING, D])
        g2b = sb("g2b", [P, D])
        xa = sb("xa", [P, 2, D])
        xb = sb("xb", [P, 2, D])
        xT = sb("xT", [P, DC, P])
        qn = sb("qn", [P, PQ])
        qT = sb("qT", [P, 2 * PH, P])
        sc = sb("sc", [P, 2 * PH, NKEYS])
        skT = sb("skT", [P, 2, NKEYS])
        gq = sb("gq", [P, 2])
        sel = sb("sel", [P, DEC])
        iot = sb("iot", [P, TOPK])
        idx = sb("idx", [P, 2, SLOTS], U32)
        gw = sb("gw", [P, 2, SLOTS])
        idst = sb("idst", [P, 2, TOPK], U32)
        dots16 = sb("dots16", [P, TOPK])
        hd = sb("hd", [P, SLOTS])
        hw = sb("hw", [P, SLOTS])
        ssx = sb("ssx", [P, 1])
        rx = sb("rx", [P, 1])
        qs = sb("qs", [P, PH])
        rq = sb("rq", [P, PH])
        sw = sb("sw", [P, 2, NKEYS])
        sw2 = sb("sw2", [P, 2, NKEYS])
        m16 = sb("m16", [P, 2, TOPK])
        i16 = sb("i16", [P, 2, TOPK], U32)
        cand = sb("cand", [P, TOPK * TOPK])
        cand2 = sb("cand2", [P, TOPK * TOPK])
        b16 = sb("b16", [P, TOPK])
        j16 = sb("j16", [P, TOPK], U32)
        itop = sb("itop", [P, PH, 2 * TOPK])
        best = sb("best", [P, PH, TOPK])
        pick = sb("pick", [P, PH, TOPK], U32)
        pk = sb("pk", [P, 2, SLOTS], U32)
        pf = sb("pf", [P, 2, PH, TOPK])
        oh = sb("oh", [P, PH // 2, TOPK, TOPK])
        e01 = sb("e01", [P, 2, PH, TOPK])
        gs = sb("gs", [P, PH])
        ps = ctx.enter_context(nc.psum_tensor("pe_ps", [P, 8, 512], F32))
        lo = ps[:, 0:4, :].rearrange("p a b -> p (a b)")
        hi = ps[:, 4:8, :].rearrange("p a b -> p (a b)")
        ident = keep["ident"]
        x1 = A["x1"]
        block = ctx.enter_context(nc.Block())

        @block.sync
        def _(sp):
            sp.dma_start(xa[:, 0, :], x1[0:P, :]).then_inc(x_in[0], 16)
            sp.dma_start(g2b[:], A["norm2_g"].to_broadcast([P, D])).then_inc(s["consts"], 16)
            sp.dma_start(sw[:], A["peer_subkeys"][0].rearrange("c k d -> k c d")).then_inc(s["consts"], 16)
            with nc.allow_non_contiguous_dma(reason="a vector, channels in partitions"):
                sp.dma_start(gq[:], A["peer_q_g"][0].rearrange("(c p) -> p c", p=P)).then_inc(s["consts"], 16)
            sp.dma_start(wq[:], A["peer_wq"][0].rearrange("(c p) n -> p c n", p=P)).then_inc(s["wq_in"], 16)

            def tile(pair, b):
                t = pair * 2 + b
                sp.dma_start(xa[:, 1 - b, :], x1[ds((t + 1) * P, P), :]).then_inc(x_in[1 - b], 16)
                sp.wait_ge(s["acc_done"], t + 1)
                sp.dma_start(A["y_prompt"][0, ds(t * P, P), :], xa[:, b, :]).then_inc(s["y_out"], 16)
                hold(sp, s["y_out"], 16 * (t + 1), s["fin_p"])

            with sp.Fori(0, NT // 2) as pair:
                for b in range(2):
                    tile(pair, b)
            sp.wait_ge(s["acc_done"], NT + 2)
            sp.dma_start(A["y_sample"][0], xb[:DEC, 1, :]).then_inc(s["y_out"], 16)
            sp.wait_ge(s["y_out"], 16 * (NT + 1))

        @block.gpsimd
        def _(pool):
            nc.gpsimd.memset(sel[:], 0.0)
            nc.gpsimd.iota(idst[:, 0, :], pattern=[[1, TOPK]], base=0, channel_multiplier=0)
            pool.drain()
            nc.gpsimd.tensor_copy(iot[:], idst[:, 0, :]).then_inc(s["setup"], 1)
            for q in range(4):
                nc.gpsimd.affine_select(out=sel[:], in_=sel[:], compare_op=ALU.not_equal, fill=1.0, base=-DEC * q,
                                        pattern=[[-1, DEC]], channel_multiplier=1)
                pool.drain()
            pool.sem_inc(s["sel_done"], 1)

            def rsqrt(dst, src, done):
                nc.gpsimd.tensor_scalar(dst, src, EPS, None, ALU.add)
                pool.drain()
                nc.gpsimd.tensor_tensor(dst, dst, keep["mhalf"][:, 0:dst.shape[1]], ALU.pow).then_inc(done, 1)

            def norm_x(t):
                hold(pool, s["xsq"], t + 1, s["passed_pool"])
                rsqrt(rx[:], ssx[:], s["r_done"])

            def norm_q(t):
                hold(pool, s["qsq"], t + 1, s["passed_pool"])
                rsqrt(rq[:], qs[:], s["rq_done"])

            def gather(src, table, first, group, par):
                for j in range(RING):
                    if j % 4 == 0:
                        hold(pool, s["used"], group * RING + j + 4, s["passed_pool"])
                    if j == 0:
                        nc.gpsimd.tensor_copy(idst[:, par, :], src[:, ds(first, TOPK)]).then_inc(s["staged"], 1)
                        hold(pool, s["staged"], group + 1, s["passed_pool"])
                    nc.gpsimd.indirect_dma_start(
                        out=ring[:, j, :], out_offset=None, in_=table,
                        in_offset=bass.IndirectOffsetOnAxis(ap=idst[:, par, j:j + 1], axis=0)).then_inc(landed[j], 16)

            def heads(t, b, table, phase, h0, h1):
                with pool.Fori(h0 // 2, h1 // 2) as half:
                    for par in range(2):
                        h = half * 2 + par
                        gather(idx[:, b, :], table, h * TOPK, t * 16 + phase * 8 + h, par)

            def tile(pair, b):
                t = pair * 2 + b
                hold(pool, s["idx_ready"], t + 1, s["passed_pool"])
                heads(t, b, A["peer_u"][0], 0, 0, 2)
                norm_x(t + 1)
                heads(t, b, A["peer_u"][0], 0, 2, 6)
                norm_q(t + 1)
                heads(t, b, A["peer_u"][0], 0, 6, 8)
                heads(t, b, A["peer_v"][0], 1, 0, 8)

            norm_x(0)
            norm_q(0)
            with pool.Fori(0, NT // 2) as pair:
                for b in range(2):
                    tile(pair, b)
            pool.wait_ge(s["idx_ready"], NT + 2)
            for k in range(4):
                gather(idx[:, 1, :], A["peer_u"][0] if k < 2 else A["peer_v"][0], (k % 2) * TOPK, NT * 16 + k, k % 2)

        @block.tensor
        def _(pe):
            pe.wait_ge(s["consts"], 48)
            for c in range(2):
                last = nc.tensor.transpose(ps[:, 7, c * P:(c + 1) * P], sw[:, c, :], ident[:])
            last.then_inc(s["sk_t"], 1)

            def query(t):
                hold(pe, s["xn_done"], t + 1, s["passed_pe"])
                for c in range(DC):
                    last = nc.tensor.transpose(lo[:, c * P:(c + 1) * P], xb_of(t)[:, c * P:(c + 1) * P], ident[:])
                last.then_inc(s["xt_done"], 1)
                hold(pe, s["xt_copied"], t + 1, s["passed_pe"])
                for q in range(4):
                    for c in range(DC):
                        last = nc.tensor.matmul(hi[:, q * 512:(q + 1) * 512], xT[:, c, :], wq[:, c, q * 512:(q + 1) * 512],
                                                start=(c == 0), stop=(c == DC - 1))
                last.then_inc(s["q_done"], 1)
                hold(pe, s["qn_done"], t + 1, s["passed_pe"])
                for k in range(2 * PH):
                    last = nc.tensor.transpose(lo[:, k * P:(k + 1) * P], qn[:, k * P:(k + 1) * P], ident[:])
                last.then_inc(s["qt_done"], 1)
                hold(pe, s["qt_copied"], t + 1, s["passed_pe"])
                for k in range(2 * PH):
                    last = nc.tensor.matmul(hi[:, k * P:(k + 1) * P], qT[:, k, :], skT[:, k % 2, :], start=True, stop=True)
                last.then_inc(s["s_done"], 1)

            half = [0]

            def xb_of(t):
                return xb[:, half[0], :]

            pe.wait_ge(s["setup"], 2)
            pe.wait_ge(s["wq_in"], 16)
            query(0)
            with pe.Fori(0, NT // 2) as pair:
                for b in range(2):
                    half[0] = 1 - b
                    query(pair * 2 + b + 1)
            pe.wait_ge(s["sel_done"], 1)
            pe.wait_ge(s["acc_done"], NT + 1)
            for h in range(2):
                last = nc.tensor.matmul(lo[:DEC, h * 512:(h + 1) * 512], sel[:], xa[:, 1, h * 512:(h + 1) * 512],
                                        start=True, stop=True)
            last.then_inc(s["fin_d"], 1)

        @block.scalar
        def _(act):
            act.wait_ge(s["sk_t"], 1)
            nc.scalar.copy(skT[:].rearrange("p c k -> p (c k)"), ps[:, 7, 0:2 * P]).then_inc(s["setup"], 1)

            def query(t, b, turn):
                act.wait_ge(x_in[b], 16 * turn)
                nc.scalar.activation(xT[:].rearrange("p c k -> p (c k)"), xa[:, b, :], ACT.Square, scale=D ** -0.5,
                                     accum_out=ssx[:]).then_inc(s["xsq"], 1)
                act.drain()
                act.wait_ge(s["xt_done"], t + 1)
                for k in range(2):
                    last = nc.scalar.copy(xT[:, 4 * k:4 * k + 4, :].rearrange("p c k -> p (c k)"), ps[:, k, :])
                last.then_inc(s["xt_copied"], 1)
                act.wait_ge(s["q_done"], t + 1)
                for h in range(PH):
                    last = nc.scalar.activation(qn[:, h * 256:(h + 1) * 256], hi[:, h * 256:(h + 1) * 256], ACT.Square,
                                                scale=256 ** -0.5, accum_out=qs[:, h:h + 1])
                last.then_inc(s["qsq"], 1)
                act.drain()
                act.wait_ge(s["rq_done"], t + 1)
                for h in range(PH):
                    last = nc.scalar.activation(qn[:, h * 256:(h + 1) * 256], hi[:, h * 256:(h + 1) * 256], ACT.Copy,
                                                scale=rq[:, h:h + 1])
                last.then_inc(s["qn_done"], 1)
                act.wait_ge(s["qt_done"], t + 1)
                lo4 = lo.rearrange("p (h c r) -> p h c r", h=PH, c=2)
                qT4 = qT[:].rearrange("p (h c) r -> p h c r", c=2)
                for k in range(4):
                    for c in range(2):
                        last = nc.scalar.activation(qT4[:, 2 * k:2 * k + 2, c, :], lo4[:, 2 * k:2 * k + 2, c, :], ACT.Copy,
                                                    scale=gq[:, c:c + 1])
                last.then_inc(s["qt_copied"], 1)
                act.wait_ge(s["s_used"], t + 1)
                act.wait_ge(s["s_done"], t + 1)
                for k in range(4):
                    last = nc.scalar.copy(sc[:, 4 * k:4 * k + 4, :].rearrange("p c k -> p (c k)"), hi[:, k * 512:(k + 1) * 512])
                last.then_inc(s["s_copied"], 1)

            def gelu(t, n):
                act.wait_ge(s["dots_done"], t + 1)
                nc.scalar.activation(hw[:, 0:n], hd[:, 0:n], ACT.Gelu).then_inc(s["gelu_done"], 1)

            def exps(t):
                act.wait_ge(s["gm_done"], t + 1)
                nc.scalar.activation(best[:], best[:], ACT.Exp).then_inc(s["ge_done"], 1)

            act.wait_ge(s["consts"], 48)
            query(0, 0, 1)
            exps(0)
            with act.Fori(0, NT // 2) as pair:
                for b in range(2):
                    t = pair * 2 + b
                    query(t + 1, 1 - b, pair + 1 + b)
                    gelu(t, SLOTS)
                    exps(t + 1)
            gelu(NT, DEC)

        @block.vector
        def _(dve):
            def top16(val, ind, src, spare):
                n = len(src)
                for k in range(n):
                    nc.vector.max(val[k][:, 0:8], src[k])
                dve.drain()
                for k in range(n):
                    nc.vector.max_index(ind[k][:, 0:8], val[k][:, 0:8], src[k])
                    nc.vector.match_replace(spare[k], val[k][:, 0:8], src[k], LOW)
                dve.drain()
                for k in range(n):
                    nc.vector.max(val[k][:, 8:16], spare[k])
                dve.drain()
                for k in range(n):
                    nc.vector.max_index(ind[k][:, 8:16], val[k][:, 8:16], spare[k])
                dve.drain()

            def topk(h):
                nc.vector.tensor_copy(sw[:], sc[:, ds(h * 2, 2), :])
                dve.drain()
                top16([m16[:, c, :] for c in range(2)], [i16[:, c, :] for c in range(2)],
                      [sw[:, c, :] for c in range(2)], [sw2[:, c, :] for c in range(2)])
                nc.vector.tensor_tensor(cand[:].rearrange("p (i j) -> p i j", i=TOPK),
                                        m16[:, 0, :].unsqueeze(2).to_broadcast([P, TOPK, TOPK]),
                                        m16[:, 1:2, :].to_broadcast([P, TOPK, TOPK]), ALU.add)
                nc.vector.tensor_copy(itop[:, ds(h, 1), :].rearrange("p h k -> p (h k)"),
                                      i16[:].rearrange("p c k -> p (c k)"))
                dve.drain()
                top16([b16[:]], [j16[:]], [cand[:]], [cand2[:]])
                nc.vector.tensor_copy(best[:, ds(h, 1), :].rearrange("p h k -> p (h k)"), b16[:])
                nc.vector.tensor_copy(pick[:, ds(h, 1), :].rearrange("p h k -> p (h k)"), j16[:])

            def places():
                flat = pick[:].rearrange("p h k -> p (h k)")
                nc.vector.tensor_scalar(pk[:, 0, :], flat, 4, None, ALU.logical_shift_right)
                nc.vector.tensor_scalar(pk[:, 1, :], flat, TOPK - 1, None, ALU.bitwise_and)
                dve.drain()
                nc.vector.tensor_copy(pf[:].rearrange("p c h k -> p (c h k)"), pk[:].rearrange("p c k -> p (c k)"))
                dve.drain()

            def keys_of(part):
                hs = slice(part * PH // 2, (part + 1) * PH // 2)
                shape = [P, PH // 2, TOPK, TOPK]
                for c in range(2):
                    nc.vector.tensor_tensor(oh[:], pf[:, c, hs, :].unsqueeze(3).to_broadcast(shape),
                                            iot[:].unsqueeze(1).unsqueeze(1).to_broadcast(shape), ALU.is_equal)
                    dve.drain()
                    nc.vector.tensor_tensor(oh[:], oh[:], itop[:, hs, c * TOPK:(c + 1) * TOPK].unsqueeze(2)
                                            .to_broadcast(shape), ALU.mult)
                    dve.drain()
                    nc.vector.tensor_reduce(e01[:, c, hs, :], oh[:], AX.X, ALU.add)
                    dve.drain()

            def experts(b):
                nc.vector.scalar_tensor_tensor(out=idx[:, b, :], in0=e01[:, 0].rearrange("p h k -> p (h k)"),
                                               scalar=float(NKEYS), in1=e01[:, 1].rearrange("p h k -> p (h k)"),
                                               op0=ALU.mult, op1=ALU.add).then_inc(s["idx_ready"], 1)

            def softmax_start():
                nc.vector.tensor_copy(gs[:], best[:, :, 0])
                dve.drain()
                nc.vector.tensor_tensor(best[:], best[:], gs[:].unsqueeze(2).to_broadcast([P, PH, TOPK]),
                                        ALU.subtract).then_inc(s["gm_done"], 1)

            def softmax_end(t, b):
                dve.wait_ge(s["ge_done"], t + 1)
                nc.vector.tensor_reduce(gs[:], best[:], AX.X, ALU.add)
                dve.drain()
                nc.vector.reciprocal(gs[:], gs[:])
                dve.drain()
                nc.vector.tensor_tensor(gw[:, b, :].rearrange("p (h k) -> p h k", h=PH), best[:],
                                        gs[:].unsqueeze(2).to_broadcast([P, PH, TOPK]), ALU.mult)
                dve.drain()

            def norm_x(t, b):
                hold(dve, s["r_done"], t + 1, s["passed_dve"])
                nc.vector.scalar_tensor_tensor(out=xb[:, b, :], in0=xa[:, b, :], scalar=rx[:, 0:1], in1=g2b[:],
                                               op0=ALU.mult, op1=ALU.mult).then_inc(s["xn_done"], 1)

            def dot_steps(b, group, first):
                for j in range(RING):
                    dve.wait_ge(landed[j], 16 * (group + 1))
                    nc.vector.tensor_tensor_reduce(out=ring[:, j, :], in0=ring[:, j, :], in1=xb[:, b, :], scale=1.0,
                                                   scalar=0.0, op0=ALU.mult, op1=ALU.add,
                                                   accum_out=dots16[:, j:j + 1]).then_inc(s["used"], 1)
                dve.drain()
                nc.vector.tensor_copy(hd[:, ds(first, TOPK)], dots16[:])
                dve.drain()

            def sum_steps(b, group, first):
                for j in range(RING):
                    dve.wait_ge(landed[j], 16 * (group + 1))
                    dve.wait_ge(s["used"], RING * (group + 1) + j)
                    nc.vector.scalar_tensor_tensor(out=xa[:, b, :], in0=ring[:, j, :], scalar=hw[:, ds(first + j, 1)],
                                                   in1=xa[:, b, :], op0=ALU.mult, op1=ALU.add).then_inc(s["used"], 1)

            def tile(pair, b):
                t = pair * 2 + b
                nb = 1 - b
                with dve.Fori(0, 2) as h:
                    dot_steps(b, t * 16 + h, h * TOPK)
                norm_x(t + 1, nb)
                with dve.Fori(2, 8) as h:
                    dot_steps(b, t * 16 + h, h * TOPK)
                nc.vector.drain().then_inc(s["dots_done"], 1)
                dve.wait_ge(s["gelu_done"], t + 1)
                nc.vector.tensor_tensor(hw[:], hw[:], gw[:, b, :], ALU.mult)
                dve.drain()
                hold(dve, s["s_copied"], t + 2, s["passed_dve"])
                with dve.Fori(0, 4) as h:
                    sum_steps(b, t * 16 + 8 + h, h * TOPK)
                    for k in range(2):
                        topk(h * 2 + k)
                dve.drain()
                dve.sem_inc(s["s_used"], 1)
                softmax_start()
                places()
                sum_steps(b, t * 16 + 12, 4 * TOPK)
                keys_of(0)
                sum_steps(b, t * 16 + 13, 5 * TOPK)
                keys_of(1)
                experts(nb)
                softmax_end(t + 1, nb)
                with dve.Fori(6, 8) as h:
                    sum_steps(b, t * 16 + 8 + h, h * TOPK)
                nc.vector.drain().then_inc(s["acc_done"], 1)

            dve.wait_ge(s["consts"], 48)
            dve.sem_inc(s["s_used"], 1)
            dve.sem_inc(s["used"], RING)
            dve.wait_ge(s["setup"], 2)
            norm_x(0, 0)
            dve.wait_ge(s["s_copied"], 1)
            with dve.Fori(0, PH) as h:
                topk(h)
            dve.drain()
            dve.sem_inc(s["s_used"], 1)
            softmax_start()
            places()
            keys_of(0)
            keys_of(1)
            experts(0)
            softmax_end(0, 0)
            with dve.Fori(0, NT // 2) as pair:
                for b in range(2):
                    tile(pair, b)
            for q in range(4):
                quad = slice(q * DEC, (q + 1) * DEC)
                nc.vector.tensor_copy(idx[quad, 1, 0:DEC], idx[quad, 0, quad])
                nc.vector.tensor_copy(gw[quad, 1, 0:DEC], gw[quad, 0, quad])
            nc.vector.drain().then_inc(s["idx_ready"], 1)
            for k in range(2):
                dot_steps(0, NT * 16 + k, k * TOPK)
            nc.vector.drain().then_inc(s["dots_done"], 1)
            dve.wait_ge(s["fin_p"], NT)
            nc.vector.memset(xa[:, 1, :], 0.0)
            dve.wait_ge(s["gelu_done"], NT + 1)
            nc.vector.tensor_tensor(hw[:, 0:DEC], hw[:, 0:DEC], gw[:, 1, 0:DEC], ALU.mult)
            dve.drain()
            for k in range(2):
                sum_steps(1, NT * 16 + 2 + k, k * TOPK)
            nc.vector.drain().then_inc(s["acc_done"], 1)
            dve.wait_ge(s["fin_d"], 1)
            nc.vector.tensor_tensor(xb[:DEC, 1, :], lo[:DEC, 0:D], xa[:DEC, 0, :], ALU.add)
            nc.vector.drain().then_inc(s["acc_done"], 1)


def build(nc, A):
    with ExitStack() as ctx:
        def sb(name, shape, dt=F32):
            return ctx.enter_context(nc.sbuf_tensor(name, shape, dt))

        keep = {"ident": sb("ident", [P, P]), "mhalf": sb("mhalf", [P, 8])}
        with ExitStack() as trunk:
            def tsb(name, shape):
                return trunk.enter_context(nc.sbuf_tensor(name, shape, F32))

            keep["xnT"] = tsb("xnT", [P, DC, ROWS])
            keep["oT"] = tsb("oT", [P, DC, ROWS])
            with ExitStack() as tables:
                for name in ("qa", "qb", "ka", "kb"):
                    keep[name] = tables.enter_context(nc.sbuf_tensor(name, [P, NT + 1, HD], F32))
                keep["subg"] = tables.enter_context(nc.sbuf_tensor("subg", [P, VD], F32))
                keep["neglam"] = tables.enter_context(nc.sbuf_tensor("neglam", [P, 1], F32))
                build_norm1(nc, A, keep)
                build_attention(nc, A, keep)
            keep["cvT"] = tsb("cvT", [P, DC, ROWS])
            build_conv(nc, A, keep)
            keep["mixT"] = tsb("mixT", [P, DC, ROWS])
            build_merge(nc, A, keep)
            build_out(nc, A, keep)
        build_peer(nc, A, keep)


INPUTS = ["x_prompt", "x_sample", "cache_k", "cache_v", "state_conv", "norm1_g", "w_in", "b_gate", "conv_w",
          "q_norm_g", "k_norm_g", "lam_q1", "lam_k1", "lam_q2", "lam_k2", "subln_g", "w_conv_out", "w_attn_out",
          "w_o", "norm2_g", "peer_wq", "peer_q_g", "peer_subkeys", "peer_u", "peer_v"]
OUTPUTS = {"y_prompt": ((1, SEQ, D), (1, SEQ, D)),
           "y_sample": ((1, DEC, D), (1, DEC, D)),
           "k_prompt": ((SEQ, D), (1, 1, SEQ, HEADS, 2, HD)),
           "v_prompt": ((SEQ, D), (1, 1, SEQ, HEADS, VD)),
           "conv_prompt": ((2, D), (1, 1, 2, D)),
           "k_sample": ((DEC, D), (1, 1, DEC, HEADS, 2, HD)),
           "v_sample": ((DEC, D), (1, 1, DEC, HEADS, VD)),
           "conv_sample": ((2, D), (1, 1, 2, D))}


def rope_tables():
    half = HD // 2
    inv = np.float32(10000.0) ** (-np.arange(half, dtype=np.float32) / np.float32(half))
    ang = np.arange((NT + 1) * P, dtype=np.float32)[:, None] * inv[None, :].astype(np.float32)
    cos, sin = np.cos(ang), np.sin(ang)
    out = []
    for table in (np.concatenate([cos, cos], 1), np.concatenate([-sin, sin], 1)):
        out.append(np.ascontiguousarray(table.reshape(NT + 1, P, HD).transpose(1, 0, 2)).astype(np.float32))
    return out


def program(nc, in_arrays):
    A = {}
    for name, a in in_arrays.items():
        A[name] = nc.dram_tensor(f"in_{name}", a.shape, mybir.dt.from_np(a.dtype), kind="ExternalInput").ap()
    for name, (shape, _) in OUTPUTS.items():
        A[name] = nc.dram_tensor(f"out_{name}", shape, F32, kind="ExternalOutput").ap()
    A["x1"] = nc.dram_tensor("x1_rows", (SEQ + P, D), F32, kind="Internal").ap()
    build(nc, A)


def kernel(**inputs):
    import concourse.bacc as bacc
    from concourse.bass_utils import run_bass_kernel_spmd as run
    arrays = {name: np.ascontiguousarray(inputs[name]) for name in INPUTS}
    for name in ("cache_k", "cache_v"):
        arrays[name] = arrays[name].reshape(PAST, D)
    arrays["rope_cos"], arrays["rope_sin"] = rope_tables()
    nc = bacc.Bacc("TRN2", target_bir_lowering=False, num_devices=1)
    program(nc, arrays)
    r = run(nc, [{f"in_{k}": v for k, v in arrays.items()}], core_ids=[0])
    got = r.results[0]
    return tuple(np.asarray(got[f"out_{name}"]).reshape(shape) for name, (_, shape) in OUTPUTS.items())
```

```python
from contextlib import ExitStack

import numpy as np
import concourse.bass as bass
from concourse import mybir

F32 = mybir.dt.float32
U32 = mybir.dt.uint32
ALU = mybir.AluOpType
ACT = mybir.ActivationFunctionType
AX = mybir.AxisListType
ds = bass.ds

P = 128
D = 1024
DC = D // P
SEQ, DEC = 1024, 32
ROWS = SEQ + DEC
NT = SEQ // P
PAST = 1024
HEADS = 8
HD = 64
VD = 128
GROUPS = 4
GW = 2 * VD
CHUNK = 64
EPS = 1e-6
LAM0 = 0.8 - 0.6
QKS = HD ** -0.5
LOW = -3.0e38
PART = ROWS // 3
QCOL, KCOL, VCOL = 3 * D, 4 * D, 5 * D
GACOL, GBCOL = 6 * D, 7 * D
TOPK = 16
NKEYS = 128
PH = 8
PQ = 2048
SLOTS = PH * TOPK
RING = 16
BY_PE = 12
DIAGS = 6


def rows_of(t):
    return DEC if isinstance(t, int) and t == NT else P


def hold(eng, sem, value, passed):
    eng.wait_ge(sem, value)
    if not isinstance(value, int):
        eng.sem_inc(passed, 1)


def semaphores(ctx, nc, block, names):
    return {n: ctx.enter_context(nc.semaphore(f"{block}_{n}")) for n in names.split()}


def build_norm1(nc, A, keep):
    with ExitStack() as ctx:
        def sb(name, shape, dt=F32):
            return ctx.enter_context(nc.sbuf_tensor("n1_" + name, shape, dt))

        s = semaphores(ctx, nc, "n1", "consts x_in0 x_in1 sq_done r_done xn_done tr_done cpa cpd passed_pool ident_done "
                 "lam_d lam_e tab_done sp_ok passed_pe passed_act passed_dve")
        x_in = [s["x_in0"], s["x_in1"]]
        xt = sb("xt", [P, 2, D])
        xn = sb("xn", [P, 2, D])
        junk = sb("junk", [P, D])
        g1b = sb("g1b", [P, D])
        ss = sb("ss", [P, 2])
        rr = sb("rr", [P, 2])
        cosd = sb("cosd", [P, NT + 1, HD])
        sind = sb("sind", [P, NT + 1, HD])
        gains = sb("gains", [P, 4, HD])
        lamv = sb("lamv", [P, 4, HD])
        lamp = sb("lamp", [P, 2, HD])
        lamd = sb("lamd", [P, 2])
        lame = sb("lame", [P, 2])
        ps = [ctx.enter_context(nc.psum_tensor(f"n1_ps{b}", [P, 2, 512], F32)) for b in range(2)]
        block = ctx.enter_context(nc.Block())
        N_CONST = 1 + 2 + 6 + 4 + 1

        def x_rows(t):
            if isinstance(t, int) and t == NT:
                return A["x_sample"][0]
            return A["x_prompt"][0, ds(t * P, P), :]

        @block.sync
        def _(sp):
            def load(t, b):
                sp.wait_ge(s["xn_done"], t + 1)
                sp.dma_start(xt[:rows_of(t), b, :], x_rows(t)).then_inc(x_in[b], 16)

            with sp.Fori(0, NT // 2) as pair:
                for b in range(2):
                    load(pair * 2 + b, b)
            load(NT, 0)

        @block.scalar
        def _(act):
            act.dma_start(g1b[:], A["norm1_g"].to_broadcast([P, D])).then_inc(s["consts"], 16)
            act.dma_start(cosd[:], A["rope_cos"]).then_inc(s["consts"], 16)
            act.dma_start(sind[:], A["rope_sin"]).then_inc(s["consts"], 16)
            h = HD // 2
            for k, name in enumerate(("q_norm_g", "k_norm_g")):
                g = A[name]
                act.dma_start(gains[:, 2 * k, :], g.to_broadcast([P, HD])).then_inc(s["consts"], 16)
                act.dma_start(gains[:, 2 * k + 1, 0:h], g[:, h:HD].to_broadcast([P, h])).then_inc(s["consts"], 16)
                act.dma_start(gains[:, 2 * k + 1, h:HD], g[:, 0:h].to_broadcast([P, h])).then_inc(s["consts"], 16)
            for k, name in enumerate(("lam_q1", "lam_k1", "lam_q2", "lam_k2")):
                act.dma_start(lamv[:, k, :], A[name].to_broadcast([P, HD])).then_inc(s["consts"], 16)
            act.dma_start(keep["subg"][:], A["subln_g"].to_broadcast([P, VD])).then_inc(s["consts"], 16)

            def tile(t, b, turn):
                n = rows_of(t)
                act.wait_ge(x_in[b], 16 * turn)
                nc.scalar.activation(junk[:n, :], xt[:n, b, :], ACT.Square, scale=D ** -0.5,
                                     accum_out=ss[:n, b:b + 1]).then_inc(s["sq_done"], 1)
                hold(act, s["tr_done"], t + 3, s["passed_act"])
                nc.scalar.copy(keep["xnT"][:, 0:4, ds(t * P, n)],
                               ps[b][:, 0, :].rearrange("p (c r) -> p c r", c=4)[:, :, 0:n]).then_inc(s["cpa"], 1)

            act.sem_inc(s["cpa"], 2)
            with act.Fori(0, NT // 2) as pair:
                for b in range(2):
                    tile(pair * 2 + b, b, pair + 1)
            tile(NT, 0, NT // 2 + 1)
            act.wait_ge(s["lam_d"], 1)
            nc.scalar.activation(lame[:], lamd[:], ACT.Exp).then_inc(s["lam_e"], 1)

        @block.gpsimd
        def _(pool):
            ident = keep["ident"]
            nc.gpsimd.memset(ident[:], 0.0)
            nc.gpsimd.memset(keep["mhalf"][:], -0.5)
            pool.drain()
            nc.gpsimd.affine_select(out=ident[:], in_=ident[:], compare_op=ALU.not_equal, fill=1.0, base=0,
                                    pattern=[[-1, P]], channel_multiplier=1).then_inc(s["ident_done"], 1)

            def tile(t, b):
                n = rows_of(t)
                hold(pool, s["sq_done"], t + 1, s["passed_pool"])
                nc.gpsimd.tensor_scalar(rr[:n, b:b + 1], ss[:n, b:b + 1], EPS, None, ALU.add)
                pool.drain()
                nc.gpsimd.tensor_tensor(rr[:n, b:b + 1], rr[:n, b:b + 1], keep["mhalf"][:n, 0:1],
                                        ALU.pow).then_inc(s["r_done"], 1)

            with pool.Fori(0, NT // 2) as pair:
                for b in range(2):
                    tile(pair * 2 + b, b)
            tile(NT, 0)

        @block.vector
        def _(dve):
            dve.sem_inc(s["xn_done"], 2)
            dve.sem_inc(s["cpd"], 2)
            dve.wait_ge(s["consts"], 16 * N_CONST)

            def tile(t, b):
                n = rows_of(t)
                dve.wait_ge(s["tr_done"], t + 1)
                dve.wait_ge(s["r_done"], t + 1)
                nc.vector.scalar_tensor_tensor(out=xn[:n, b, :], in0=xt[:n, b, :], scalar=rr[:n, b:b + 1],
                                               in1=g1b[:n, :], op0=ALU.mult, op1=ALU.mult).then_inc(s["xn_done"], 1)
                hold(dve, s["tr_done"], t + 3, s["passed_dve"])
                nc.vector.tensor_copy(keep["xnT"][:, 4:8, ds(t * P, n)],
                                      ps[b][:, 1, :].rearrange("p (c r) -> p c r", c=4)[:, :, 0:n]).then_inc(s["cpd"], 1)

            with dve.Fori(0, NT // 2) as pair:
                for b in range(2):
                    tile(pair * 2 + b, b)
            tile(NT, 0)

            for k, (ta, tb) in enumerate(((keep["qa"], keep["qb"]), (keep["ka"], keep["kb"]))):
                ga = gains[:, 2 * k:2 * k + 1, :].to_broadcast([P, NT + 1, HD])
                gb = gains[:, 2 * k + 1:2 * k + 2, :].to_broadcast([P, NT + 1, HD])
                nc.vector.tensor_tensor(ta[:], cosd[:], ga, ALU.mult)
                nc.vector.tensor_tensor(tb[:], sind[:], gb, ALU.mult)
            nc.vector.tensor_scalar(keep["subg"][:], keep["subg"][:], 1.0 - LAM0, None, ALU.mult)
            lv = lamv[:].rearrange("p (a b) d -> p a b d", b=2)
            nc.vector.tensor_tensor(lamp[:], lv[:, :, 0, :], lv[:, :, 1, :], ALU.mult)
            dve.drain()
            nc.vector.tensor_reduce(lamd[:], lamp[:], AX.X, ALU.add).then_inc(s["lam_d"], 1)
            dve.wait_ge(s["lam_e"], 1)
            nc.vector.tensor_tensor(keep["neglam"][:], lame[:, 1:2], lame[:, 0:1], ALU.subtract)
            dve.drain()
            nc.vector.tensor_scalar(keep["neglam"][:], keep["neglam"][:], -LAM0, None, ALU.add)

        @block.tensor
        def _(pe):
            pe.sem_inc(s["tr_done"], 2)
            pe.wait_ge(s["ident_done"], 1)

            def tile(t, b):
                n = rows_of(t)
                hold(pe, s["cpa"], t + 1, s["passed_pe"])
                hold(pe, s["cpd"], t + 1, s["passed_pe"])
                hold(pe, s["xn_done"], t + 3, s["passed_pe"])
                for c in range(DC):
                    o = ps[b][:, c // 4, (c % 4) * P:(c % 4) * P + n]
                    last = nc.tensor.transpose(o, xn[:n, b, c * P:(c + 1) * P], keep["ident"][:n, :n])
                last.then_inc(s["tr_done"], 1)

            with pe.Fori(0, NT // 2) as pair:
                for b in range(2):
                    tile(pair * 2 + b, b)
            tile(NT, 0)


def build_attention(nc, A, keep):
    NU = 2 * (NT + 1)
    with ExitStack() as ctx:
        def sb(name, shape, dt=F32):
            return ctx.enter_context(nc.sbuf_tensor("at_" + name, shape, dt))

        s = semaphores(ctx, nc, "at", "w_in0 w_in1 w_in2 kc_in vc_in pj_done evq evv sq_done ss_done rr_done qf_done tr_done trc "
                 "kct_done kct_cp k_out v_out kv_free wf_in0 wf_in1 consts f_done c_done u_done y_done tails out cv_out clear o_out sc_done mx_done ex_done a_done at_a at_d tc_a tc_d pv_done "
                 "so_done ro_done on_done ot_done otc passed_pe passed_act passed_dve passed_pool passed_sp")
        w_in = [s["w_in0"], s["w_in1"], s["w_in2"]]
        wf_in = [s["wf_in0"], s["wf_in1"]]
        w = [sb(f"w{k}", [P, DC, GW]) for k in range(3)]
        wf = sb("wf", [P, 2, DC, P])
        cw = sb("cw", [P, 3, DC])
        st = sb("st", [P, 2, DC])
        U = sb("U", [P, ROWS + 4])
        Y = sb("Y", [P, ROWS + 2])
        C = sb("C", [P, ROWS])
        cvr = sb("cvr", [P, 2, ROWS])
        oTg = sb("oTg", [P, 2, ROWS])
        tail = sb("tail", [P, 4, DC])
        kc = sb("kc", [P, DC, GW])
        vc = sb("vc", [P, DC, GW])
        kcT = sb("kcT", [P, 2, PAST])
        qT = sb("qT", [P, 2, ROWS])
        kT = sb("kT", [P, 2, ROWS])
        kf = sb("kf", [P, NT + 1, GW])
        V = sb("V", [P, NT + 1, GW])
        sq = sb("sq", [P, 2, GW])
        qn = sb("qn", [P, GW])
        t1 = sb("t1", [P, GW])
        t2 = sb("t2", [P, GW])
        qf = sb("qf", [P, 4, GW])
        ss = sb("ss", [P, 2, 4])
        rr = sb("rr", [P, 2, 4])
        p = sb("p", [P, 2, 2, ROWS])
        aT = sb("aT", [P, 2, (NT + 1) * P])
        mx = sb("mx", [P, 2, 2])
        nb = sb("nb", [P, 2, 2])
        Z = sb("Z", [P, 2, 2])
        rz = sb("rz", [P, 2])
        rl = sb("rl", [P, 1])
        so = sb("so", [P, 2])
        ro = sb("ro", [P, 2])
        on = sb("on", [P, 2, VD])
        oj = sb("oj", [P, VD])
        S = ctx.enter_context(nc.psum_tensor("at_S", [P, 4, 512], F32))
        B = [ctx.enter_context(nc.psum_tensor(f"at_B{k}", [P, 512], F32)) for k in range(4)]
        T = B[0:2]
        O = [B[2][:, 0:GW], B[2][:, GW:2 * GW]]
        F = B[3]
        ident, xnT = keep["ident"], keep["xnT"]
        block = ctx.enter_context(nc.Block())

        def wcols(kind, g):
            return A["w_in"][0, :, ds((QCOL, KCOL, VCOL)[kind] + g * GW, GW)].rearrange("(c p) n -> p c n", p=P)

        def cache(name, g):
            return A[name][:, ds(g * GW, GW)].rearrange("(c p) n -> p c n", p=P)

        def keys(t):
            return (t + 1) * P if t < NT else PAST + DEC

        def scores(c, t, n):
            first = 0 if t == NT else 2 * c
            banks = 3 if t == NT else 2
            return S[:n, first:first + banks, :].rearrange("p a b -> p (a b)")

        def part_pieces(z, row, part, shift):
            if part < 2:
                return [(z[:, 0:PART], row[:, part * PART:(part + 1) * PART])]
            cut = SEQ - 2 * PART
            return [(z[:, 0:cut], row[:, 2 * PART:SEQ]), (z[:, cut:PART], row[:, SEQ + shift:SEQ + shift + DEC])]

        @block.sync
        def _(sp):
            def load_wf(n, b, col):
                sp.dma_start(wf[:, b, :, :], A["w_in"][0, :, ds(col, P)]
                             .rearrange("(c p) n -> p c n", p=P)).then_inc(wf_in[b], 16)

            def conv_col(g, m):
                return (D, 2 * D, 0)[m % 3] + (g * 2 + m // 3) * P

            def load_w(kind, g):
                sp.dma_start(w[kind][:], wcols(kind, g)).then_inc(w_in[kind], 16)

            def stores(g, then_load):
                if then_load:
                    sp.wait_ge(s["kct_done"], 4 * (g + 1))
                    sp.dma_start(kc[:], cache("cache_k", g + 1)).then_inc(s["kc_in"], 16)
                    for kind in range(2):
                        sp.wait_ge(s["pj_done"], 27 * g + 9 * (kind + 1))
                        load_w(kind, g + 1)
                sp.wait_ge(s["qf_done"], NU * (g + 1))
                sp.dma_start(A["k_prompt"][:, ds(g * GW, GW)].rearrange("(t p) n -> p t n", p=P),
                             kf[:, 0:NT, :]).then_inc(s["k_out"], 16)
                sp.dma_start(A["k_sample"][:, ds(g * GW, GW)], kf[:DEC, NT, :]).then_inc(s["k_out"], 16)
                if then_load:
                    sp.wait_ge(s["pj_done"], 27 * (g + 1))
                    load_w(2, g + 1)
                sp.wait_ge(s["evv"], 9 * (g + 2))
                sp.dma_start(A["v_prompt"][:, ds(g * GW, GW)].rearrange("(t p) n -> p t n", p=P),
                             V[:, 0:NT, :]).then_inc(s["v_out"], 16)
                sp.dma_start(A["v_sample"][:, ds(g * GW, GW)], V[:DEC, NT, :]).then_inc(s["v_out"], 16)
                sp.wait_ge(s["k_out"], 32 * (g + 1))
                hold(sp, s["v_out"], 32 * (g + 1), s["passed_sp"])
                sp.sem_inc(s["kv_free"], 1)
                for m in range(6):
                    hold(sp, s["f_done"], NU * g + 3 * (m + 1), s["passed_sp"])
                    if m < 4:
                        load_wf(m, m % 2, conv_col(g, m + 2))
                    elif then_load:
                        load_wf(m, m % 2, conv_col(g + 1, m - 4))
                    if m % 3 == 2:
                        hold(sp, s["y_done"], 3 * (g * 2 + m // 3) + 6, s["passed_sp"])
                        sp.dma_start(A["cv_t"][ds((g * 2 + m // 3) * P, P), :], cvr[:, m // 3, :]).then_inc(s["cv_out"], 16)
                if then_load:
                    sp.wait_ge(s["pv_done"], NU * (g + 1))
                    sp.dma_start(vc[:], cache("cache_v", g + 1)).then_inc(s["vc_in"], 16)
                hold(sp, s["otc"], NU * (g + 1) + 2, s["passed_sp"])
                sp.dma_start(A["o_t"][ds(g * GW, GW), :].rearrange("(h p) r -> p h r", p=P), oTg[:]).then_inc(s["o_out"], 16)
                hold(sp, s["cv_out"], 32 * (g + 1), s["passed_sp"])
                hold(sp, s["o_out"], 16 * (g + 1), s["passed_sp"])
                sp.sem_inc(s["clear"], 1)

            sp.sem_inc(s["kv_free"], 1)
            sp.sem_inc(s["clear"], 1)
            sp.dma_start(kc[:], cache("cache_k", 0)).then_inc(s["kc_in"], 16)
            for kind in range(3):
                load_w(kind, 0)
            for m in range(2):
                load_wf(m, m, conv_col(0, m))
            sp.dma_start(vc[:], cache("cache_v", 0)).then_inc(s["vc_in"], 16)
            with sp.Fori(0, GROUPS - 1) as g:
                stores(g, True)
            stores(GROUPS - 1, False)
            with nc.allow_non_contiguous_dma(reason="two rows of state, channels in partitions"):
                for j in range(2):
                    for k, name in enumerate(("conv_prompt", "conv_sample")):
                        sp.dma_start(A[name][j].rearrange("(c p) -> p c", p=P), tail[:, 2 * k + j, :]).then_inc(s["out"], 16)
            sp.wait_ge(s["out"], 64)

        @block.tensor
        def _(pe):
            def cached_keys(g):
                pe.wait_ge(s["kc_in"], 16 * (g + 1))
                for m in range(4):
                    pe.wait_ge(s["kct_cp"], 4 * g + m + 1)
                    for k in range(4):
                        last = nc.tensor.transpose(S[:, 2 + m % 2, k * P:(k + 1) * P],
                                                   kc[:, 4 * (m % 2) + k, (m // 2) * P:(m // 2 + 1) * P], ident[:])
                    last.then_inc(s["kct_done"], 1)

            def project(g, u):
                kind, t = divmod(u, NT + 1)
                n = rows_of(t)
                if t == 0:
                    pe.wait_ge(w_in[kind], 16 * (g + 1))
                if u >= 4:
                    if u - 4 < NU:
                        hold(pe, s["evq"], NU * g + u - 3, s["passed_pe"])
                    else:
                        hold(pe, s["evv"], 9 * (g + 1) + u - 4 - NU + 1, s["passed_pe"])
                for c in range(DC):
                    last = nc.tensor.matmul(B[u % 4][:n, 0:GW], xnT[:, c, t * P:t * P + n], w[kind][:, c, :],
                                            start=(c == 0), stop=(c == DC - 1))
                last.then_inc(s["pj_done"], 1)

            def turn(g, u):
                kind, t = divmod(u, NT + 1)
                n = rows_of(t)
                hold(pe, s["trc"], NU * g + u + 1, s["passed_pe"])
                hold(pe, s["qf_done"], NU * g + u + 1, s["passed_pe"])
                for h in range(2):
                    src = qf[:n, u % 4, h * P:(h + 1) * P] if kind == 0 else kf[:n, t, h * P:(h + 1) * P]
                    last = nc.tensor.transpose(S[:, u % 2, h * P:h * P + n], src, ident[:n, :n])
                last.then_inc(s["tr_done"], 1)

            def score(g, i):
                h, t = divmod(i, NT + 1)
                n, nk = rows_of(t), keys(t)
                for c in range(2):
                    need = 2 * i + c if t == NT else (2 * i if t == 0 else 2 * i - 1 + c)
                    if i:
                        hold(pe, s["ex_done"], 4 * (NT + 1) * g + need, s["passed_pe"])
                    o = scores(c, t, n)
                    rows = slice(c * HD, (c + 1) * HD)
                    q = qT[rows, h, t * P:t * P + n]
                    if t < NT:
                        parts = [(k, kT[rows, h, k:min(k + 512, nk)]) for k in range(0, nk, 512)]
                    else:
                        parts = [(k, kcT[rows, h, k:k + 512]) for k in range(0, PAST, 512)]
                        parts.append((PAST, kT[rows, h, SEQ:ROWS]))
                    for k, keys_ap in parts:
                        last = nc.tensor.matmul(o[:, k:k + keys_ap.shape[1]], q, keys_ap, start=True, stop=True)
                    last.then_inc(s["sc_done"], 1)

            def turn_weights(g, i):
                h, t = divmod(i, NT + 1)
                n, nk = rows_of(t), keys(t)
                blocks = (nk + P - 1) // P
                hold(pe, s["tc_a"], NU * g + i + 1, s["passed_pe"])
                if t in range(4, NT):
                    hold(pe, s["tc_d"], 8 * g + 4 * h + t - 4 + 1, s["passed_pe"])
                hold(pe, s["a_done"], NU * g + i + 1, s["passed_pe"])
                for k in range(blocks):
                    m = min(P, nk - k * P)
                    o = T[0][:m, k * DEC:(k + 1) * DEC] if t == NT else T[k // 4][:, (k % 4) * P:(k % 4 + 1) * P]
                    last = nc.tensor.transpose(o, p[:n, i % 2, 0, k * P:k * P + m], ident[:n, :n])
                    if k == min(3, blocks - 1) and t < NT or t == NT and k == blocks - 1:
                        last.then_inc(s["at_a"], 1)
                    elif k == blocks - 1:
                        last.then_inc(s["at_d"], 1)

            def turn_out(g, i):
                n = rows_of(i % (NT + 1))
                hold(pe, s["on_done"], NU * g + i + 1, s["passed_pe"])
                nc.tensor.transpose(O[i % 2][:, P:P + n], on[:n, i % 2, :], ident[:n, :n]).then_inc(s["ot_done"], 1)

            def weigh(g, i):
                h, t = divmod(i, NT + 1)
                n, nk = rows_of(t), keys(t)
                blocks = (nk + P - 1) // P
                if i == NT:
                    hold(pe, s["vc_in"], 16 * (g + 1), s["passed_pe"])
                hold(pe, s["otc"], NU * g + i + 2, s["passed_pe"])
                hold(pe, s["tc_a"], NU * g + i + 2, s["passed_pe"])
                for k in range(blocks):
                    if t in range(4, NT) and k == 4:
                        hold(pe, s["tc_d"], 8 * g + 4 * h + t - 4 + 2, s["passed_pe"])
                    m = min(P, nk - k * P)
                    a = aT[:m, i % 2, k * n:(k + 1) * n]
                    v = (V[:m, k, h * P:(h + 1) * P] if t < NT or k == PAST // P
                         else vc[:, k, h * P:(h + 1) * P])
                    last = nc.tensor.matmul(O[i % 2][:n, 0:VD], a, v, start=(k == 0), stop=(k == blocks - 1))
                last.then_inc(s["pv_done"], 1)

            def conv_unit(g, i, halfway):
                cc, (kind, part) = i // 9, divmod(i % 9, 3)
                m = i // 3
                if part == 0:
                    hold(pe, wf_in[m % 2], 16 * (3 * g + m // 2 + 1), s["passed_pe"])
                left = 3 * (2 * g + cc)
                if i % 9 == 0:
                    hold(pe, s["y_done"], left + 3, s["passed_pe"])
                else:
                    before, p0 = divmod(i % 9 - 1, 3)
                    hold(pe, s[("c_done", "u_done", "y_done")[before]], left + p0 + 1 + (3 if before == 2 else 0),
                         s["passed_pe"])
                for c in range(DC):
                    if c == DC // 2:
                        halfway()
                    last = nc.tensor.matmul(F[:, 0:PART], wf[:, m % 2, c, :], xnT[:, c, part * PART:(part + 1) * PART],
                                            start=(c == 0), stop=(c == DC - 1))
                last.then_inc(s["f_done"], 1)

            with pe.Fori(0, GROUPS) as g:
                hold(pe, s["y_done"], 6 * g + 3, s["passed_pe"])
                hold(pe, s["otc"], NU * g + 2, s["passed_pe"])
                hold(pe, s["evv"], 9 * (g + 1), s["passed_pe"])
                cached_keys(g)
                for u in range(3 * (NT + 1)):
                    project(g, u)
                    if 0 <= u - 2 < NU:
                        turn(g, u - 2)
                hold(pe, s["evv"], 9 * (g + 2), s["passed_pe"])
                hold(pe, s["trc"], NU * (g + 1) + 2, s["passed_pe"])
                hold(pe, s["kct_cp"], 4 * (g + 1) + 2, s["passed_pe"])
                score(g, 0)
                for i in range(NU):
                    if i + 1 < NU:
                        score(g, i + 1)
                    turn_weights(g, i)
                    conv_unit(g, i, lambda: turn_out(g, i - 1) if i else None)
                    weigh(g, i)
                turn_out(g, NU - 1)

        @block.scalar
        def _(act):
            def square(g, u):
                n = rows_of(u % (NT + 1))
                if u >= 2:
                    act.wait_ge(s["ss_done"], NU * g + u - 1)
                act.wait_ge(s["pj_done"], 27 * g + u + 1)
                nc.scalar.activation(sq[:n, u % 2, :], B[u % 4][:n, 0:GW], ACT.Square,
                                     scale=HD ** -0.5).then_inc(s["sq_done"], 1)

            def keep_turned(g, u):
                kind, t = divmod(u, NT + 1)
                n = rows_of(t)
                act.wait_ge(s["tr_done"], NU * g + u + 5)
                dst = (qT, kT)[kind]
                nc.scalar.copy(dst[:, :, t * P:t * P + n],
                               S[:, u % 2, 0:GW].rearrange("p (h r) -> p h r", h=2)[:, :, 0:n]).then_inc(s["trc"], 1)

            def keep_value(g, u):
                t = u - NU
                n = rows_of(t)
                if t == 0:
                    act.wait_ge(s["kv_free"], g + 1)
                act.wait_ge(s["pj_done"], 27 * g + u + 1)
                nc.scalar.copy(V[:n, t, :], B[u % 4][:n, 0:GW]).then_inc(s["evv"], 1)

            def exps(g, i):
                t = i % (NT + 1)
                n, nk = rows_of(t), keys(t)
                for c in range(2):
                    act.wait_ge(s["mx_done"], 2 * NU * g + 2 * i + c + 1)
                    nc.scalar.activation(p[:n, i % 2, c, 0:nk], scores(c, t, n)[:, 0:nk], ACT.Exp, scale=QKS,
                                         bias=nb[:n, i % 2, c:c + 1],
                                         accum_out=Z[:n, i % 2, c:c + 1]).then_inc(s["ex_done"], 1)

            def keep_weights(g, i):
                t = i % (NT + 1)
                cols = (NT + 1) * DEC if t == NT else min(t + 1, 4) * P
                act.wait_ge(s["at_a"], NU * g + i + 1)
                if t == NT:
                    last = PAST // P * DEC
                    nc.scalar.copy(aT[:, i % 2, 0:last], T[0][:, 0:last])
                    nc.scalar.copy(aT[:DEC, i % 2, last:cols], T[0][:DEC, last:cols]).then_inc(s["tc_a"], 1)
                else:
                    nc.scalar.copy(aT[:, i % 2, 0:cols], T[0][:, 0:cols]).then_inc(s["tc_a"], 1)

            def keep_out(g, i):
                h, t = divmod(i, NT + 1)
                n = rows_of(t)
                hold(act, s["ot_done"], NU * g + i + 3, s["passed_act"])
                if i == 0:
                    hold(act, s["clear"], g + 1, s["passed_act"])
                nc.scalar.copy(oTg[:, h, t * P:t * P + n], O[i % 2][:, P:P + n]).then_inc(s["otc"], 1)

            def keep_c(g, i):
                part = i % 9
                if part < 3:
                    act.wait_ge(s["f_done"], NU * g + i + 1)
                    nc.scalar.copy(C[:, part * PART:(part + 1) * PART], F[:, 0:PART]).then_inc(s["c_done"], 1)

            def square_out(g, i):
                n = rows_of(i % (NT + 1))
                act.wait_ge(s["pv_done"], NU * g + i + 1)
                nc.scalar.activation(oj[:n, :], O[i % 2][:n, 0:VD], ACT.Square, scale=VD ** -0.5,
                                     accum_out=so[:n, i % 2:i % 2 + 1]).then_inc(s["so_done"], 1)

            for sem, credit in ((s["evv"], 9), (s["trc"], 2), (s["kct_cp"], 2), (s["tc_a"], 1), (s["otc"], 2)):
                act.sem_inc(sem, credit)
            with act.Fori(0, GROUPS) as g:
                for m in range(4):
                    act.wait_ge(s["kct_done"], 4 * g + m + 1)
                    nc.scalar.copy(kcT[:, m // 2, 512 * (m % 2):512 * (m % 2 + 1)],
                                   S[:, 2 + m % 2, :]).then_inc(s["kct_cp"], 1)
                for u in range(3 * (NT + 1)):
                    if u < NU:
                        square(g, u)
                    else:
                        keep_value(g, u)
                    if 0 <= u - 2 < NU:
                        keep_turned(g, u - 2)
                exps(g, 0)
                for i in range(NU):
                    if i + 1 < NU:
                        exps(g, i + 1)
                    keep_weights(g, i)
                    if i:
                        keep_out(g, i - 1)
                    keep_c(g, i)
                    square_out(g, i)
                keep_out(g, NU - 1)

        @block.gpsimd
        def _(pool):
            def rsqrt(dst, src, done):
                nc.gpsimd.tensor_scalar(dst, src, EPS, None, ALU.add)
                pool.drain()
                nc.gpsimd.tensor_tensor(dst, dst, keep["mhalf"][:dst.shape[0], 0:dst.shape[1]],
                                        ALU.pow).then_inc(done, 1)

            with nc.allow_non_contiguous_dma(reason="small vectors, channels in partitions"):
                for j in range(3):
                    pool.dma_start(cw[:, j, :], A["conv_w"][0, j].rearrange("(c p) -> p c", p=P)).then_inc(s["consts"], 16)
                for j in range(2):
                    pool.dma_start(st[:, j, :], A["state_conv"][0, 0, j].rearrange("(c p) -> p c", p=P)).then_inc(s["consts"], 16)

            with pool.Fori(0, GROUPS) as g:
                for u in range(NU):
                    n = rows_of(u % (NT + 1))
                    hold(pool, s["ss_done"], NU * g + u + 1, s["passed_pool"])
                    rsqrt(rr[:n, u % 2, :], ss[:n, u % 2, :], s["rr_done"])
                for i in range(NU):
                    n = rows_of(i % (NT + 1))
                    hold(pool, s["so_done"], NU * g + i + 1, s["passed_pool"])
                    rsqrt(ro[:n, i % 2:i % 2 + 1], so[:n, i % 2:i % 2 + 1], s["ro_done"])

        @block.vector
        def _(dve):
            def segs(ap):
                return ap.rearrange("p (a d) -> p a d", d=HD)

            def mean_square(g, u):
                n = rows_of(u % (NT + 1))
                dve.wait_ge(s["sq_done"], NU * g + u + 1)
                nc.vector.tensor_reduce(ss[:n, u % 2, :], segs(sq[:n, u % 2, :]), AX.X, ALU.add).then_inc(s["ss_done"], 1)

            def rotate(g, u):
                kind, t = divmod(u, NT + 1)
                n = rows_of(t)
                h = HD // 2
                ta, tb = ((keep["qa"], keep["qb"]), (keep["ka"], keep["kb"]))[kind]
                dve.wait_ge(s["rr_done"], NU * g + u + 1)
                nc.vector.tensor_tensor(segs(qn[:n, :]), segs(B[u % 4][:n, 0:GW]),
                                        rr[:n, u % 2, :].unsqueeze(2).to_broadcast([n, 4, HD]),
                                        ALU.mult).then_inc(s["evq"], 1)
                dve.drain()
                q3 = segs(qn[:n, :])
                nc.vector.tensor_tensor(segs(t1[:n, :]), q3, ta[:n, t:t + 1, :].to_broadcast([n, 4, HD]), ALU.mult)
                nc.vector.tensor_tensor(segs(t2[:n, :])[:, :, 0:h], q3[:, :, h:HD],
                                        tb[:n, t:t + 1, 0:h].to_broadcast([n, 4, h]), ALU.mult)
                nc.vector.tensor_tensor(segs(t2[:n, :])[:, :, h:HD], q3[:, :, 0:h],
                                        tb[:n, t:t + 1, h:HD].to_broadcast([n, 4, h]), ALU.mult)
                dve.drain()
                if kind == 0:
                    dve.wait_ge(s["tr_done"], NU * g + u + 1)
                    dst = qf[:n, u % 4, :]
                else:
                    if t == 0:
                        dve.wait_ge(s["kv_free"], g + 1)
                    dst = kf[:n, t, :]
                nc.vector.tensor_tensor(dst, t1[:n, :], t2[:n, :], ALU.add).then_inc(s["qf_done"], 1)

            def row_max(g, i):
                t = i % (NT + 1)
                n, nk = rows_of(t), keys(t)
                for c in range(2):
                    sc = scores(c, t, n)
                    dve.wait_ge(s["sc_done"], 2 * NU * g + 2 * i + c + 1)
                    if t < NT:
                        nc.vector.memset(sc[0:CHUNK, nk - CHUNK:nk], LOW)
                        dve.drain()
                    nc.vector.tensor_reduce(mx[:n, i % 2, c:c + 1], sc[:, 0:nk], AX.X, ALU.max)
                    dve.drain()
                    nc.vector.tensor_scalar(nb[:n, i % 2, c:c + 1], mx[:n, i % 2, c:c + 1], -QKS, None,
                                            ALU.mult).then_inc(s["mx_done"], 1)

            def difference(g, i):
                t = i % (NT + 1)
                n, nk = rows_of(t), keys(t)
                dve.wait_ge(s["ex_done"], 2 * NU * g + 2 * i + 2)
                nc.vector.reciprocal(rz[:n, :], Z[:n, i % 2, :])
                dve.drain()
                nc.vector.tensor_tensor(rl[:n, :], rz[:n, 1:2], keep["neglam"][:n, :], ALU.mult)
                dve.drain()
                nc.vector.tensor_scalar(p[:n, i % 2, 1, 0:nk], p[:n, i % 2, 1, 0:nk], rl[:n, 0:1], None, ALU.mult)
                dve.drain()
                nc.vector.scalar_tensor_tensor(out=p[:n, i % 2, 0, 0:nk], in0=p[:n, i % 2, 0, 0:nk],
                                               scalar=rz[:n, 0:1], in1=p[:n, i % 2, 1, 0:nk],
                                               op0=ALU.mult, op1=ALU.add).then_inc(s["a_done"], 1)

            def keep_weights(g, i):
                h, t = divmod(i, NT + 1)
                if t in range(4, NT):
                    cols = (t - 3) * P
                    dve.wait_ge(s["at_d"], 8 * g + 4 * h + t - 4 + 1)
                    nc.vector.tensor_copy(aT[:, i % 2, 4 * P:4 * P + cols], T[1][:, 0:cols]).then_inc(s["tc_d"], 1)

            def norm_out(g, i):
                n = rows_of(i % (NT + 1))
                dve.wait_ge(s["ot_done"], NU * g + i + 1)
                dve.wait_ge(s["ro_done"], NU * g + i + 1)
                nc.vector.scalar_tensor_tensor(out=on[:n, i % 2, :], in0=O[i % 2][:n, 0:VD],
                                               scalar=ro[:n, i % 2:i % 2 + 1], in1=keep["subg"][:n, :],
                                               op0=ALU.mult, op1=ALU.mult).then_inc(s["on_done"], 1)

            def conv_step(g, i):
                half, (kind, part) = i // 9, divmod(i % 9, 3)
                cc = g * 2 + half
                if kind == 1:
                    if part == 0:
                        nc.vector.tensor_copy(U[:, SEQ + 2:SEQ + 4], st[:, :, ds(cc, 1)].rearrange("p j c -> p (j c)"))
                    dve.wait_ge(s["c_done"], 3 * cc + 3)
                    hold(dve, s["f_done"], NU * g + i + 1, s["passed_dve"])
                    for (zp, up), (_, cp) in zip(part_pieces(F, U[:, 2:], part, 2), part_pieces(F, C, part, 0)):
                        last = nc.vector.tensor_tensor(up, zp, cp, ALU.mult)
                    last.then_inc(s["u_done"], 1)
                    if part == 2:
                        m = ROWS + 2
                        dve.drain()
                        nc.vector.tensor_scalar(Y[:], U[:, 0:m], cw[:, 0, ds(cc, 1)], None, ALU.mult)
                        for j in (1, 2):
                            dve.drain()
                            nc.vector.scalar_tensor_tensor(out=Y[:], in0=U[:, j:j + m], scalar=cw[:, j, ds(cc, 1)],
                                                           in1=Y[:], op0=ALU.mult, op1=ALU.add)
                        nc.vector.tensor_copy(tail[:, 0:2, ds(cc, 1)].rearrange("p j c -> p (j c)"), U[:, SEQ:SEQ + 2])
                        nc.vector.tensor_copy(tail[:, 2:4, ds(cc, 1)].rearrange("p j c -> p (j c)"),
                                              U[:, SEQ + 2 + DEC:SEQ + 4 + DEC])
                        dve.drain()
                elif kind == 2:
                    if i == 6:
                        hold(dve, s["clear"], g + 1, s["passed_dve"])
                    dve.wait_ge(s["f_done"], NU * g + i + 1)
                    for (zp, yp), (_, op) in zip(part_pieces(F, Y, part, 2), part_pieces(F, cvr[:, half, :], part, 0)):
                        last = nc.vector.tensor_tensor(op, zp, yp, ALU.mult)
                    last.then_inc(s["y_done"], 1)

            dve.sem_inc(s["y_done"], 3)
            nc.vector.memset(U[:, 0:2], 0.0)
            dve.wait_ge(s["consts"], 80)
            dve.sem_inc(s["tc_d"], 1)
            dve.sem_inc(s["tr_done"], 4)
            dve.sem_inc(s["ot_done"], 2)
            with dve.Fori(0, GROUPS) as g:
                for u in range(NU):
                    mean_square(g, u)
                    if u:
                        rotate(g, u - 1)
                rotate(g, NU - 1)
                row_max(g, 0)
                for i in range(NU):
                    difference(g, i)
                    if i + 1 < NU:
                        row_max(g, i + 1)
                    if i:
                        norm_out(g, i - 1)
                    keep_weights(g, i)
                    conv_step(g, i)
                norm_out(g, NU - 1)


def products(nc, pe, out, w, src, done):
    for part in range(3):
        for c in range(DC):
            last = nc.tensor.matmul(out[:, part, 0:PART], w[:, c, :], src[:, c, part * PART:(part + 1) * PART],
                                    start=(c == 0), stop=(c == DC - 1))
    last.then_inc(done, 1)


def thirds(ap):
    return ap.rearrange("p (a b) -> p a b", a=3)


def build_merge(nc, A, keep):
    with ExitStack() as ctx:
        def sb(name, shape, dt=F32):
            return ctx.enter_context(nc.sbuf_tensor("mg_" + name, shape, dt))

        s = semaphores(ctx, nc, "mg", "w_in0 w_in1 consts cv_in o_in z_done g_done m_done passed_dve passed_act")
        w_in = [s["w_in0"], s["w_in1"]]
        w = sb("w", [P, 2, 4, DC, P])
        bg = sb("bg", [P, 2, DC])
        G = sb("G", [P, 2, ROWS])
        M = sb("M", [P, 2, ROWS])
        Z = [ctx.enter_context(nc.psum_tensor(f"mg_Z{b}", [P, 3, 512], F32)) for b in range(2)]
        mixT = keep["mixT"]
        block = ctx.enter_context(nc.Block())

        @block.sync
        def _(sp):
            def load(cc, b):
                srcs = (A["w_in"][0, :, ds(GACOL + cc * P, P)], A["w_conv_out"][0, :, ds(cc * P, P)],
                        A["w_in"][0, :, ds(GBCOL + cc * P, P)], A["w_attn_out"][0, :, ds(cc * P, P)])
                for k in range(4):
                    sp.dma_start(w[:, b, k, :, :], srcs[k].rearrange("(c p) n -> p c n", p=P)).then_inc(w_in[b], 16)

            load(0, 0)
            sp.dma_start(keep["cvT"][:], A["cv_t"].rearrange("(c p) r -> p c r", p=P)).then_inc(s["cv_in"], 16)
            sp.dma_start(keep["oT"][:], A["o_t"].rearrange("(c p) r -> p c r", p=P)).then_inc(s["o_in"], 16)
            load(1, 1)
            with sp.Fori(0, DC // 2 - 1) as pair:
                for b in range(2):
                    sp.wait_ge(s["z_done"], 8 * pair + 4 * (b + 1))
                    load(pair * 2 + 2 + b, b)

        @block.gpsimd
        def _(pool):
            with nc.allow_non_contiguous_dma(reason="gate biases, channels in partitions"):
                for j in range(2):
                    pool.dma_start(bg[:, j, :], A["b_gate"][0, j].rearrange("(c p) -> p c", p=P)).then_inc(s["consts"], 16)

        @block.tensor
        def _(pe):
            with pe.Fori(0, DC // 2) as pair:
                for b in range(2):
                    pe.wait_ge(w_in[b], 64 * (pair + 1))
                    for k in range(4):
                        if k % 2 == 0:
                            pe.wait_ge(s["g_done"], 4 * pair + 2 * b + k // 2 + 1)
                        else:
                            pe.wait_ge(s["m_done"], 4 * pair + 2 * b + k // 2 + 1)
                            pe.wait_ge(s["cv_in"] if k == 1 else s["o_in"], 16)
                        products(nc, pe, Z[k % 2], w[:, b, k], (keep["xnT"], keep["cvT"], keep["xnT"], keep["oT"])[k],
                                 s["z_done"])

        @block.scalar
        def _(act):
            act.sem_inc(s["g_done"], 1)
            act.wait_ge(s["consts"], 32)
            with act.Fori(0, DC // 2) as pair:
                for b in range(2):
                    for k in range(2):
                        act.wait_ge(s["m_done"], 4 * pair + max(2 * b + k, 1))
                        hold(act, s["z_done"], 8 * pair + 4 * b + 2 * k + 1, s["passed_act"])
                        nc.scalar.activation(thirds(G[:, k, :]), Z[0][:, :, 0:PART], ACT.Sigmoid,
                                             bias=bg[:, k, ds(pair * 2 + b, 1)]).then_inc(s["g_done"], 1)

        @block.vector
        def _(dve):
            dve.sem_inc(s["m_done"], 1)
            with dve.Fori(0, DC // 2) as pair:
                for b in range(2):
                    for k in range(2):
                        dve.wait_ge(s["g_done"], 4 * pair + 2 * b + k + 2)
                        dve.wait_ge(s["z_done"], 8 * pair + 4 * b + 2 * k + 2)
                        nc.vector.tensor_tensor(thirds(M[:, k, :]), Z[1][:, :, 0:PART], thirds(G[:, k, :]),
                                                ALU.mult).then_inc(s["m_done"], 1)
                    dve.drain()
                    nc.vector.tensor_tensor(mixT[:, ds(pair * 2 + b, 1), :], M[:, 0:1, :], M[:, 1:2, :], ALU.add)
                    dve.drain()


def build_out(nc, A, keep):
    with ExitStack() as ctx:
        def sb(name, shape, dt=F32):
            return ctx.enter_context(nc.sbuf_tensor("ou_" + name, shape, dt))

        s = semaphores(ctx, nc, "ou", "w_in0 w_in1 x_in0 x_in1 x_in2 z_done a_done out0 out1 out2")
        w_in = [s["w_in0"], s["w_in1"]]
        x_in = [s["x_in0"], s["x_in1"], s["x_in2"]]
        out = [s["out0"], s["out1"], s["out2"]]
        w = sb("w", [P, DC, D])
        xt = sb("xt", [P, 3, D])
        Z = [ctx.enter_context(nc.psum_tensor(f"ou_Z{b}", [P, 2, 512], F32)) for b in range(2)]
        mixT = keep["mixT"]
        x1 = A["x1"]
        block = ctx.enter_context(nc.Block())

        def load_x(eng, t):
            src = A["x_sample"][0] if t == NT else A["x_prompt"][0, t * P:(t + 1) * P, :]
            eng.dma_start(xt[:rows_of(t), t % 3, :], src).then_inc(x_in[t % 3], 16)

        @block.sync
        def _(sp):
            for h in range(2):
                sp.dma_start(w[:, :, h * 512:(h + 1) * 512],
                             A["w_o"][0, :, h * 512:(h + 1) * 512].rearrange("(c p) n -> p c n", p=P)).then_inc(w_in[h], 16)
            for t in range(3):
                load_x(sp, t)
            for t in range(NT + 1):
                sp.wait_ge(s["a_done"], t + 1)
                if t < NT:
                    sp.dma_start(x1[t * P:(t + 1) * P, :], xt[:, t % 3, :]).then_inc(out[t % 3], 16)
                else:
                    for q in range(4):
                        sp.dma_start(x1[SEQ + q * DEC:SEQ + (q + 1) * DEC, :], xt[:DEC, t % 3, :]).then_inc(out[t % 3], 16)
                if 1 <= t and t + 2 <= NT:
                    sp.wait_ge(out[(t - 1) % 3], 16 * ((t - 1) // 3 + 1))
                    load_x(sp, t + 2)
            for b in range(3):
                tiles = len(range(b, NT + 1, 3)) + (3 if NT % 3 == b else 0)
                sp.wait_ge(out[b], 16 * tiles)

        @block.tensor
        def _(pe):
            for t in range(NT + 1):
                n = rows_of(t)
                if t >= 2:
                    pe.wait_ge(s["a_done"], t - 1)
                for h in range(2):
                    if t == 0:
                        pe.wait_ge(w_in[h], 16)
                    for c in range(DC):
                        last = nc.tensor.matmul(Z[t % 2][:n, h, :], mixT[:, c, t * P:t * P + n],
                                                w[:, c, h * 512:(h + 1) * 512], start=(c == 0), stop=(c == DC - 1))
                last.then_inc(s["z_done"], 1)

        @block.vector
        def _(dve):
            for t in range(NT + 1):
                n = rows_of(t)
                dve.wait_ge(x_in[t % 3], 16 * (t // 3 + 1))
                dve.wait_ge(s["z_done"], t + 1)
                nc.vector.tensor_tensor(xt[:n, t % 3, :], Z[t % 2][:n, :, :].rearrange("p a b -> p (a b)"),
                                        xt[:n, t % 3, :], ALU.add).then_inc(s["a_done"], 1)


def build_peer(nc, A, keep):
    with ExitStack() as ctx:
        def sb(name, shape, dt=F32):
            return ctx.enter_context(nc.sbuf_tensor("pe_" + name, shape, dt))

        s = semaphores(ctx, nc, "pe", "wq_in consts setup sk_t x_in0 x_in1 y_out used_u used_pe used_dve dg_done part_done idx_ready staged xsq r_done xn_done xt_done "
                 "xt_copied q_done qsq rq_done qn_done qt_done qt_copied s_done s_copied s_used dots_done gelu_done "
                 "acc_done hw_done gm_done ge_done fin_p fin_d passed_pool passed_dve passed_act passed_pe sel_done")
        landed = [ctx.enter_context(nc.semaphore(f"pe_landed{j}")) for j in range(RING)]
        x_in = [s["x_in0"], s["x_in1"]]
        wq = sb("wq", [P, DC, PQ])
        ring = sb("ring", [P, RING, D])
        g2b = sb("g2b", [P, D])
        xa = sb("xa", [P, 2, D])
        xb = sb("xb", [P, 2, D])
        xT = sb("xT", [P, DC, P])
        qn = sb("qn", [P, PQ])
        qT = sb("qT", [P, 2 * PH, P])
        sc = sb("sc", [P, 2 * PH, NKEYS])
        skT = sb("skT", [P, 2, NKEYS])
        gq = sb("gq", [P, 2])
        sel = sb("sel", [P, DEC])
        iot = sb("iot", [P, TOPK])
        idx = sb("idx", [P, 2, SLOTS], U32)
        gw = sb("gw", [P, 2, SLOTS])
        idst = sb("idst", [P, 2, TOPK], U32)
        dots16 = sb("dots16", [P, TOPK])
        hd = sb("hd", [P, SLOTS])
        hw = sb("hw", [P, SLOTS])
        ssx = sb("ssx", [P, 1])
        rx = sb("rx", [P, 1])
        qs = sb("qs", [P, PH])
        rq = sb("rq", [P, PH])
        sw = sb("sw", [P, 2, NKEYS])
        sw2 = sb("sw2", [P, 2, NKEYS])
        m16 = sb("m16", [P, 2, TOPK])
        i16 = sb("i16", [P, 2, TOPK], U32)
        cand = sb("cand", [P, TOPK * TOPK])
        cand2 = sb("cand2", [P, TOPK * TOPK])
        b16 = sb("b16", [P, TOPK])
        j16 = sb("j16", [P, TOPK], U32)
        itop = sb("itop", [P, PH, 2 * TOPK])
        best = sb("best", [P, PH, TOPK])
        pick = sb("pick", [P, PH, TOPK], U32)
        pk = sb("pk", [P, 2, SLOTS], U32)
        pf = sb("pf", [P, 2, PH, TOPK])
        oh = sb("oh", [P, PH // 2, TOPK, TOPK])
        e01 = sb("e01", [P, 2, PH, TOPK])
        gs = sb("gs", [P, PH])
        dg = sb("dg", [P, DIAGS, P])
        ps = ctx.enter_context(nc.psum_tensor("pe_ps", [P, 8, 512], F32))
        acc = ps[:, 0:2, :].rearrange("p a b -> p (a b)")
        lo = ps[:, 2:4, :].rearrange("p a b -> p (a b)")
        hi = ps[:, 4:8, :].rearrange("p a b -> p (a b)")
        ident = keep["ident"]
        x1 = A["x1"]
        block = ctx.enter_context(nc.Block())

        @block.sync
        def _(sp):
            sp.dma_start(xa[:, 0, :], x1[0:P, :]).then_inc(x_in[0], 16)
            sp.dma_start(g2b[:], A["norm2_g"].to_broadcast([P, D])).then_inc(s["consts"], 16)
            sp.dma_start(sw[:], A["peer_subkeys"][0].rearrange("c k d -> k c d")).then_inc(s["consts"], 16)
            with nc.allow_non_contiguous_dma(reason="a vector, channels in partitions"):
                sp.dma_start(gq[:], A["peer_q_g"][0].rearrange("(c p) -> p c", p=P)).then_inc(s["consts"], 16)
            sp.dma_start(wq[:], A["peer_wq"][0].rearrange("(c p) n -> p c n", p=P)).then_inc(s["wq_in"], 16)

            def tile(pair, b):
                t = pair * 2 + b
                sp.dma_start(xa[:, 1 - b, :], x1[ds((t + 1) * P, P), :]).then_inc(x_in[1 - b], 16)
                sp.wait_ge(s["acc_done"], t + 1)
                sp.dma_start(A["y_prompt"][0, ds(t * P, P), :], xa[:, b, :]).then_inc(s["y_out"], 16)
                hold(sp, s["y_out"], 16 * (t + 1), s["fin_p"])

            with sp.Fori(0, NT // 2) as pair:
                for b in range(2):
                    tile(pair, b)
            sp.wait_ge(s["acc_done"], NT + 2)
            sp.dma_start(A["y_sample"][0], xb[:DEC, 1, :]).then_inc(s["y_out"], 16)
            sp.wait_ge(s["y_out"], 16 * (NT + 1))

        @block.gpsimd
        def _(pool):
            nc.gpsimd.memset(sel[:], 0.0)
            nc.gpsimd.iota(idst[:, 0, :], pattern=[[1, TOPK]], base=0, channel_multiplier=0)
            pool.drain()
            nc.gpsimd.tensor_copy(iot[:], idst[:, 0, :]).then_inc(s["setup"], 1)
            for q in range(4):
                nc.gpsimd.affine_select(out=sel[:], in_=sel[:], compare_op=ALU.not_equal, fill=1.0, base=-DEC * q,
                                        pattern=[[-1, DEC]], channel_multiplier=1)
                pool.drain()
            pool.sem_inc(s["sel_done"], 1)

            def rsqrt(dst, src, done):
                nc.gpsimd.tensor_scalar(dst, src, EPS, None, ALU.add)
                pool.drain()
                nc.gpsimd.tensor_tensor(dst, dst, keep["mhalf"][:, 0:dst.shape[1]], ALU.pow).then_inc(done, 1)

            def norm_x(t):
                hold(pool, s["xsq"], t + 1, s["passed_pool"])
                rsqrt(rx[:], ssx[:], s["r_done"])

            def norm_q(t):
                hold(pool, s["qsq"], t + 1, s["passed_pool"])
                rsqrt(rq[:], qs[:], s["rq_done"])

            def gather(src, table, first, group, par, before):
                kind, old = before
                for j in range(RING):
                    if j % 4 == 0:
                        if kind == "u":
                            hold(pool, s["used_u"], old * RING + j + 4, s["passed_pool"])
                        elif j < BY_PE:
                            hold(pool, s["used_pe"], (old + 1) * BY_PE + j + 4, s["passed_pool"])
                        else:
                            hold(pool, s["used_dve"], (old + 1) * (RING - BY_PE) + j + 4 - BY_PE, s["passed_pool"])
                    if j == 0:
                        nc.gpsimd.tensor_copy(idst[:, par, :], src[:, ds(first, TOPK)]).then_inc(s["staged"], 1)
                        hold(pool, s["staged"], group + 1, s["passed_pool"])
                    nc.gpsimd.indirect_dma_start(
                        out=ring[:, j, :], out_offset=None, in_=table,
                        in_offset=bass.IndirectOffsetOnAxis(ap=idst[:, par, j:j + 1], axis=0)).then_inc(landed[j], 16)

            def pair_of(t, b, name, h, before):
                phase = 0 if name == "peer_u" else 8
                for par in range(2):
                    kind, old = before if par == 0 else (name[-1], t * 8 + h)
                    gather(idx[:, b, :], A[name][0], (h + par) * TOPK, t * 16 + phase + h + par, par, (kind, old))

            def tile(pair, b):
                t = pair * 2 + b
                hold(pool, s["idx_ready"], t + 1, s["passed_pool"])
                pair_of(t, b, "peer_u", 0, ("v", t * 8 - 1))
                norm_x(t + 1)
                with pool.Fori(1, 3) as k:
                    pair_of(t, b, "peer_u", k * 2, ("u", t * 8 + k * 2 - 1))
                norm_q(t + 1)
                pair_of(t, b, "peer_u", 6, ("u", t * 8 + 5))
                pair_of(t, b, "peer_v", 0, ("u", t * 8 + 7))
                with pool.Fori(1, 4) as k:
                    pair_of(t, b, "peer_v", k * 2, ("v", t * 8 + k * 2 - 1))

            norm_x(0)
            norm_q(0)
            with pool.Fori(0, NT // 2) as pair:
                for b in range(2):
                    tile(pair, b)
            pool.wait_ge(s["idx_ready"], NT + 2)
            for k, before in enumerate((("v", NT * 8 - 1), ("u", NT * 8), ("u", NT * 8 + 1), ("v", NT * 8))):
                gather(idx[:, 1, :], A["peer_u"][0] if k < 2 else A["peer_v"][0], (k % 2) * TOPK, NT * 16 + k, k % 2,
                       before)

        @block.tensor
        def _(pe):
            pe.wait_ge(s["consts"], 48)
            for c in range(2):
                last = nc.tensor.transpose(ps[:, 7, c * P:(c + 1) * P], sw[:, c, :], ident[:])
            last.then_inc(s["sk_t"], 1)

            def query(t):
                hold(pe, s["xn_done"], t + 1, s["passed_pe"])
                for c in range(DC):
                    last = nc.tensor.transpose(lo[:, c * P:(c + 1) * P], xb_of(t)[:, c * P:(c + 1) * P], ident[:])
                last.then_inc(s["xt_done"], 1)
                hold(pe, s["xt_copied"], t + 1, s["passed_pe"])
                for q in range(4):
                    for c in range(DC):
                        last = nc.tensor.matmul(hi[:, q * 512:(q + 1) * 512], xT[:, c, :], wq[:, c, q * 512:(q + 1) * 512],
                                                start=(c == 0), stop=(c == DC - 1))
                last.then_inc(s["q_done"], 1)
                hold(pe, s["qn_done"], t + 1, s["passed_pe"])
                for m in range(2):
                    if m:
                        hold(pe, s["qt_copied"], 2 * t + 1, s["passed_pe"])
                    for k in range(PH):
                        last = nc.tensor.transpose(lo[:, k * P:(k + 1) * P],
                                                   qn[:, (m * PH + k) * P:(m * PH + k + 1) * P], ident[:])
                    last.then_inc(s["qt_done"], 1)
                hold(pe, s["qt_copied"], 2 * t + 2, s["passed_pe"])
                for k in range(2 * PH):
                    last = nc.tensor.matmul(hi[:, k * P:(k + 1) * P], qT[:, k, :], skT[:, k % 2, :], start=True, stop=True)
                last.then_inc(s["s_done"], 1)

            half = [0]

            def xb_of(t):
                return xb[:, half[0], :]

            pe.wait_ge(s["setup"], 2)
            pe.wait_ge(s["wq_in"], 16)
            query(0)

            def weigh(t, h, group, start, stop):
                for j in range(BY_PE):
                    hold(pe, s["dg_done"], (t * 8 + h) * BY_PE + j + 1, s["passed_pe"])
                    pe.wait_ge(landed[j], 16 * (group + 1))
                    for k in range(2):
                        last = nc.tensor.matmul(acc[:, k * 512:(k + 1) * 512], dg[:, j % DIAGS, :],
                                                ring[:, j, k * 512:(k + 1) * 512], start=start and j == 0,
                                                stop=stop and j == BY_PE - 1, skip_group_check=True)
                    last.then_inc(s["used_pe"], 1)

            pe.sem_inc(s["used_pe"], BY_PE)
            with pe.Fori(0, NT // 2) as pair:
                for b in range(2):
                    t = pair * 2 + b
                    half[0] = 1 - b
                    query(t + 1)
                    hold(pe, s["part_done"], t + 1, s["passed_pe"])
                    weigh(t, 0, t * 16 + 8, True, False)
                    with pe.Fori(1, 7) as h:
                        weigh(t, h, t * 16 + 8 + h, False, False)
                    weigh(t, 7, t * 16 + 15, False, True)
            pe.wait_ge(s["part_done"], NT + 1)
            for k in range(2):
                weigh(NT, k, NT * 16 + 2 + k, k == 0, k == 1)
            pe.wait_ge(s["sel_done"], 1)
            pe.wait_ge(s["acc_done"], NT + 1)
            for h in range(2):
                last = nc.tensor.matmul(lo[:DEC, h * 512:(h + 1) * 512], sel[:], xa[:, 1, h * 512:(h + 1) * 512],
                                        start=True, stop=True)
            last.then_inc(s["fin_d"], 1)

        @block.scalar
        def _(act):
            act.wait_ge(s["sk_t"], 1)
            nc.scalar.copy(skT[:].rearrange("p c k -> p (c k)"), ps[:, 7, 0:2 * P]).then_inc(s["setup"], 1)

            def query(t, b, turn):
                act.wait_ge(x_in[b], 16 * turn)
                nc.scalar.activation(xT[:].rearrange("p c k -> p (c k)"), xa[:, b, :], ACT.Square, scale=D ** -0.5,
                                     accum_out=ssx[:]).then_inc(s["xsq"], 1)
                act.drain()
                act.wait_ge(s["xt_done"], t + 1)
                for k in range(2):
                    last = nc.scalar.copy(xT[:, 4 * k:4 * k + 4, :].rearrange("p c k -> p (c k)"), lo[:, k * 512:(k + 1) * 512])
                last.then_inc(s["xt_copied"], 1)
                act.wait_ge(s["q_done"], t + 1)
                for h in range(PH):
                    last = nc.scalar.activation(qn[:, h * 256:(h + 1) * 256], hi[:, h * 256:(h + 1) * 256], ACT.Square,
                                                scale=256 ** -0.5, accum_out=qs[:, h:h + 1])
                last.then_inc(s["qsq"], 1)
                act.drain()
                act.wait_ge(s["rq_done"], t + 1)
                for h in range(PH):
                    last = nc.scalar.activation(qn[:, h * 256:(h + 1) * 256], hi[:, h * 256:(h + 1) * 256], ACT.Copy,
                                                scale=rq[:, h:h + 1])
                last.then_inc(s["qn_done"], 1)
                lo4 = lo.rearrange("p (h c r) -> p h c r", h=PH // 2, c=2)
                qT4 = qT[:].rearrange("p (h c) r -> p h c r", c=2)
                for m in range(2):
                    act.wait_ge(s["qt_done"], 2 * t + m + 1)
                    for k in range(2):
                        for c in range(2):
                            last = nc.scalar.activation(qT4[:, 4 * m + 2 * k:4 * m + 2 * k + 2, c, :],
                                                        lo4[:, 2 * k:2 * k + 2, c, :], ACT.Copy, scale=gq[:, c:c + 1])
                    last.then_inc(s["qt_copied"], 1)
                act.wait_ge(s["s_used"], t + 1)
                act.wait_ge(s["s_done"], t + 1)
                for k in range(4):
                    last = nc.scalar.copy(sc[:, 4 * k:4 * k + 4, :].rearrange("p c k -> p (c k)"), hi[:, k * 512:(k + 1) * 512])
                last.then_inc(s["s_copied"], 1)

            def gelu(t, n):
                act.wait_ge(s["dots_done"], t + 1)
                nc.scalar.activation(hw[:, 0:n], hd[:, 0:n], ACT.Gelu).then_inc(s["gelu_done"], 1)

            def diagonals(t, h):
                for j in range(BY_PE):
                    hold(act, s["used_pe"], (t * 8 + h + 1) * BY_PE + j + 1 - DIAGS, s["passed_act"])
                    nc.scalar.activation(dg[:, j % DIAGS, :], ident[:], ACT.Copy,
                                         scale=hw[:, ds(h * TOPK + j, 1)]).then_inc(s["dg_done"], 1)

            def exps(t):
                act.wait_ge(s["gm_done"], t + 1)
                nc.scalar.activation(best[:], best[:], ACT.Exp).then_inc(s["ge_done"], 1)

            act.wait_ge(s["consts"], 48)
            query(0, 0, 1)
            exps(0)
            with act.Fori(0, NT // 2) as pair:
                for b in range(2):
                    t = pair * 2 + b
                    query(t + 1, 1 - b, pair + 1 + b)
                    gelu(t, SLOTS)
                    hold(act, s["hw_done"], t + 1, s["passed_act"])
                    with act.Fori(0, PH) as h:
                        diagonals(t, h)
                    exps(t + 1)
            gelu(NT, DEC)
            act.wait_ge(s["hw_done"], NT + 1)
            for k in range(2):
                diagonals(NT, k)

        @block.vector
        def _(dve):
            def top16(val, ind, src, spare):
                n = len(src)
                for k in range(n):
                    nc.vector.max(val[k][:, 0:8], src[k])
                dve.drain()
                for k in range(n):
                    nc.vector.max_index(ind[k][:, 0:8], val[k][:, 0:8], src[k])
                    nc.vector.match_replace(spare[k], val[k][:, 0:8], src[k], LOW)
                dve.drain()
                for k in range(n):
                    nc.vector.max(val[k][:, 8:16], spare[k])
                dve.drain()
                for k in range(n):
                    nc.vector.max_index(ind[k][:, 8:16], val[k][:, 8:16], spare[k])
                dve.drain()

            def topk(h):
                nc.vector.tensor_copy(sw[:], sc[:, ds(h * 2, 2), :])
                dve.drain()
                top16([m16[:, c, :] for c in range(2)], [i16[:, c, :] for c in range(2)],
                      [sw[:, c, :] for c in range(2)], [sw2[:, c, :] for c in range(2)])
                nc.vector.tensor_tensor(cand[:].rearrange("p (i j) -> p i j", i=TOPK),
                                        m16[:, 0, :].unsqueeze(2).to_broadcast([P, TOPK, TOPK]),
                                        m16[:, 1:2, :].to_broadcast([P, TOPK, TOPK]), ALU.add)
                nc.vector.tensor_copy(itop[:, ds(h, 1), :].rearrange("p h k -> p (h k)"),
                                      i16[:].rearrange("p c k -> p (c k)"))
                dve.drain()
                top16([b16[:]], [j16[:]], [cand[:]], [cand2[:]])
                nc.vector.tensor_copy(best[:, ds(h, 1), :].rearrange("p h k -> p (h k)"), b16[:])
                nc.vector.tensor_copy(pick[:, ds(h, 1), :].rearrange("p h k -> p (h k)"), j16[:])

            def places():
                flat = pick[:].rearrange("p h k -> p (h k)")
                nc.vector.tensor_scalar(pk[:, 0, :], flat, 4, None, ALU.logical_shift_right)
                nc.vector.tensor_scalar(pk[:, 1, :], flat, TOPK - 1, None, ALU.bitwise_and)
                dve.drain()
                nc.vector.tensor_copy(pf[:].rearrange("p c h k -> p (c h k)"), pk[:].rearrange("p c k -> p (c k)"))
                dve.drain()

            def keys_of(part):
                hs = slice(part * PH // 2, (part + 1) * PH // 2)
                shape = [P, PH // 2, TOPK, TOPK]
                for c in range(2):
                    nc.vector.tensor_tensor(oh[:], pf[:, c, hs, :].unsqueeze(3).to_broadcast(shape),
                                            iot[:].unsqueeze(1).unsqueeze(1).to_broadcast(shape), ALU.is_equal)
                    dve.drain()
                    nc.vector.tensor_tensor(oh[:], oh[:], itop[:, hs, c * TOPK:(c + 1) * TOPK].unsqueeze(2)
                                            .to_broadcast(shape), ALU.mult)
                    dve.drain()
                    nc.vector.tensor_reduce(e01[:, c, hs, :], oh[:], AX.X, ALU.add)
                    dve.drain()

            def experts(b):
                nc.vector.scalar_tensor_tensor(out=idx[:, b, :], in0=e01[:, 0].rearrange("p h k -> p (h k)"),
                                               scalar=float(NKEYS), in1=e01[:, 1].rearrange("p h k -> p (h k)"),
                                               op0=ALU.mult, op1=ALU.add).then_inc(s["idx_ready"], 1)

            def softmax_start():
                nc.vector.tensor_copy(gs[:], best[:, :, 0])
                dve.drain()
                nc.vector.tensor_tensor(best[:], best[:], gs[:].unsqueeze(2).to_broadcast([P, PH, TOPK]),
                                        ALU.subtract).then_inc(s["gm_done"], 1)

            def softmax_end(t, b):
                dve.wait_ge(s["ge_done"], t + 1)
                nc.vector.tensor_reduce(gs[:], best[:], AX.X, ALU.add)
                dve.drain()
                nc.vector.reciprocal(gs[:], gs[:])
                dve.drain()
                nc.vector.tensor_tensor(gw[:, b, :].rearrange("p (h k) -> p h k", h=PH), best[:],
                                        gs[:].unsqueeze(2).to_broadcast([P, PH, TOPK]), ALU.mult)
                dve.drain()

            def norm_x(t, b):
                hold(dve, s["r_done"], t + 1, s["passed_dve"])
                nc.vector.scalar_tensor_tensor(out=xb[:, b, :], in0=xa[:, b, :], scalar=rx[:, 0:1], in1=g2b[:],
                                               op0=ALU.mult, op1=ALU.mult).then_inc(s["xn_done"], 1)

            def dot_steps(b, group, first):
                for j in range(RING):
                    dve.wait_ge(landed[j], 16 * (group + 1))
                    nc.vector.tensor_tensor_reduce(out=ring[:, j, :], in0=ring[:, j, :], in1=xb[:, b, :], scale=1.0,
                                                   scalar=0.0, op0=ALU.mult, op1=ALU.add,
                                                   accum_out=dots16[:, j:j + 1]).then_inc(s["used_u"], 1)
                dve.drain()
                nc.vector.tensor_copy(hd[:, ds(first, TOPK)], dots16[:])
                dve.drain()

            def sum_steps(t, h, b, group, first):
                n = RING - BY_PE
                for j in range(BY_PE, RING):
                    dve.wait_ge(landed[j], 16 * (group + 1))
                    dve.wait_ge(s["used_dve"], (t * 8 + h + 1) * n + j - BY_PE)
                    nc.vector.scalar_tensor_tensor(out=xa[:, b, :], in0=ring[:, j, :], scalar=hw[:, ds(first + j, 1)],
                                                   in1=xa[:, b, :], op0=ALU.mult, op1=ALU.add).then_inc(s["used_dve"], 1)

            def weights(t, b, n):
                nc.vector.drain().then_inc(s["dots_done"], 1)
                dve.wait_ge(s["gelu_done"], t + 1)
                nc.vector.tensor_tensor(hw[:, 0:n], hw[:, 0:n], gw[:, b, 0:n], ALU.mult)
                nc.vector.drain().then_inc(s["hw_done"], 1)

            def add_part(t, b):
                groups = 2 if isinstance(t, int) and t == NT else PH
                hold(dve, s["used_pe"], (t * 8 + groups + 1) * BY_PE, s["passed_dve"])
                dve.drain()
                nc.vector.tensor_tensor(xa[:, b, :], acc[:, :], xa[:, b, :], ALU.add).then_inc(s["part_done"], 1)
                nc.vector.drain().then_inc(s["acc_done"], 1)

            def tile(pair, b):
                t = pair * 2 + b
                nb = 1 - b
                with dve.Fori(0, 2) as h:
                    dot_steps(b, t * 16 + h, h * TOPK)
                norm_x(t + 1, nb)
                with dve.Fori(2, 8) as h:
                    dot_steps(b, t * 16 + h, h * TOPK)
                weights(t, b, SLOTS)
                hold(dve, s["s_copied"], t + 2, s["passed_dve"])
                with dve.Fori(0, 6) as h:
                    sum_steps(t, h, b, t * 16 + 8 + h, h * TOPK)
                    topk(h)
                for h in (6, 7):
                    topk(h)
                dve.drain()
                dve.sem_inc(s["s_used"], 1)
                softmax_start()
                sum_steps(t, 6, b, t * 16 + 14, 6 * TOPK)
                places()
                keys_of(0)
                keys_of(1)
                experts(nb)
                sum_steps(t, 7, b, t * 16 + 15, 7 * TOPK)
                add_part(t, b)
                softmax_end(t + 1, nb)

            dve.wait_ge(s["consts"], 48)
            dve.sem_inc(s["s_used"], 1)
            dve.sem_inc(s["used_dve"], RING - BY_PE)
            dve.sem_inc(s["part_done"], 1)
            dve.wait_ge(s["setup"], 2)
            norm_x(0, 0)
            dve.wait_ge(s["s_copied"], 1)
            with dve.Fori(0, PH) as h:
                topk(h)
            dve.drain()
            dve.sem_inc(s["s_used"], 1)
            softmax_start()
            places()
            keys_of(0)
            keys_of(1)
            experts(0)
            softmax_end(0, 0)
            with dve.Fori(0, NT // 2) as pair:
                for b in range(2):
                    tile(pair, b)
            for q in range(4):
                quad = slice(q * DEC, (q + 1) * DEC)
                nc.vector.tensor_copy(idx[quad, 1, 0:DEC], idx[quad, 0, quad])
                nc.vector.tensor_copy(gw[quad, 1, 0:DEC], gw[quad, 0, quad])
            nc.vector.drain().then_inc(s["idx_ready"], 1)
            for k in range(2):
                dot_steps(0, NT * 16 + k, k * TOPK)
            dve.wait_ge(s["fin_p"], NT)
            nc.vector.memset(xa[:, 1, :], 0.0)
            weights(NT, 1, DEC)
            for k in range(2):
                sum_steps(NT, k, 1, NT * 16 + 2 + k, k * TOPK)
            add_part(NT, 1)
            dve.wait_ge(s["fin_d"], 1)
            nc.vector.tensor_tensor(xb[:DEC, 1, :], lo[:DEC, 0:D], xa[:DEC, 0, :], ALU.add)
            nc.vector.drain().then_inc(s["acc_done"], 1)


def build(nc, A):
    with ExitStack() as ctx:
        def sb(name, shape, dt=F32):
            return ctx.enter_context(nc.sbuf_tensor(name, shape, dt))

        keep = {"ident": sb("ident", [P, P]), "mhalf": sb("mhalf", [P, 8])}
        with ExitStack() as trunk:
            def tsb(name, shape):
                return trunk.enter_context(nc.sbuf_tensor(name, shape, F32))

            keep["xnT"] = tsb("xnT", [P, DC, ROWS])
            with ExitStack() as tables:
                for name in ("qa", "qb", "ka", "kb"):
                    keep[name] = tables.enter_context(nc.sbuf_tensor(name, [P, NT + 1, HD], F32))
                keep["subg"] = tables.enter_context(nc.sbuf_tensor("subg", [P, VD], F32))
                keep["neglam"] = tables.enter_context(nc.sbuf_tensor("neglam", [P, 1], F32))
                build_norm1(nc, A, keep)
                build_attention(nc, A, keep)
            keep["cvT"] = tsb("cvT", [P, DC, ROWS])
            keep["oT"] = tsb("oT", [P, DC, ROWS])
            keep["mixT"] = tsb("mixT", [P, DC, ROWS])
            build_merge(nc, A, keep)
            build_out(nc, A, keep)
        build_peer(nc, A, keep)


INPUTS = ["x_prompt", "x_sample", "cache_k", "cache_v", "state_conv", "norm1_g", "w_in", "b_gate", "conv_w",
          "q_norm_g", "k_norm_g", "lam_q1", "lam_k1", "lam_q2", "lam_k2", "subln_g", "w_conv_out", "w_attn_out",
          "w_o", "norm2_g", "peer_wq", "peer_q_g", "peer_subkeys", "peer_u", "peer_v"]
OUTPUTS = {"y_prompt": ((1, SEQ, D), (1, SEQ, D)),
           "y_sample": ((1, DEC, D), (1, DEC, D)),
           "k_prompt": ((SEQ, D), (1, 1, SEQ, HEADS, 2, HD)),
           "v_prompt": ((SEQ, D), (1, 1, SEQ, HEADS, VD)),
           "conv_prompt": ((2, D), (1, 1, 2, D)),
           "k_sample": ((DEC, D), (1, 1, DEC, HEADS, 2, HD)),
           "v_sample": ((DEC, D), (1, 1, DEC, HEADS, VD)),
           "conv_sample": ((2, D), (1, 1, 2, D))}


def rope_tables():
    half = HD // 2
    inv = np.float32(10000.0) ** (-np.arange(half, dtype=np.float32) / np.float32(half))
    ang = np.arange((NT + 1) * P, dtype=np.float32)[:, None] * inv[None, :].astype(np.float32)
    cos, sin = np.cos(ang), np.sin(ang)
    out = []
    for table in (np.concatenate([cos, cos], 1), np.concatenate([-sin, sin], 1)):
        out.append(np.ascontiguousarray(table.reshape(NT + 1, P, HD).transpose(1, 0, 2)).astype(np.float32))
    return out


def program(nc, in_arrays):
    A = {}
    for name, a in in_arrays.items():
        A[name] = nc.dram_tensor(f"in_{name}", a.shape, mybir.dt.from_np(a.dtype), kind="ExternalInput").ap()
    for name, (shape, _) in OUTPUTS.items():
        A[name] = nc.dram_tensor(f"out_{name}", shape, F32, kind="ExternalOutput").ap()
    for name in ("cv_t", "o_t"):
        A[name] = nc.dram_tensor(name, (D, ROWS), F32, kind="Internal").ap()
    A["x1"] = nc.dram_tensor("x1_rows", (SEQ + P, D), F32, kind="Internal").ap()
    build(nc, A)


def kernel(**inputs):
    import concourse.bacc as bacc
    from concourse.bass_utils import run_bass_kernel_spmd as run
    arrays = {name: np.ascontiguousarray(inputs[name]) for name in INPUTS}
    for name in ("cache_k", "cache_v"):
        arrays[name] = arrays[name].reshape(PAST, D)
    arrays["rope_cos"], arrays["rope_sin"] = rope_tables()
    nc = bacc.Bacc("TRN2", target_bir_lowering=False, num_devices=1)
    program(nc, arrays)
    r = run(nc, [{f"in_{k}": v for k, v in arrays.items()}], core_ids=[0])
    got = r.results[0]
    return tuple(np.asarray(got[f"out_{name}"]).reshape(shape) for name, (_, shape) in OUTPUTS.items())
```

```python
from contextlib import ExitStack

import numpy as np
import concourse.bass as bass
from concourse import mybir

F32 = mybir.dt.float32
U32 = mybir.dt.uint32
ALU = mybir.AluOpType
ACT = mybir.ActivationFunctionType
AX = mybir.AxisListType
ds = bass.ds

P = 128
D = 1024
DC = D // P
SEQ, DEC = 1024, 32
ROWS = SEQ + DEC
NT = SEQ // P
PAST = 1024
HEADS = 8
HD = 64
VD = 128
GROUPS = 4
GW = 2 * VD
CHUNK = 64
EPS = 1e-6
LAM0 = 0.8 - 0.6
QKS = HD ** -0.5
LOW = -3.0e38
PART = ROWS // 3
QCOL, KCOL, VCOL = 3 * D, 4 * D, 5 * D
GACOL, GBCOL = 6 * D, 7 * D
TOPK = 16
NKEYS = 128
PH = 8
PQ = 2048
SLOTS = PH * TOPK
RING = 16
BY_PE = 12
QUAD = 4
DIAGS = 6


def rows_of(t):
    return DEC if isinstance(t, int) and t == NT else P


def hold(eng, sem, value, passed):
    eng.wait_ge(sem, value)
    if not isinstance(value, int):
        eng.sem_inc(passed, 1)


def semaphores(ctx, nc, block, names):
    return {n: ctx.enter_context(nc.semaphore(f"{block}_{n}")) for n in names.split()}


def parts(tensor, first, n, width):
    return tensor[:, first:first + n * width].rearrange("p (n w) -> p n w", n=n)


def group_cols(a, col):
    return a[:, ds(col, GW)].rearrange("(c p) n -> p c n", p=P)


def build_norm1(nc, A, keep):
    with ExitStack() as ctx:
        def sb(name, shape, dt=F32):
            return ctx.enter_context(nc.sbuf_tensor("n1_" + name, shape, dt))

        s = semaphores(ctx, nc, "n1", "gain consts x_in0 x_in1 x_in2 x_in3 sq_done r_done xn_done tr_done cpa cpd "
                       "ident_done lam_d lam_e ahead passed_sp passed_pool passed_pe passed_act "
                       "passed_dve")
        x_in = [s["x_in0"], s["x_in1"], s["x_in2"], s["x_in3"]]
        xt = sb("xt", [P, QUAD, D])
        xn = sb("xn", [P, 2, D])
        junk = sb("junk", [P, D])
        g1b = sb("g1b", [P, D])
        ss = sb("ss", [P, QUAD])
        rr = sb("rr", [P, QUAD])
        cosd = sb("cosd", [P, NT + 1, HD])
        sind = sb("sind", [P, NT + 1, HD])
        gains = sb("gains", [P, 4, HD])
        lamv = sb("lamv", [P, 4, HD])
        lamp = sb("lamp", [P, 2, HD])
        lamd = sb("lamd", [P, 2])
        lame = sb("lame", [P, 2])
        ps = [ctx.enter_context(nc.psum_tensor(f"n1_ps{b}", [P, 2, 512], F32)) for b in range(2)]
        block = ctx.enter_context(nc.Block())
        N_CONST = 2 + 6 + 4 + 1

        @block.sync
        def _(sp):
            for b in range(QUAD):
                sp.dma_start(xt[:, b, :], A["x_prompt"][0, b * P:(b + 1) * P, :]).then_inc(x_in[b], 16)
                if b == 0:
                    sp.dma_start(g1b[:], A["norm1_g"].to_broadcast([P, D])).then_inc(s["gain"], 16)
            sp.dma_start(cosd[:], A["rope_cos"]).then_inc(s["consts"], 16)
            sp.dma_start(sind[:], A["rope_sin"]).then_inc(s["consts"], 16)
            h = HD // 2
            for k, name in enumerate(("q_norm_g", "k_norm_g")):
                g = A[name]
                sp.dma_start(gains[:, 2 * k, :], g.to_broadcast([P, HD])).then_inc(s["consts"], 16)
                sp.dma_start(gains[:, 2 * k + 1, 0:h], g[:, h:HD].to_broadcast([P, h])).then_inc(s["consts"], 16)
                sp.dma_start(gains[:, 2 * k + 1, h:HD], g[:, 0:h].to_broadcast([P, h])).then_inc(s["consts"], 16)
            for k, name in enumerate(("lam_q1", "lam_k1", "lam_q2", "lam_k2")):
                sp.dma_start(lamv[:, k, :], A[name].to_broadcast([P, HD])).then_inc(s["consts"], 16)
            sp.dma_start(keep["subg"][:], A["subln_g"].to_broadcast([P, VD])).then_inc(s["consts"], 16)

            def load(t, b, src):
                hold(sp, s["xn_done"], t + 1, s["passed_sp"])
                sp.dma_start(xt[:rows_of(t), b, :], src).then_inc(x_in[b], 16)

            with sp.Fori(1, NT // QUAD) as quad:
                for b in range(QUAD):
                    t = quad * QUAD + b
                    load(t, b, A["x_prompt"][0, ds(t * P, P), :])
            load(NT, 0, A["x_sample"][0])
            sp.dma_start(keep["kc"][:], group_cols(A["cache_k"], 0)).then_inc(s["ahead"], 16)
            for kind in range(3):
                sp.dma_start(keep["w"][kind][:], group_cols(A["w_in"][0], (QCOL, KCOL, VCOL)[kind])).then_inc(s["ahead"], 16)
            sp.wait_ge(s["ahead"], 64)

        @block.scalar
        def _(act):
            def square(b, turn):
                act.drain()
                act.wait_ge(x_in[b], 16 * turn)
                nc.scalar.activation(junk[:], xt[:, b, :], ACT.Square, scale=D ** -0.5,
                                     accum_out=ss[:, b:b + 1]).then_inc(s["sq_done"], 1)

            def keep_turned(t, b):
                n = rows_of(t)
                hold(act, s["tr_done"], t + 3, s["passed_act"])
                nc.scalar.copy(keep["xnT"][:, 0:4, ds(t * P, n)],
                               ps[b][:, 0, :].rearrange("p (c r) -> p c r", c=4)[:, :, 0:n]).then_inc(s["cpa"], 1)

            act.sem_inc(s["cpa"], 2)
            square(0, 1)
            with act.Fori(0, NT // QUAD) as quad:
                for b in range(QUAD):
                    square((b + 1) % QUAD, quad + 1 + (b + 1) // QUAD)
                    keep_turned(quad * QUAD + b, b % 2)
            keep_turned(NT, 0)
            act.wait_ge(s["lam_d"], 1)
            nc.scalar.activation(lame[:], lamd[:], ACT.Exp).then_inc(s["lam_e"], 1)

        @block.gpsimd
        def _(pool):
            ident = keep["ident"]
            nc.gpsimd.memset(ident[:], 0.0)
            nc.gpsimd.memset(keep["mhalf"][:], -0.5)
            pool.drain()
            nc.gpsimd.affine_select(out=ident[:], in_=ident[:], compare_op=ALU.not_equal, fill=1.0, base=0,
                                    pattern=[[-1, P]], channel_multiplier=1).then_inc(s["ident_done"], 1)

            def rsqrt(t, b):
                hold(pool, s["sq_done"], t + 1, s["passed_pool"])
                nc.gpsimd.tensor_scalar(rr[:, b:b + 1], ss[:, b:b + 1], EPS, None, ALU.add)
                pool.drain()
                nc.gpsimd.tensor_tensor(rr[:, b:b + 1], rr[:, b:b + 1], keep["mhalf"][:, 0:1],
                                        ALU.pow).then_inc(s["r_done"], 1)

            with pool.Fori(0, NT // QUAD) as quad:
                for b in range(QUAD):
                    rsqrt(quad * QUAD + b, b)
            rsqrt(NT, 0)

        @block.vector
        def _(dve):
            dve.sem_inc(s["xn_done"], QUAD)
            dve.sem_inc(s["cpd"], 2)
            dve.wait_ge(s["gain"], 16)

            def normalise(t, b):
                dve.wait_ge(s["tr_done"], t + 1)
                dve.wait_ge(s["r_done"], t + 1)
                nc.vector.scalar_tensor_tensor(out=xn[:, b % 2, :], in0=xt[:, b, :], scalar=rr[:, b:b + 1],
                                               in1=g1b[:], op0=ALU.mult, op1=ALU.mult).then_inc(s["xn_done"], 1)

            def keep_turned(t, b):
                n = rows_of(t)
                hold(dve, s["tr_done"], t + 3, s["passed_dve"])
                nc.vector.tensor_copy(keep["xnT"][:, 4:8, ds(t * P, n)],
                                      ps[b][:, 1, :].rearrange("p (c r) -> p c r", c=4)[:, :, 0:n]).then_inc(s["cpd"], 1)

            normalise(0, 0)
            with dve.Fori(0, NT // QUAD) as quad:
                for b in range(QUAD):
                    t = quad * QUAD + b
                    normalise(t + 1, (b + 1) % QUAD)
                    keep_turned(t, b % 2)
            keep_turned(NT, 0)

            dve.wait_ge(s["consts"], 16 * N_CONST)
            for k, (ta, tb) in enumerate(((keep["qa"], keep["qb"]), (keep["ka"], keep["kb"]))):
                ga = gains[:, 2 * k:2 * k + 1, :].to_broadcast([P, NT + 1, HD])
                gb = gains[:, 2 * k + 1:2 * k + 2, :].to_broadcast([P, NT + 1, HD])
                nc.vector.tensor_tensor(ta[:], cosd[:], ga, ALU.mult)
                nc.vector.tensor_tensor(tb[:], sind[:], gb, ALU.mult)
            nc.vector.tensor_scalar(keep["subg"][:], keep["subg"][:], 1.0 - LAM0, None, ALU.mult)
            lv = lamv[:].rearrange("p (a b) d -> p a b d", b=2)
            nc.vector.tensor_tensor(lamp[:], lv[:, :, 0, :], lv[:, :, 1, :], ALU.mult)
            dve.drain()
            nc.vector.tensor_reduce(lamd[:], lamp[:], AX.X, ALU.add).then_inc(s["lam_d"], 1)
            dve.wait_ge(s["lam_e"], 1)
            nc.vector.tensor_tensor(keep["neglam"][:], lame[:, 1:2], lame[:, 0:1], ALU.subtract)
            dve.drain()
            nc.vector.tensor_scalar(keep["neglam"][:], keep["neglam"][:], -LAM0, None, ALU.add)

        @block.tensor
        def _(pe):
            pe.sem_inc(s["tr_done"], 2)
            pe.wait_ge(s["ident_done"], 1)

            def tile(t, b):
                n = rows_of(t)
                hold(pe, s["cpa"], t + 1, s["passed_pe"])
                hold(pe, s["cpd"], t + 1, s["passed_pe"])
                hold(pe, s["xn_done"], t + QUAD + 1, s["passed_pe"])
                for c in range(DC):
                    o = ps[b][:, c // 4, (c % 4) * P:(c % 4) * P + n]
                    last = nc.tensor.transpose(o, xn[:n, b, c * P:(c + 1) * P], keep["ident"][:n, :n])
                last.then_inc(s["tr_done"], 1)

            with pe.Fori(0, NT // 2) as pair:
                for b in range(2):
                    tile(pair * 2 + b, b)
            tile(NT, 0)


def build_attention(nc, A, keep):
    NU = 2 * (NT + 1)
    with ExitStack() as ctx:
        def sb(name, shape, dt=F32):
            return ctx.enter_context(nc.sbuf_tensor("at_" + name, shape, dt))

        s = semaphores(ctx, nc, "at", "w_in0 w_in1 w_in2 kc_in vc_in pj_done evq evv sq_done ss_done rr_done "
                       "qf_done tr_done trc kct_done kct_cp k_out v_out kv_free wf_in0 wf_in1 ahead "
                       "consts f_done c_done u_done y_done out cv_out clear o_out sc_done mx_done "
                       "ex_done a_done at_a at_d tc_a tc_d pv_done so_done ro_done on_done ot_done "
                       "otc passed_pe passed_act passed_dve passed_pool passed_sp")
        w_in = [s["w_in0"], s["w_in1"], s["w_in2"]]
        wf_in = [s["wf_in0"], s["wf_in1"]]
        w = keep["w"]
        upper = DC * D // 2
        wf = [parts(keep["low"], upper + b * DC * P, DC, P) for b in range(2)]
        cw = sb("cw", [P, 3, DC])
        st = sb("st", [P, 2, DC])
        U = sb("U", [P, ROWS + 4])
        Y = sb("Y", [P, ROWS + 2])
        C = sb("C", [P, ROWS])
        cvr = sb("cvr", [P, 2, ROWS])
        oTg = sb("oTg", [P, 2, ROWS])
        tail = sb("tail", [P, 4, DC])
        kc = keep["kc"]
        vc = parts(keep["low"], upper + 2 * DC * P, DC, GW)
        kcT = parts(keep["low"], upper // 2, 2, PAST)
        qT = sb("qT", [P, 2, ROWS])
        kT = sb("kT", [P, 2, ROWS])
        kf = sb("kf", [P, NT + 1, GW])
        V = sb("V", [P, NT + 1, GW])
        sq = sb("sq", [P, 2, GW])
        qn = sb("qn", [P, GW])
        t1 = sb("t1", [P, GW])
        t2 = sb("t2", [P, GW])
        qf = sb("qf", [P, 4, GW])
        ss = sb("ss", [P, 2, 4])
        rr = sb("rr", [P, 2, 4])
        p = sb("p", [P, 2, 2, ROWS])
        aT = sb("aT", [P, 2, NT * P])
        mx = sb("mx", [P, 2, 2])
        nb = sb("nb", [P, 2, 2])
        Z = sb("Z", [P, 2, 2])
        rz = sb("rz", [P, 2])
        rl = sb("rl", [P, 1])
        so = sb("so", [P, 2])
        ro = sb("ro", [P, 2])
        on = sb("on", [P, 2, VD])
        oj = sb("oj", [P, VD])
        S = ctx.enter_context(nc.psum_tensor("at_S", [P, 4, 512], F32))
        B = [ctx.enter_context(nc.psum_tensor(f"at_B{k}", [P, 512], F32)) for k in range(4)]
        T = B[0:2]
        O = [B[2][:, 0:GW], B[2][:, GW:2 * GW]]
        F = B[3]
        ident, xnT = keep["ident"], keep["xnT"]
        block = ctx.enter_context(nc.Block())

        def cache(name, g):
            return group_cols(A[name], g * GW)

        def keys(t):
            return (t + 1) * P if t < NT else PAST + DEC

        def scores(c, t, n):
            first = 0 if t == NT else 2 * c
            banks = 3 if t == NT else 2
            return S[:n, first:first + banks, :].rearrange("p a b -> p (a b)")

        def part_pieces(z, row, part, shift):
            if part < 2:
                return [(z[:, 0:PART], row[:, part * PART:(part + 1) * PART])]
            cut = SEQ - 2 * PART
            return [(z[:, 0:cut], row[:, 2 * PART:SEQ]), (z[:, cut:PART], row[:, SEQ + shift:SEQ + shift + DEC])]

        @block.sync
        def _(sp):
            def load_wf(n, b, col):
                sp.dma_start(wf[b], A["w_in"][0, :, ds(col, P)]
                             .rearrange("(c p) n -> p c n", p=P)).then_inc(wf_in[b], 16)

            def conv_col(g, m):
                return (D, 2 * D, 0)[m % 3] + (g * 2 + m // 3) * P

            def load_w(kind, g):
                sp.dma_start(w[kind][:], group_cols(A["w_in"][0], (QCOL, KCOL, VCOL)[kind] + g * GW)).then_inc(w_in[kind], 16)

            def stores(g, then_load):
                if then_load:
                    sp.wait_ge(s["kct_done"], 4 * (g + 1))
                    sp.dma_start(kc[:], cache("cache_k", g + 1)).then_inc(s["kc_in"], 16)
                    for kind in range(2):
                        sp.wait_ge(s["pj_done"], 27 * g + 9 * (kind + 1))
                        load_w(kind, g + 1)
                sp.wait_ge(s["qf_done"], NU * (g + 1))
                sp.dma_start(A["k_prompt"][:, ds(g * GW, GW)].rearrange("(t p) n -> p t n", p=P),
                             kf[:, 0:NT, :]).then_inc(s["k_out"], 16)
                sp.dma_start(A["k_sample"][:, ds(g * GW, GW)], kf[:DEC, NT, :]).then_inc(s["k_out"], 16)
                if then_load:
                    sp.wait_ge(s["pj_done"], 27 * (g + 1))
                    load_w(2, g + 1)
                sp.wait_ge(s["evv"], 9 * (g + 2))
                sp.dma_start(A["v_prompt"][:, ds(g * GW, GW)].rearrange("(t p) n -> p t n", p=P),
                             V[:, 0:NT, :]).then_inc(s["v_out"], 16)
                sp.dma_start(A["v_sample"][:, ds(g * GW, GW)], V[:DEC, NT, :]).then_inc(s["v_out"], 16)
                sp.wait_ge(s["k_out"], 32 * (g + 1))
                hold(sp, s["v_out"], 32 * (g + 1), s["passed_sp"])
                sp.sem_inc(s["kv_free"], 1)
                for m in range(6):
                    hold(sp, s["f_done"], NU * g + 3 * (m + 1), s["passed_sp"])
                    if m < 4:
                        load_wf(m, m % 2, conv_col(g, m + 2))
                    elif then_load:
                        load_wf(m, m % 2, conv_col(g + 1, m - 4))
                    if m % 3 == 2:
                        hold(sp, s["y_done"], 3 * (g * 2 + m // 3) + 6, s["passed_sp"])
                        sp.dma_start(A["cv_t"][ds((g * 2 + m // 3) * P, P), :], cvr[:, m // 3, :]).then_inc(s["cv_out"], 16)
                if then_load:
                    sp.wait_ge(s["pv_done"], NU * (g + 1))
                    sp.dma_start(vc[:], cache("cache_v", g + 1)).then_inc(s["vc_in"], 16)
                if not then_load:
                    with nc.allow_non_contiguous_dma(reason="two rows of state, channels in partitions"):
                        for j in range(2):
                            for k, name in enumerate(("conv_prompt", "conv_sample")):
                                sp.dma_start(A[name][j].rearrange("(c p) -> p c", p=P),
                                             tail[:, 2 * k + j, :]).then_inc(s["out"], 16)
                hold(sp, s["otc"], NU * (g + 1) + 2, s["passed_sp"])
                sp.dma_start(A["o_t"][ds(g * GW, GW), :].rearrange("(h p) r -> p h r", p=P), oTg[:]).then_inc(s["o_out"], 16)
                hold(sp, s["cv_out"], 32 * (g + 1), s["passed_sp"])
                hold(sp, s["o_out"], 16 * (g + 1), s["passed_sp"])
                sp.sem_inc(s["clear"], 1)

            sp.sem_inc(s["kv_free"], 1)
            sp.sem_inc(s["clear"], 1)
            sp.sem_inc(s["kc_in"], 16)
            for kind in range(3):
                sp.sem_inc(w_in[kind], 16)
            for m in range(2):
                load_wf(m, m, conv_col(0, m))
            sp.dma_start(vc[:], cache("cache_v", 0)).then_inc(s["vc_in"], 16)
            for k, src in enumerate(merge_weights(A, 0)[0:2]):
                sp.dma_start(merge_places(keep, 0)[:, k], src).then_inc(s["ahead"], 16)
            with sp.Fori(0, GROUPS - 1) as g:
                stores(g, True)
            stores(GROUPS - 1, False)
            sp.wait_ge(s["out"], 64)
            sp.wait_ge(s["ahead"], 32)

        @block.tensor
        def _(pe):
            def cached_keys(g):
                pe.wait_ge(s["kc_in"], 16 * (g + 1))
                for m in range(4):
                    pe.wait_ge(s["kct_cp"], 4 * g + m + 1)
                    for k in range(4):
                        last = nc.tensor.transpose(S[:, 2 + m % 2, k * P:(k + 1) * P],
                                                   kc[:, 4 * (m % 2) + k, (m // 2) * P:(m // 2 + 1) * P], ident[:])
                    last.then_inc(s["kct_done"], 1)

            def project(g, u):
                kind, t = divmod(u, NT + 1)
                n = rows_of(t)
                if t == 0:
                    pe.wait_ge(w_in[kind], 16 * (g + 1))
                if u >= 4:
                    if u - 4 < NU:
                        hold(pe, s["evq"], NU * g + u - 3, s["passed_pe"])
                    else:
                        hold(pe, s["evv"], 9 * (g + 1) + u - 4 - NU + 1, s["passed_pe"])
                for c in range(DC):
                    last = nc.tensor.matmul(B[u % 4][:n, 0:GW], xnT[:, c, t * P:t * P + n], w[kind][:, c, :],
                                            start=(c == 0), stop=(c == DC - 1))
                last.then_inc(s["pj_done"], 1)

            def turn(g, u):
                kind, t = divmod(u, NT + 1)
                n = rows_of(t)
                hold(pe, s["trc"], NU * g + u + 1, s["passed_pe"])
                hold(pe, s["qf_done"], NU * g + u + 1, s["passed_pe"])
                for h in range(2):
                    src = qf[:n, u % 4, h * P:(h + 1) * P] if kind == 0 else kf[:n, t, h * P:(h + 1) * P]
                    last = nc.tensor.transpose(S[:, u % 2, h * P:h * P + n], src, ident[:n, :n])
                last.then_inc(s["tr_done"], 1)

            def score(g, i, components=(0, 1)):
                h, t = divmod(i, NT + 1)
                n, nk = rows_of(t), keys(t)
                for c in components:
                    need = 2 * i + c if t == NT else (2 * i if t == 0 else 2 * i - 1 + c)
                    if i:
                        hold(pe, s["ex_done"], 4 * (NT + 1) * g + need, s["passed_pe"])
                    o = scores(c, t, n)
                    rows = slice(c * HD, (c + 1) * HD)
                    q = qT[rows, h, t * P:t * P + n]
                    if t < NT:
                        parts = [(k, kT[rows, h, k:min(k + 512, nk)]) for k in range(0, nk, 512)]
                    else:
                        parts = [(k, kcT[rows, h, k:k + 512]) for k in range(0, PAST, 512)]
                        parts.append((PAST, kT[rows, h, SEQ:ROWS]))
                    for k, keys_ap in parts:
                        last = nc.tensor.matmul(o[:, k:k + keys_ap.shape[1]], q, keys_ap, start=True, stop=True)
                    last.then_inc(s["sc_done"], 1)

            def turn_weights(g, i):
                h, t = divmod(i, NT + 1)
                n, nk = rows_of(t), keys(t)
                blocks = (nk + P - 1) // P
                hold(pe, s["tc_a"], NU * g + i + 1, s["passed_pe"])
                if t in range(4, NT):
                    hold(pe, s["tc_d"], 8 * g + 4 * h + t - 4 + 1, s["passed_pe"])
                hold(pe, s["a_done"], NU * g + i + 1, s["passed_pe"])
                for k in range(blocks):
                    m = min(P, nk - k * P)
                    o = T[0][:m, k * DEC:(k + 1) * DEC] if t == NT else T[k // 4][:, (k % 4) * P:(k % 4 + 1) * P]
                    last = nc.tensor.transpose(o, p[:n, i % 2, 0, k * P:k * P + m], ident[:n, :n])
                    if k == min(3, blocks - 1) and t < NT or t == NT and k == blocks - 1:
                        last.then_inc(s["at_a"], 1)
                    elif k == blocks - 1:
                        last.then_inc(s["at_d"], 1)

            def turn_out(g, i):
                n = rows_of(i % (NT + 1))
                hold(pe, s["on_done"], NU * g + i + 1, s["passed_pe"])
                nc.tensor.transpose(O[i % 2][:, P:P + n], on[:n, i % 2, :], ident[:n, :n]).then_inc(s["ot_done"], 1)

            def weigh(g, i):
                h, t = divmod(i, NT + 1)
                n, nk = rows_of(t), keys(t)
                blocks = (nk + P - 1) // P
                if i == NT:
                    hold(pe, s["vc_in"], 16 * (g + 1), s["passed_pe"])
                hold(pe, s["otc"], NU * g + i + 2, s["passed_pe"])
                hold(pe, s["tc_a"], NU * g + i + 2, s["passed_pe"])
                for k in range(blocks):
                    if t in range(4, NT) and k == 4:
                        hold(pe, s["tc_d"], 8 * g + 4 * h + t - 4 + 2, s["passed_pe"])
                    m = min(P, nk - k * P)
                    a = aT[:m, i % 2, k * n:(k + 1) * n]
                    v = (V[:m, k, h * P:(h + 1) * P] if t < NT or k == PAST // P
                         else vc[:, k, h * P:(h + 1) * P])
                    last = nc.tensor.matmul(O[i % 2][:n, 0:VD], a, v, start=(k == 0), stop=(k == blocks - 1))
                last.then_inc(s["pv_done"], 1)

            def conv_unit(g, i, halfway=None):
                cc, (kind, part) = i // 9, divmod(i % 9, 3)
                m = i // 3
                if part == 0:
                    hold(pe, wf_in[m % 2], 16 * (3 * g + m // 2 + 1), s["passed_pe"])
                left = 3 * (2 * g + cc)
                if i % 9 == 0:
                    hold(pe, s["y_done"], left + 3, s["passed_pe"])
                else:
                    before, p0 = divmod(i % 9 - 1, 3)
                    hold(pe, s[("c_done", "u_done", "y_done")[before]], left + p0 + 1 + (3 if before == 2 else 0),
                         s["passed_pe"])
                for c in range(DC):
                    if halfway and c == DC // 2:
                        halfway()
                    last = nc.tensor.matmul(F[:, 0:PART], wf[m % 2][:, c, :], xnT[:, c, part * PART:(part + 1) * PART],
                                            start=(c == 0), stop=(c == DC - 1))
                last.then_inc(s["f_done"], 1)

            with pe.Fori(0, GROUPS) as g:
                hold(pe, s["y_done"], 6 * g + 3, s["passed_pe"])
                hold(pe, s["otc"], NU * g + 2, s["passed_pe"])
                hold(pe, s["evv"], 9 * (g + 1), s["passed_pe"])
                cached_keys(g)
                for u in range(3 * (NT + 1)):
                    project(g, u)
                    if 0 <= u - 2 < NU:
                        turn(g, u - 2)
                hold(pe, s["evv"], 9 * (g + 2), s["passed_pe"])
                hold(pe, s["trc"], NU * (g + 1) + 2, s["passed_pe"])
                hold(pe, s["kct_cp"], 4 * (g + 1) + 2, s["passed_pe"])
                score(g, 0)
                for i in range(NU):
                    t = i % (NT + 1)
                    if t == NT - 1:
                        score(g, i + 1, (0,))
                        turn_weights(g, i)
                        conv_unit(g, i, lambda: turn_out(g, i - 1))
                        score(g, i + 1, (1,))
                    elif t == NT or i == 0:
                        if i == 0:
                            score(g, 1)
                        conv_unit(g, i)
                        if 0 < i < NU - 1:
                            score(g, i + 1)
                        turn_weights(g, i)
                        if i:
                            turn_out(g, i - 1)
                    else:
                        score(g, i + 1)
                        turn_weights(g, i)
                        conv_unit(g, i, lambda: turn_out(g, i - 1))
                    weigh(g, i)
                turn_out(g, NU - 1)

        @block.scalar
        def _(act):
            def square(g, u):
                n = rows_of(u % (NT + 1))
                if u >= 2:
                    act.wait_ge(s["ss_done"], NU * g + u - 1)
                act.wait_ge(s["pj_done"], 27 * g + u + 1)
                nc.scalar.activation(sq[:n, u % 2, :], B[u % 4][:n, 0:GW], ACT.Square,
                                     scale=HD ** -0.5).then_inc(s["sq_done"], 1)

            def keep_turned(g, u):
                kind, t = divmod(u, NT + 1)
                n = rows_of(t)
                act.wait_ge(s["tr_done"], NU * g + u + 5)
                dst = (qT, kT)[kind]
                nc.scalar.copy(dst[:, :, t * P:t * P + n],
                               S[:, u % 2, 0:GW].rearrange("p (h r) -> p h r", h=2)[:, :, 0:n]).then_inc(s["trc"], 1)

            def keep_value(g, u):
                t = u - NU
                n = rows_of(t)
                if t == 0:
                    act.wait_ge(s["kv_free"], g + 1)
                act.wait_ge(s["pj_done"], 27 * g + u + 1)
                nc.scalar.copy(V[:n, t, :], B[u % 4][:n, 0:GW]).then_inc(s["evv"], 1)

            def exps(g, i, components=(0, 1)):
                t = i % (NT + 1)
                n, nk = rows_of(t), keys(t)
                for c in components:
                    act.wait_ge(s["mx_done"], 2 * NU * g + 2 * i + c + 1)
                    nc.scalar.activation(p[:n, i % 2, c, 0:nk], scores(c, t, n)[:, 0:nk], ACT.Exp, scale=QKS,
                                         bias=nb[:n, i % 2, c:c + 1],
                                         accum_out=Z[:n, i % 2, c:c + 1]).then_inc(s["ex_done"], 1)

            def keep_weights(g, i):
                t = i % (NT + 1)
                cols = (NT + 1) * DEC if t == NT else min(t + 1, 4) * P
                act.wait_ge(s["at_a"], NU * g + i + 1)
                if t == NT:
                    last = PAST // P * DEC
                    nc.scalar.copy(aT[:, i % 2, 0:last], T[0][:, 0:last])
                    nc.scalar.copy(aT[:DEC, i % 2, last:cols], T[0][:DEC, last:cols]).then_inc(s["tc_a"], 1)
                else:
                    nc.scalar.copy(aT[:, i % 2, 0:cols], T[0][:, 0:cols]).then_inc(s["tc_a"], 1)

            def keep_out(g, i):
                h, t = divmod(i, NT + 1)
                n = rows_of(t)
                hold(act, s["ot_done"], NU * g + i + 3, s["passed_act"])
                if i == 0:
                    hold(act, s["clear"], g + 1, s["passed_act"])
                nc.scalar.copy(oTg[:, h, t * P:t * P + n], O[i % 2][:, P:P + n]).then_inc(s["otc"], 1)

            def keep_c(g, i):
                part = i % 9
                if part < 3:
                    act.wait_ge(s["f_done"], NU * g + i + 1)
                    nc.scalar.copy(C[:, part * PART:(part + 1) * PART], F[:, 0:PART]).then_inc(s["c_done"], 1)

            def square_out(g, i):
                n = rows_of(i % (NT + 1))
                act.wait_ge(s["pv_done"], NU * g + i + 1)
                nc.scalar.activation(oj[:n, :], O[i % 2][:n, 0:VD], ACT.Square, scale=VD ** -0.5,
                                     accum_out=so[:n, i % 2:i % 2 + 1]).then_inc(s["so_done"], 1)

            for sem, credit in ((s["evv"], 9), (s["trc"], 2), (s["kct_cp"], 2), (s["tc_a"], 1), (s["otc"], 2)):
                act.sem_inc(sem, credit)
            with act.Fori(0, GROUPS) as g:
                for m in range(4):
                    act.wait_ge(s["kct_done"], 4 * g + m + 1)
                    nc.scalar.copy(kcT[:, m // 2, 512 * (m % 2):512 * (m % 2 + 1)],
                                   S[:, 2 + m % 2, :]).then_inc(s["kct_cp"], 1)
                for u in range(3 * (NT + 1)):
                    if u < NU:
                        square(g, u)
                    else:
                        keep_value(g, u)
                    if 0 <= u - 2 < NU:
                        keep_turned(g, u - 2)
                exps(g, 0)
                for i in range(NU):
                    before_sample = i % (NT + 1) == NT - 1
                    if i + 1 < NU:
                        exps(g, i + 1, (0,) if before_sample else (0, 1))
                    keep_weights(g, i)
                    if i:
                        keep_out(g, i - 1)
                    keep_c(g, i)
                    if before_sample:
                        exps(g, i + 1, (1,))
                    square_out(g, i)
                keep_out(g, NU - 1)

        @block.gpsimd
        def _(pool):
            def rsqrt(dst, src, done):
                nc.gpsimd.tensor_scalar(dst, src, EPS, None, ALU.add)
                pool.drain()
                nc.gpsimd.tensor_tensor(dst, dst, keep["mhalf"][:dst.shape[0], 0:dst.shape[1]],
                                        ALU.pow).then_inc(done, 1)

            with nc.allow_non_contiguous_dma(reason="small vectors, channels in partitions"):
                for j in range(3):
                    pool.dma_start(cw[:, j, :], A["conv_w"][0, j].rearrange("(c p) -> p c", p=P)).then_inc(s["consts"], 16)
                for j in range(2):
                    pool.dma_start(st[:, j, :], A["state_conv"][0, 0, j].rearrange("(c p) -> p c", p=P)).then_inc(s["consts"], 16)

            with pool.Fori(0, GROUPS) as g:
                for u in range(NU):
                    n = rows_of(u % (NT + 1))
                    hold(pool, s["ss_done"], NU * g + u + 1, s["passed_pool"])
                    rsqrt(rr[:n, u % 2, :], ss[:n, u % 2, :], s["rr_done"])
                for i in range(NU):
                    n = rows_of(i % (NT + 1))
                    hold(pool, s["so_done"], NU * g + i + 1, s["passed_pool"])
                    rsqrt(ro[:n, i % 2:i % 2 + 1], so[:n, i % 2:i % 2 + 1], s["ro_done"])

        @block.vector
        def _(dve):
            def segs(ap):
                return ap.rearrange("p (a d) -> p a d", d=HD)

            def mean_square(g, u):
                n = rows_of(u % (NT + 1))
                dve.wait_ge(s["sq_done"], NU * g + u + 1)
                nc.vector.tensor_reduce(ss[:n, u % 2, :], segs(sq[:n, u % 2, :]), AX.X, ALU.add).then_inc(s["ss_done"], 1)

            def rotate(g, u):
                kind, t = divmod(u, NT + 1)
                n = rows_of(t)
                h = HD // 2
                ta, tb = ((keep["qa"], keep["qb"]), (keep["ka"], keep["kb"]))[kind]
                dve.wait_ge(s["rr_done"], NU * g + u + 1)
                nc.vector.tensor_tensor(segs(qn[:n, :]), segs(B[u % 4][:n, 0:GW]),
                                        rr[:n, u % 2, :].unsqueeze(2).to_broadcast([n, 4, HD]),
                                        ALU.mult).then_inc(s["evq"], 1)
                dve.drain()
                q3 = segs(qn[:n, :])
                nc.vector.tensor_tensor(segs(t1[:n, :]), q3, ta[:n, t:t + 1, :].to_broadcast([n, 4, HD]), ALU.mult)
                nc.vector.tensor_tensor(segs(t2[:n, :])[:, :, 0:h], q3[:, :, h:HD],
                                        tb[:n, t:t + 1, 0:h].to_broadcast([n, 4, h]), ALU.mult)
                nc.vector.tensor_tensor(segs(t2[:n, :])[:, :, h:HD], q3[:, :, 0:h],
                                        tb[:n, t:t + 1, h:HD].to_broadcast([n, 4, h]), ALU.mult)
                dve.drain()
                if kind == 0:
                    dve.wait_ge(s["tr_done"], NU * g + u + 1)
                    dst = qf[:n, u % 4, :]
                else:
                    if t == 0:
                        dve.wait_ge(s["kv_free"], g + 1)
                    dst = kf[:n, t, :]
                nc.vector.tensor_tensor(dst, t1[:n, :], t2[:n, :], ALU.add).then_inc(s["qf_done"], 1)

            def row_max(g, i, components=(0, 1)):
                t = i % (NT + 1)
                n, nk = rows_of(t), keys(t)
                for c in components:
                    sc = scores(c, t, n)
                    dve.wait_ge(s["sc_done"], 2 * NU * g + 2 * i + c + 1)
                    if t < NT:
                        nc.vector.memset(sc[0:CHUNK, nk - CHUNK:nk], LOW)
                        dve.drain()
                    nc.vector.tensor_reduce(mx[:n, i % 2, c:c + 1], sc[:, 0:nk], AX.X, ALU.max)
                    dve.drain()
                    nc.vector.tensor_scalar(nb[:n, i % 2, c:c + 1], mx[:n, i % 2, c:c + 1], -QKS, None,
                                            ALU.mult).then_inc(s["mx_done"], 1)

            def difference(g, i):
                t = i % (NT + 1)
                n, nk = rows_of(t), keys(t)
                dve.wait_ge(s["ex_done"], 2 * NU * g + 2 * i + 2)
                nc.vector.reciprocal(rz[:n, :], Z[:n, i % 2, :])
                dve.drain()
                nc.vector.tensor_tensor(rl[:n, :], rz[:n, 1:2], keep["neglam"][:n, :], ALU.mult)
                dve.drain()
                nc.vector.tensor_scalar(p[:n, i % 2, 1, 0:nk], p[:n, i % 2, 1, 0:nk], rl[:n, 0:1], None, ALU.mult)
                dve.drain()
                nc.vector.scalar_tensor_tensor(out=p[:n, i % 2, 0, 0:nk], in0=p[:n, i % 2, 0, 0:nk],
                                               scalar=rz[:n, 0:1], in1=p[:n, i % 2, 1, 0:nk],
                                               op0=ALU.mult, op1=ALU.add).then_inc(s["a_done"], 1)

            def keep_weights(g, i):
                h, t = divmod(i, NT + 1)
                if t in range(4, NT):
                    cols = (t - 3) * P
                    dve.wait_ge(s["at_d"], 8 * g + 4 * h + t - 4 + 1)
                    nc.vector.tensor_copy(aT[:, i % 2, 4 * P:4 * P + cols], T[1][:, 0:cols]).then_inc(s["tc_d"], 1)

            def norm_out(g, i):
                n = rows_of(i % (NT + 1))
                dve.wait_ge(s["ot_done"], NU * g + i + 1)
                dve.wait_ge(s["ro_done"], NU * g + i + 1)
                nc.vector.scalar_tensor_tensor(out=on[:n, i % 2, :], in0=O[i % 2][:n, 0:VD],
                                               scalar=ro[:n, i % 2:i % 2 + 1], in1=keep["subg"][:n, :],
                                               op0=ALU.mult, op1=ALU.mult).then_inc(s["on_done"], 1)

            def conv_step(g, i):
                half, (kind, part) = i // 9, divmod(i % 9, 3)
                cc = g * 2 + half
                if kind == 1:
                    if part == 0:
                        nc.vector.tensor_copy(U[:, SEQ + 2:SEQ + 4], st[:, :, ds(cc, 1)].rearrange("p j c -> p (j c)"))
                    dve.wait_ge(s["c_done"], 3 * cc + 3)
                    hold(dve, s["f_done"], NU * g + i + 1, s["passed_dve"])
                    for (zp, up), (_, cp) in zip(part_pieces(F, U[:, 2:], part, 2), part_pieces(F, C, part, 0)):
                        last = nc.vector.tensor_tensor(up, zp, cp, ALU.mult)
                    last.then_inc(s["u_done"], 1)
                elif kind == 2:
                    if part == 0:
                        m = ROWS + 2
                        dve.drain()
                        nc.vector.tensor_scalar(Y[:], U[:, 0:m], cw[:, 0, ds(cc, 1)], None, ALU.mult)
                        for j in (1, 2):
                            dve.drain()
                            nc.vector.scalar_tensor_tensor(out=Y[:], in0=U[:, j:j + m], scalar=cw[:, j, ds(cc, 1)],
                                                           in1=Y[:], op0=ALU.mult, op1=ALU.add)
                        nc.vector.tensor_copy(tail[:, 0:2, ds(cc, 1)].rearrange("p j c -> p (j c)"), U[:, SEQ:SEQ + 2])
                        nc.vector.tensor_copy(tail[:, 2:4, ds(cc, 1)].rearrange("p j c -> p (j c)"),
                                              U[:, SEQ + 2 + DEC:SEQ + 4 + DEC])
                        dve.drain()
                    if i == 6:
                        hold(dve, s["clear"], g + 1, s["passed_dve"])
                    dve.wait_ge(s["f_done"], NU * g + i + 1)
                    for (zp, yp), (_, op) in zip(part_pieces(F, Y, part, 2), part_pieces(F, cvr[:, half, :], part, 0)):
                        last = nc.vector.tensor_tensor(op, zp, yp, ALU.mult)
                    last.then_inc(s["y_done"], 1)

            dve.sem_inc(s["y_done"], 3)
            nc.vector.memset(U[:, 0:2], 0.0)
            dve.sem_inc(s["tc_d"], 1)
            dve.sem_inc(s["tr_done"], 4)
            dve.sem_inc(s["ot_done"], 2)
            with dve.Fori(0, GROUPS) as g:
                for u in range(NU):
                    mean_square(g, u)
                    if u:
                        rotate(g, u - 1)
                rotate(g, NU - 1)
                row_max(g, 0)
                dve.wait_ge(s["consts"], 80)
                for i in range(NU):
                    difference(g, i)
                    before_sample = i % (NT + 1) == NT - 1
                    if i + 1 < NU:
                        row_max(g, i + 1, (0,) if before_sample else (0, 1))
                    if i:
                        norm_out(g, i - 1)
                    keep_weights(g, i)
                    conv_step(g, i)
                    if before_sample:
                        row_max(g, i + 1, (1,))
                norm_out(g, NU - 1)


def products(nc, pe, out, w, src, done):
    for part in range(3):
        for c in range(DC):
            last = nc.tensor.matmul(out[:, part, 0:PART], w[:, c, :], src[:, c, part * PART:(part + 1) * PART],
                                    start=(c == 0), stop=(c == DC - 1))
    last.then_inc(done, 1)


def thirds(ap):
    return ap.rearrange("p (a b) -> p a b", a=3)


def merge_weights(A, cc):
    srcs = (A["w_in"][0, :, ds(GACOL + cc * P, P)], A["w_conv_out"][0, :, ds(cc * P, P)],
            A["w_in"][0, :, ds(GBCOL + cc * P, P)], A["w_attn_out"][0, :, ds(cc * P, P)])
    return [a.rearrange("(c p) n -> p c n", p=P) for a in srcs]


def merge_places(keep, b):
    return parts(keep["low"], b * DC * D // 2, 4, DC * P).rearrange("p k (c n) -> p k c n", c=DC)


def load_w_o(eng, A, keep, h, done):
    eng.dma_start(w_o_half(keep, h), A["w_o"][0, :, h * 512:(h + 1) * 512]
                  .rearrange("(c p) n -> p c n", p=P)).then_inc(done, 16)


def w_o_half(keep, h):
    return parts(keep["low"], h * DC * D // 2, DC, D // 2)


def build_merge(nc, A, keep):
    with ExitStack() as ctx:
        def sb(name, shape, dt=F32):
            return ctx.enter_context(nc.sbuf_tensor("mg_" + name, shape, dt))

        s = semaphores(ctx, nc, "mg", "ahead a_in0 a_in1 b_in0 b_in1 consts cv_in o_in z_done g_done m_done "
                       "passed_act")
        w_in = [[s[f"a_in{b}"], s[f"b_in{b}"]] for b in range(2)]
        w = [merge_places(keep, b) for b in range(2)]
        bg = sb("bg", [P, 2, DC])
        G = sb("G", [P, 2, ROWS])
        M = sb("M", [P, 2, ROWS])
        Z = [ctx.enter_context(nc.psum_tensor(f"mg_Z{b}", [P, 3, 512], F32)) for b in range(2)]
        mixT = keep["mixT"]
        block = ctx.enter_context(nc.Block())

        @block.sync
        def _(sp):
            def load(cc, b, first=0):
                for k, src in enumerate(merge_weights(A, cc)[first:]):
                    sp.dma_start(w[b][:, first + k], src).then_inc(w_in[b][(first + k) // 2], 16)
            sp.sem_inc(w_in[0][0], 32)
            load(0, 0, 2)
            sp.dma_start(keep["cvT"][:], A["cv_t"].rearrange("(c p) r -> p c r", p=P)).then_inc(s["cv_in"], 16)
            sp.dma_start(keep["oT"][:], A["o_t"].rearrange("(c p) r -> p c r", p=P)).then_inc(s["o_in"], 16)
            load(1, 1)
            with sp.Fori(0, DC // 2 - 1) as pair:
                for b in range(2):
                    sp.wait_ge(s["z_done"], 8 * pair + 4 * (b + 1))
                    load(pair * 2 + 2 + b, b)
            sp.wait_ge(s["z_done"], 4 * (DC - 1))
            load_w_o(sp, A, keep, 0, s["ahead"])
            sp.wait_ge(s["ahead"], 16)

        @block.gpsimd
        def _(pool):
            with nc.allow_non_contiguous_dma(reason="gate biases, channels in partitions"):
                for j in range(2):
                    pool.dma_start(bg[:, j, :], A["b_gate"][0, j].rearrange("(c p) -> p c", p=P)).then_inc(s["consts"], 16)

        @block.tensor
        def _(pe):
            with pe.Fori(0, DC // 2) as pair:
                for b in range(2):
                    for k in range(4):
                        if k % 2 == 0:
                            pe.wait_ge(w_in[b][k // 2], 32 * (pair + 1))
                        if k % 2 == 0:
                            pe.wait_ge(s["g_done"], 4 * pair + 2 * b + k // 2 + 1)
                        else:
                            pe.wait_ge(s["m_done"], 4 * pair + 2 * b + k // 2 + 1)
                            pe.wait_ge(s["cv_in"] if k == 1 else s["o_in"], 16)
                        products(nc, pe, Z[k % 2], w[b][:, k], (keep["xnT"], keep["cvT"], keep["xnT"], keep["oT"])[k],
                                 s["z_done"])

        @block.scalar
        def _(act):
            act.sem_inc(s["g_done"], 1)
            act.wait_ge(s["consts"], 32)
            with act.Fori(0, DC // 2) as pair:
                for b in range(2):
                    for k in range(2):
                        act.wait_ge(s["m_done"], 4 * pair + max(2 * b + k, 1))
                        hold(act, s["z_done"], 8 * pair + 4 * b + 2 * k + 1, s["passed_act"])
                        nc.scalar.activation(thirds(G[:, k, :]), Z[0][:, :, 0:PART], ACT.Sigmoid,
                                             bias=bg[:, k, ds(pair * 2 + b, 1)]).then_inc(s["g_done"], 1)

        @block.vector
        def _(dve):
            dve.sem_inc(s["m_done"], 1)
            with dve.Fori(0, DC // 2) as pair:
                for b in range(2):
                    for k in range(2):
                        dve.wait_ge(s["g_done"], 4 * pair + 2 * b + k + 2)
                        dve.wait_ge(s["z_done"], 8 * pair + 4 * b + 2 * k + 2)
                        nc.vector.tensor_tensor(thirds(M[:, k, :]), Z[1][:, :, 0:PART], thirds(G[:, k, :]),
                                                ALU.mult).then_inc(s["m_done"], 1)
                    dve.drain()
                    nc.vector.tensor_tensor(mixT[:, ds(pair * 2 + b, 1), :], M[:, 0:1, :], M[:, 1:2, :], ALU.add)
                    dve.drain()


def build_peer(nc, A, keep):
    with ExitStack() as ctx:
        def sb(name, shape, dt=F32):
            return ctx.enter_context(nc.sbuf_tensor("pe_" + name, shape, dt))

        s = semaphores(ctx, nc, "pe", "wq_in0 wq_in1 wq_in2 wq_in3 consts setup sk_t x_in0 x_in1 y_out used_u "
                       "used_pe used_dve dg_done part_done idx_ready staged xsq r_done xn_done "
                       "xt_done xt_copied q_done qsq rq_done qn_done qt_done qt_copied s_done "
                       "s_copied s_used dots_done gelu_done wo_in xo_in0 xo_in1 xo_out z_done "
                       "x_done acc_done hw_done gm_done ge_done fin_p fin_d passed_pool passed_dve "
                       "passed_act passed_pe sel_done")
        landed = [ctx.enter_context(nc.semaphore(f"pe_landed{j}")) for j in range(RING)]
        x_in = [s["x_in0"], s["x_in1"]]
        wq = sb("wq", [P, DC, PQ])
        w_o = [w_o_half(keep, h) for h in range(2)]
        mixT = keep["mixT"]
        ring = [parts(keep["low"] if j < RING // 2 else keep["mix"], j % (RING // 2) * D, 1, D)[:, 0, :] for j in range(RING)]
        g2b = sb("g2b", [P, D])
        xa = sb("xa", [P, 2, D])
        xb = sb("xb", [P, 2, D])
        xT = sb("xT", [P, DC, P])
        qn = sb("qn", [P, PQ])
        qT = sb("qT", [P, 2 * PH, P])
        sc = sb("sc", [P, 2 * PH, NKEYS])
        skT = sb("skT", [P, 2, NKEYS])
        gq = sb("gq", [P, 2])
        sel = sb("sel", [P, DEC])
        iot = sb("iot", [P, TOPK])
        idx = sb("idx", [P, 2, SLOTS], U32)
        gw = sb("gw", [P, 2, SLOTS])
        idst = sb("idst", [P, 2, TOPK], U32)
        dots16 = sb("dots16", [P, TOPK])
        hd = sb("hd", [P, SLOTS])
        hw = sb("hw", [P, SLOTS])
        ssx = sb("ssx", [P, 1])
        rx = sb("rx", [P, 1])
        qs = sb("qs", [P, PH])
        rq = sb("rq", [P, PH])
        sw = sb("sw", [P, 2, NKEYS])
        sw2 = sb("sw2", [P, 2, NKEYS])
        m16 = sb("m16", [P, 2, TOPK])
        i16 = sb("i16", [P, 2, TOPK], U32)
        cand = sb("cand", [P, TOPK * TOPK])
        cand2 = sb("cand2", [P, TOPK * TOPK])
        b16 = sb("b16", [P, TOPK])
        j16 = sb("j16", [P, TOPK], U32)
        itop = sb("itop", [P, PH, 2 * TOPK])
        best = sb("best", [P, PH, TOPK])
        pick = sb("pick", [P, PH, TOPK], U32)
        pk = sb("pk", [P, 2, SLOTS], U32)
        pf = sb("pf", [P, 2, PH, TOPK])
        oh = sb("oh", [P, PH // 2, TOPK, TOPK])
        e01 = sb("e01", [P, 2, PH, TOPK])
        gs = sb("gs", [P, PH])
        stage = [xb[:, 1, :], xa[:, 1, :]]
        xo_in = [s["xo_in0"], s["xo_in1"]]
        dg = sb("dg", [P, DIAGS, P])
        ps = ctx.enter_context(nc.psum_tensor("pe_ps", [P, 8, 512], F32))
        acc = ps[:, 0:2, :].rearrange("p a b -> p (a b)")
        lo = ps[:, 2:4, :].rearrange("p a b -> p (a b)")
        hi = ps[:, 4:8, :].rearrange("p a b -> p (a b)")
        sums = [acc, hi[:, 0:D]]
        ident = keep["ident"]
        x1 = A["x1"]
        block = ctx.enter_context(nc.Block())

        @block.sync
        def _(sp):
            sp.dma_start(xa[:, 0, :], A["x_prompt"][0, 0:P, :]).then_inc(x_in[0], 16)
            load_w_o(sp, A, keep, 1, s["wo_in"])
            for t in (1, 2):
                sp.dma_start(stage[t % 2], A["x_prompt"][0, t * P:(t + 1) * P, :]).then_inc(xo_in[t % 2], 16)
            sp.dma_start(g2b[:], A["norm2_g"].to_broadcast([P, D])).then_inc(s["consts"], 16)
            sp.dma_start(sw[:], A["peer_subkeys"][0].rearrange("c k d -> k c d")).then_inc(s["consts"], 16)
            with nc.allow_non_contiguous_dma(reason="a vector, channels in partitions"):
                sp.dma_start(gq[:], A["peer_q_g"][0].rearrange("(c p) -> p c", p=P)).then_inc(s["consts"], 16)
            for q in range(4):
                sp.dma_start(wq[:, :, q * 512:(q + 1) * 512], A["peer_wq"][0, :, q * 512:(q + 1) * 512]
                             .rearrange("(c p) n -> p c n", p=P)).then_inc(s[f"wq_in{q}"], 16)

            for t in range(1, NT + 1):
                sp.wait_ge(s["x_done"], t + 1)
                copies = 1 if t < NT else P // DEC
                for q in range(copies):
                    sp.dma_start(x1[t * P + q * DEC:t * P + q * DEC + rows_of(t), :],
                                 stage[t % 2][:rows_of(t), :]).then_inc(s["xo_out"], 16)
                sp.wait_ge(s["xo_out"], 16 * (t - 1 + copies))
                if t + 2 <= NT:
                    src = A["x_sample"][0] if t + 2 == NT else A["x_prompt"][0, (t + 2) * P:(t + 3) * P, :]
                    sp.dma_start(stage[t % 2][:rows_of(t + 2), :], src).then_inc(xo_in[t % 2], 16)

            def tile(pair, b):
                t = pair * 2 + b
                sp.dma_start(xa[:, 1 - b, :], x1[ds((t + 1) * P, P), :]).then_inc(x_in[1 - b], 16)
                sp.wait_ge(s["acc_done"], t + 1)
                sp.dma_start(A["y_prompt"][0, ds(t * P, P), :], xa[:, b, :]).then_inc(s["y_out"], 16)
                hold(sp, s["y_out"], 16 * (t + 1), s["fin_p"])

            with sp.Fori(0, NT // 2) as pair:
                for b in range(2):
                    tile(pair, b)
            sp.wait_ge(s["acc_done"], NT + 2)
            sp.dma_start(A["y_sample"][0], xb[:DEC, 1, :]).then_inc(s["y_out"], 16)
            sp.wait_ge(s["y_out"], 16 * (NT + 1))

        @block.gpsimd
        def _(pool):
            nc.gpsimd.memset(sel[:], 0.0)
            nc.gpsimd.iota(idst[:, 0, :], pattern=[[1, TOPK]], base=0, channel_multiplier=0)
            pool.drain()
            nc.gpsimd.tensor_copy(iot[:], idst[:, 0, :]).then_inc(s["setup"], 1)
            for q in range(4):
                nc.gpsimd.affine_select(out=sel[:], in_=sel[:], compare_op=ALU.not_equal, fill=1.0, base=-DEC * q,
                                        pattern=[[-1, DEC]], channel_multiplier=1)
                pool.drain()
            pool.sem_inc(s["sel_done"], 1)

            def rsqrt(dst, src, done):
                nc.gpsimd.tensor_scalar(dst, src, EPS, None, ALU.add)
                pool.drain()
                nc.gpsimd.tensor_tensor(dst, dst, keep["mhalf"][:, 0:dst.shape[1]], ALU.pow).then_inc(done, 1)

            def norm_x(t):
                hold(pool, s["xsq"], t + 1, s["passed_pool"])
                rsqrt(rx[:], ssx[:], s["r_done"])

            def norm_q(t):
                hold(pool, s["qsq"], t + 1, s["passed_pool"])
                rsqrt(rq[:], qs[:], s["rq_done"])

            def gather(src, table, first, group, par, before):
                kind, old = before
                for j in range(RING):
                    if j % 4 == 0:
                        if kind == "u":
                            hold(pool, s["used_u"], old * RING + j + 4, s["passed_pool"])
                        elif j < BY_PE:
                            hold(pool, s["used_pe"], (old + 1) * BY_PE + j + 4, s["passed_pool"])
                        else:
                            hold(pool, s["used_dve"], (old + 1) * (RING - BY_PE) + j + 4 - BY_PE, s["passed_pool"])
                    if j == 0:
                        nc.gpsimd.tensor_copy(idst[:, par, :], src[:, ds(first, TOPK)]).then_inc(s["staged"], 1)
                        hold(pool, s["staged"], group + 1, s["passed_pool"])
                    nc.gpsimd.indirect_dma_start(
                        out=ring[j], out_offset=None, in_=table,
                        in_offset=bass.IndirectOffsetOnAxis(ap=idst[:, par, j:j + 1], axis=0)).then_inc(landed[j], 16)

            def pair_of(t, b, name, h, before):
                phase = 0 if name == "peer_u" else 8
                for par in range(2):
                    kind, old = before if par == 0 else (name[-1], t * 8 + h)
                    gather(idx[:, b, :], A[name][0], (h + par) * TOPK, t * 16 + phase + h + par, par, (kind, old))

            def tile(pair, b):
                t = pair * 2 + b
                hold(pool, s["idx_ready"], 2 * t + 1, s["passed_pool"])
                pair_of(t, b, "peer_u", 0, ("v", t * 8 - 1))
                norm_x(t + 1)
                with pool.Fori(1, 3) as k:
                    hold(pool, s["idx_ready"], 2 * t + k, s["passed_pool"])
                    pair_of(t, b, "peer_u", k * 2, ("u", t * 8 + k * 2 - 1))
                norm_q(t + 1)
                pair_of(t, b, "peer_u", 6, ("u", t * 8 + 5))
                pair_of(t, b, "peer_v", 0, ("u", t * 8 + 7))
                with pool.Fori(1, 4) as k:
                    pair_of(t, b, "peer_v", k * 2, ("v", t * 8 + k * 2 - 1))

            norm_x(0)
            norm_q(0)
            pool.wait_ge(s["z_done"], NT + 1)
            with pool.Fori(0, NT // 2) as pair:
                for b in range(2):
                    tile(pair, b)
            pool.wait_ge(s["idx_ready"], 2 * (NT + 1) + 1)
            for k, before in enumerate((("v", NT * 8 - 1), ("u", NT * 8), ("u", NT * 8 + 1), ("v", NT * 8))):
                gather(idx[:, 1, :], A["peer_u"][0] if k < 2 else A["peer_v"][0], (k % 2) * TOPK, NT * 16 + k, k % 2,
                       before)

        @block.tensor
        def _(pe):
            def project(t):
                if t >= 2:
                    pe.wait_ge(s["x_done"], t - 1)
                if t == 3:
                    pe.wait_ge(s["s_copied"], 1)
                n = rows_of(t)
                for h in range(2):
                    if t == 0 and h == 1:
                        pe.wait_ge(s["wo_in"], 16)
                    for c in range(DC):
                        last = nc.tensor.matmul(sums[t % 2][:n, h * 512:(h + 1) * 512], mixT[:, c, t * P:t * P + n],
                                                w_o[h][:, c, :], start=(c == 0), stop=(c == DC - 1))
                last.then_inc(s["z_done"], 1)

            def query(t, meanwhile=None):
                hold(pe, s["xn_done"], t + 1, s["passed_pe"])
                for c in range(DC):
                    last = nc.tensor.transpose(lo[:, c * P:(c + 1) * P], xb_of(t)[:, c * P:(c + 1) * P], ident[:])
                last.then_inc(s["xt_done"], 1)
                hold(pe, s["xt_copied"], t + 1, s["passed_pe"])
                for q in range(4):
                    if meanwhile:
                        pe.wait_ge(s[f"wq_in{q}"], 16)
                    for c in range(DC):
                        last = nc.tensor.matmul(hi[:, q * 512:(q + 1) * 512], xT[:, c, :], wq[:, c, q * 512:(q + 1) * 512],
                                                start=(c == 0), stop=(c == DC - 1))
                last.then_inc(s["q_done"], 1)
                if meanwhile:
                    meanwhile()
                hold(pe, s["qn_done"], t + 1, s["passed_pe"])
                for m in range(2):
                    if m:
                        hold(pe, s["qt_copied"], 2 * t + 1, s["passed_pe"])
                    for k in range(PH):
                        last = nc.tensor.transpose(lo[:, k * P:(k + 1) * P],
                                                   qn[:, (m * PH + k) * P:(m * PH + k + 1) * P], ident[:])
                    last.then_inc(s["qt_done"], 1)
                hold(pe, s["qt_copied"], 2 * t + 2, s["passed_pe"])
                for k in range(2 * PH):
                    last = nc.tensor.matmul(hi[:, k * P:(k + 1) * P], qT[:, k, :], skT[:, k % 2, :], start=True, stop=True)
                last.then_inc(s["s_done"], 1)

            half = [0]

            def xb_of(t):
                return xb[:, half[0], :]

            project(0)
            pe.wait_ge(s["consts"], 48)
            for c in range(2):
                last = nc.tensor.transpose(ps[:, 7, c * P:(c + 1) * P], sw[:, c, :], ident[:])
            last.then_inc(s["sk_t"], 1)
            project(1)
            pe.wait_ge(s["setup"], 2)
            pe.wait_ge(s["x_done"], 2)
            query(0, lambda: project(2))
            for t in range(3, NT + 1):
                project(t)
            pe.wait_ge(s["x_done"], NT + 1)

            def weigh(t, h, group, start, stop):
                for j in range(BY_PE):
                    hold(pe, s["dg_done"], (t * 8 + h) * BY_PE + j + 1, s["passed_pe"])
                    pe.wait_ge(landed[j], 16 * (group + 1))
                    for k in range(2):
                        last = nc.tensor.matmul(acc[:, k * 512:(k + 1) * 512], dg[:, j % DIAGS, :],
                                                ring[j][:, k * 512:(k + 1) * 512], start=start and j == 0,
                                                stop=stop and j == BY_PE - 1, skip_group_check=True)
                    last.then_inc(s["used_pe"], 1)

            pe.sem_inc(s["used_pe"], BY_PE)
            with pe.Fori(0, NT // 2) as pair:
                for b in range(2):
                    t = pair * 2 + b
                    half[0] = 1 - b
                    query(t + 1)
                    hold(pe, s["part_done"], t + 1, s["passed_pe"])
                    weigh(t, 0, t * 16 + 8, True, False)
                    with pe.Fori(1, 7) as h:
                        weigh(t, h, t * 16 + 8 + h, False, False)
                    weigh(t, 7, t * 16 + 15, False, True)
            pe.wait_ge(s["part_done"], NT + 1)
            for k in range(2):
                weigh(NT, k, NT * 16 + 2 + k, k == 0, k == 1)
            pe.wait_ge(s["sel_done"], 1)
            pe.wait_ge(s["acc_done"], NT + 1)
            for h in range(2):
                last = nc.tensor.matmul(lo[:DEC, h * 512:(h + 1) * 512], sel[:], xa[:, 1, h * 512:(h + 1) * 512],
                                        start=True, stop=True)
            last.then_inc(s["fin_d"], 1)

        @block.scalar
        def _(act):
            act.wait_ge(s["sk_t"], 1)
            nc.scalar.copy(skT[:].rearrange("p c k -> p (c k)"), ps[:, 7, 0:2 * P]).then_inc(s["setup"], 1)

            def query(t, b, turn):
                act.wait_ge(x_in[b], 16 * turn)
                nc.scalar.activation(xT[:].rearrange("p c k -> p (c k)"), xa[:, b, :], ACT.Square, scale=D ** -0.5,
                                     accum_out=ssx[:]).then_inc(s["xsq"], 1)
                act.drain()
                act.wait_ge(s["xt_done"], t + 1)
                for k in range(2):
                    last = nc.scalar.copy(xT[:, 4 * k:4 * k + 4, :].rearrange("p c k -> p (c k)"), lo[:, k * 512:(k + 1) * 512])
                last.then_inc(s["xt_copied"], 1)
                act.wait_ge(s["q_done"], t + 1)
                for h in range(PH):
                    last = nc.scalar.activation(qn[:, h * 256:(h + 1) * 256], hi[:, h * 256:(h + 1) * 256], ACT.Square,
                                                scale=256 ** -0.5, accum_out=qs[:, h:h + 1])
                last.then_inc(s["qsq"], 1)
                act.drain()
                act.wait_ge(s["rq_done"], t + 1)
                for h in range(PH):
                    last = nc.scalar.activation(qn[:, h * 256:(h + 1) * 256], hi[:, h * 256:(h + 1) * 256], ACT.Copy,
                                                scale=rq[:, h:h + 1])
                last.then_inc(s["qn_done"], 1)
                lo4 = lo.rearrange("p (h c r) -> p h c r", h=PH // 2, c=2)
                qT4 = qT[:].rearrange("p (h c) r -> p h c r", c=2)
                for m in range(2):
                    act.wait_ge(s["qt_done"], 2 * t + m + 1)
                    for k in range(2):
                        for c in range(2):
                            last = nc.scalar.activation(qT4[:, 4 * m + 2 * k:4 * m + 2 * k + 2, c, :],
                                                        lo4[:, 2 * k:2 * k + 2, c, :], ACT.Copy, scale=gq[:, c:c + 1])
                    last.then_inc(s["qt_copied"], 1)
                act.wait_ge(s["s_used"], t + 1)
                act.wait_ge(s["s_done"], t + 1)
                for k in range(4):
                    last = nc.scalar.copy(sc[:, 4 * k:4 * k + 4, :].rearrange("p c k -> p (c k)"), hi[:, k * 512:(k + 1) * 512])
                last.then_inc(s["s_copied"], 1)

            def gelu(t, n):
                act.wait_ge(s["dots_done"], t + 1)
                nc.scalar.activation(hw[:, 0:n], hd[:, 0:n], ACT.Gelu).then_inc(s["gelu_done"], 1)

            def diagonals(t, h):
                for j in range(BY_PE):
                    hold(act, s["used_pe"], (t * 8 + h + 1) * BY_PE + j + 1 - DIAGS, s["passed_act"])
                    nc.scalar.activation(dg[:, j % DIAGS, :], ident[:], ACT.Copy,
                                         scale=hw[:, ds(h * TOPK + j, 1)]).then_inc(s["dg_done"], 1)

            def exps(t):
                act.wait_ge(s["gm_done"], t + 1)
                nc.scalar.activation(best[:], best[:], ACT.Exp).then_inc(s["ge_done"], 1)

            act.wait_ge(s["consts"], 48)
            act.wait_ge(s["x_done"], 1)
            query(0, 0, 1)
            exps(0)
            with act.Fori(0, NT // 2) as pair:
                for b in range(2):
                    t = pair * 2 + b
                    query(t + 1, 1 - b, pair + 1 + b)
                    gelu(t, SLOTS)
                    hold(act, s["hw_done"], t + 1, s["passed_act"])
                    with act.Fori(0, PH) as h:
                        diagonals(t, h)
                    exps(t + 1)
            gelu(NT, DEC)
            act.wait_ge(s["hw_done"], NT + 1)
            for k in range(2):
                diagonals(NT, k)

        @block.vector
        def _(dve):
            def top16(val, ind, src, spare):
                n = len(src)
                for k in range(n):
                    nc.vector.max(val[k][:, 0:8], src[k])
                dve.drain()
                for k in range(n):
                    nc.vector.max_index(ind[k][:, 0:8], val[k][:, 0:8], src[k])
                    nc.vector.match_replace(spare[k], val[k][:, 0:8], src[k], LOW)
                dve.drain()
                for k in range(n):
                    nc.vector.max(val[k][:, 8:16], spare[k])
                dve.drain()
                for k in range(n):
                    nc.vector.max_index(ind[k][:, 8:16], val[k][:, 8:16], spare[k])
                dve.drain()

            def topk(h):
                nc.vector.tensor_copy(sw[:], sc[:, ds(h * 2, 2), :])
                dve.drain()
                top16([m16[:, c, :] for c in range(2)], [i16[:, c, :] for c in range(2)],
                      [sw[:, c, :] for c in range(2)], [sw2[:, c, :] for c in range(2)])
                nc.vector.tensor_tensor(cand[:].rearrange("p (i j) -> p i j", i=TOPK),
                                        m16[:, 0, :].unsqueeze(2).to_broadcast([P, TOPK, TOPK]),
                                        m16[:, 1:2, :].to_broadcast([P, TOPK, TOPK]), ALU.add)
                nc.vector.tensor_copy(itop[:, ds(h, 1), :].rearrange("p h k -> p (h k)"),
                                      i16[:].rearrange("p c k -> p (c k)"))
                dve.drain()
                top16([b16[:]], [j16[:]], [cand[:]], [cand2[:]])
                nc.vector.tensor_copy(best[:, ds(h, 1), :].rearrange("p h k -> p (h k)"), b16[:])
                nc.vector.tensor_copy(pick[:, ds(h, 1), :].rearrange("p h k -> p (h k)"), j16[:])

            def places(heads):
                flat = pick[:, heads, :].rearrange("p h k -> p (h k)")
                slots = slice(heads.start * TOPK, heads.stop * TOPK)
                nc.vector.tensor_scalar(pk[:, 0, slots], flat, 4, None, ALU.logical_shift_right)
                nc.vector.tensor_scalar(pk[:, 1, slots], flat, TOPK - 1, None, ALU.bitwise_and)
                dve.drain()
                for c in range(2):
                    nc.vector.tensor_copy(pf[:, c, heads, :].rearrange("p h k -> p (h k)"), pk[:, c, slots])
                dve.drain()

            def keys_of(part):
                hs = slice(part * PH // 2, (part + 1) * PH // 2)
                shape = [P, PH // 2, TOPK, TOPK]
                for c in range(2):
                    nc.vector.tensor_tensor(oh[:], pf[:, c, hs, :].unsqueeze(3).to_broadcast(shape),
                                            iot[:].unsqueeze(1).unsqueeze(1).to_broadcast(shape), ALU.is_equal)
                    dve.drain()
                    nc.vector.tensor_tensor(oh[:], oh[:], itop[:, hs, c * TOPK:(c + 1) * TOPK].unsqueeze(2)
                                            .to_broadcast(shape), ALU.mult)
                    dve.drain()
                    nc.vector.tensor_reduce(e01[:, c, hs, :], oh[:], AX.X, ALU.add)
                    dve.drain()

            def experts(b, part):
                hs = slice(part * PH // 2, (part + 1) * PH // 2)
                nc.vector.scalar_tensor_tensor(out=idx[:, b, part * SLOTS // 2:(part + 1) * SLOTS // 2],
                                               in0=e01[:, 0, hs].rearrange("p h k -> p (h k)"),
                                               scalar=float(NKEYS), in1=e01[:, 1, hs].rearrange("p h k -> p (h k)"),
                                               op0=ALU.mult, op1=ALU.add).then_inc(s["idx_ready"], 1)

            def softmax_start():
                nc.vector.tensor_copy(gs[:], best[:, :, 0])
                dve.drain()
                nc.vector.tensor_tensor(best[:], best[:], gs[:].unsqueeze(2).to_broadcast([P, PH, TOPK]),
                                        ALU.subtract).then_inc(s["gm_done"], 1)

            def softmax_end(t, b):
                dve.wait_ge(s["ge_done"], t + 1)
                nc.vector.tensor_reduce(gs[:], best[:], AX.X, ALU.add)
                dve.drain()
                nc.vector.reciprocal(gs[:], gs[:])
                dve.drain()
                nc.vector.tensor_tensor(gw[:, b, :].rearrange("p (h k) -> p h k", h=PH), best[:],
                                        gs[:].unsqueeze(2).to_broadcast([P, PH, TOPK]), ALU.mult)
                dve.drain()

            def norm_x(t, b):
                hold(dve, s["r_done"], t + 1, s["passed_dve"])
                nc.vector.scalar_tensor_tensor(out=xb[:, b, :], in0=xa[:, b, :], scalar=rx[:, 0:1], in1=g2b[:],
                                               op0=ALU.mult, op1=ALU.mult).then_inc(s["xn_done"], 1)

            def dot_steps(b, group, first):
                for j in range(RING):
                    dve.wait_ge(landed[j], 16 * (group + 1))
                    nc.vector.tensor_tensor_reduce(out=ring[j], in0=ring[j], in1=xb[:, b, :], scale=1.0,
                                                   scalar=0.0, op0=ALU.mult, op1=ALU.add,
                                                   accum_out=dots16[:, j:j + 1]).then_inc(s["used_u"], 1)
                dve.drain()
                nc.vector.tensor_copy(hd[:, ds(first, TOPK)], dots16[:])
                dve.drain()

            def sum_steps(t, h, b, group, first):
                n = RING - BY_PE
                for j in range(BY_PE, RING):
                    dve.wait_ge(landed[j], 16 * (group + 1))
                    dve.wait_ge(s["used_dve"], (t * 8 + h + 1) * n + j - BY_PE)
                    nc.vector.scalar_tensor_tensor(out=xa[:, b, :], in0=ring[j], scalar=hw[:, ds(first + j, 1)],
                                                   in1=xa[:, b, :], op0=ALU.mult, op1=ALU.add).then_inc(s["used_dve"], 1)

            def weights(t, b, n):
                nc.vector.drain().then_inc(s["dots_done"], 1)
                dve.wait_ge(s["gelu_done"], t + 1)
                nc.vector.tensor_tensor(hw[:, 0:n], hw[:, 0:n], gw[:, b, 0:n], ALU.mult)
                nc.vector.drain().then_inc(s["hw_done"], 1)

            def add_part(t, b):
                groups = 2 if isinstance(t, int) and t == NT else PH
                hold(dve, s["used_pe"], (t * 8 + groups + 1) * BY_PE, s["passed_dve"])
                dve.drain()
                nc.vector.tensor_tensor(xa[:, b, :], acc[:, :], xa[:, b, :], ALU.add).then_inc(s["part_done"], 1)
                nc.vector.drain().then_inc(s["acc_done"], 1)

            def tile(pair, b):
                t = pair * 2 + b
                nb = 1 - b
                with dve.Fori(0, 2) as h:
                    dot_steps(b, t * 16 + h, h * TOPK)
                norm_x(t + 1, nb)
                with dve.Fori(2, 8) as h:
                    dot_steps(b, t * 16 + h, h * TOPK)
                weights(t, b, SLOTS)
                hold(dve, s["s_copied"], t + 2, s["passed_dve"])
                with dve.Fori(0, 6) as h:
                    sum_steps(t, h, b, t * 16 + 8 + h, h * TOPK)
                    topk(h)
                for h in (6, 7):
                    topk(h)
                dve.drain()
                dve.sem_inc(s["s_used"], 1)
                softmax_start()
                sum_steps(t, 6, b, t * 16 + 14, 6 * TOPK)
                places(slice(0, PH))
                for part in range(2):
                    keys_of(part)
                    experts(nb, part)
                sum_steps(t, 7, b, t * 16 + 15, 7 * TOPK)
                add_part(t, b)
                softmax_end(t + 1, nb)

            def add_x(t, turn, b, n):
                dve.wait_ge(xo_in[b], 16 * turn)
                dve.wait_ge(s["z_done"], t + 1)
                nc.vector.tensor_tensor(stage[b][:n, :], sums[b][:n, :], stage[b][:n, :], ALU.add).then_inc(s["x_done"], 1)

            dve.wait_ge(s["consts"], 48)
            dve.sem_inc(s["s_used"], 1)
            dve.sem_inc(s["used_dve"], RING - BY_PE)
            dve.sem_inc(s["part_done"], 1)
            dve.wait_ge(x_in[0], 16)
            dve.wait_ge(s["z_done"], 1)
            nc.vector.tensor_tensor(xa[:, 0, :], sums[0], xa[:, 0, :], ALU.add).then_inc(s["x_done"], 1)
            dve.drain()
            norm_x(0, 0)
            add_x(1, 1, 1, P)
            add_x(2, 1, 0, P)
            dve.wait_ge(s["setup"], 2)
            dve.wait_ge(s["s_copied"], 1)
            with dve.Fori(0, 2) as pair:
                for b in range(2):
                    h = pair * 2 + b
                    topk(h)
                    add_x(h + 3, pair + 2, 1 - b, P)
            dve.drain()
            places(slice(0, PH // 2))
            keys_of(0)
            experts(0, 0)
            for h in (4, 5):
                topk(h)
                add_x(h + 3, 4, (h + 3) % 2, rows_of(h + 3))
            with dve.Fori(6, PH) as h:
                topk(h)
            dve.drain()
            dve.sem_inc(s["s_used"], 1)
            softmax_start()
            places(slice(PH // 2, PH))
            keys_of(1)
            experts(0, 1)
            softmax_end(0, 0)
            with dve.Fori(0, NT // 2) as pair:
                for b in range(2):
                    tile(pair, b)
            for q in range(4):
                quad = slice(q * DEC, (q + 1) * DEC)
                nc.vector.tensor_copy(idx[quad, 1, 0:DEC], idx[quad, 0, quad])
                nc.vector.tensor_copy(gw[quad, 1, 0:DEC], gw[quad, 0, quad])
            nc.vector.drain().then_inc(s["idx_ready"], 1)
            for k in range(2):
                dot_steps(0, NT * 16 + k, k * TOPK)
            dve.wait_ge(s["fin_p"], NT)
            nc.vector.memset(xa[:, 1, :], 0.0)
            weights(NT, 1, DEC)
            for k in range(2):
                sum_steps(NT, k, 1, NT * 16 + 2 + k, k * TOPK)
            add_part(NT, 1)
            dve.wait_ge(s["fin_d"], 1)
            nc.vector.tensor_tensor(xb[:DEC, 1, :], lo[:DEC, 0:D], xa[:DEC, 0, :], ALU.add)
            nc.vector.drain().then_inc(s["acc_done"], 1)


def build(nc, A):
    with ExitStack() as ctx:
        def sb(name, shape, dt=F32):
            return ctx.enter_context(nc.sbuf_tensor(name, shape, dt))

        keep = {"ident": sb("ident", [P, P]), "mhalf": sb("mhalf", [P, 8]), "mix": sb("mix", [P, DC * ROWS]),
                "low": sb("low", [P, DC * D])}
        keep["mixT"] = parts(keep["mix"], 0, DC, ROWS)
        with ExitStack() as trunk:
            def tsb(name, shape):
                return trunk.enter_context(nc.sbuf_tensor(name, shape, F32))

            keep["xnT"] = tsb("xnT", [P, DC, ROWS])
            with ExitStack() as tables:
                for name in ("qa", "qb", "ka", "kb"):
                    keep[name] = tables.enter_context(nc.sbuf_tensor(name, [P, NT + 1, HD], F32))
                keep["subg"] = tables.enter_context(nc.sbuf_tensor("subg", [P, VD], F32))
                keep["neglam"] = tables.enter_context(nc.sbuf_tensor("neglam", [P, 1], F32))
                keep["w"] = [parts(keep["mix"], k * DC * GW, DC, GW) for k in range(3)]
                keep["kc"] = parts(keep["mix"], 3 * DC * GW, DC, GW)
                build_norm1(nc, A, keep)
                build_attention(nc, A, keep)
            keep["cvT"] = tsb("cvT", [P, DC, ROWS])
            keep["oT"] = tsb("oT", [P, DC, ROWS])
            build_merge(nc, A, keep)
        build_peer(nc, A, keep)


INPUTS = ["x_prompt", "x_sample", "cache_k", "cache_v", "state_conv", "norm1_g", "w_in", "b_gate", "conv_w",
          "q_norm_g", "k_norm_g", "lam_q1", "lam_k1", "lam_q2", "lam_k2", "subln_g", "w_conv_out", "w_attn_out",
          "w_o", "norm2_g", "peer_wq", "peer_q_g", "peer_subkeys", "peer_u", "peer_v"]
OUTPUTS = {"y_prompt": ((1, SEQ, D), (1, SEQ, D)),
           "y_sample": ((1, DEC, D), (1, DEC, D)),
           "k_prompt": ((SEQ, D), (1, 1, SEQ, HEADS, 2, HD)),
           "v_prompt": ((SEQ, D), (1, 1, SEQ, HEADS, VD)),
           "conv_prompt": ((2, D), (1, 1, 2, D)),
           "k_sample": ((DEC, D), (1, 1, DEC, HEADS, 2, HD)),
           "v_sample": ((DEC, D), (1, 1, DEC, HEADS, VD)),
           "conv_sample": ((2, D), (1, 1, 2, D))}


def rope_tables():
    half = HD // 2
    inv = np.float32(10000.0) ** (-np.arange(half, dtype=np.float32) / np.float32(half))
    ang = np.arange((NT + 1) * P, dtype=np.float32)[:, None] * inv[None, :].astype(np.float32)
    cos, sin = np.cos(ang), np.sin(ang)
    out = []
    for table in (np.concatenate([cos, cos], 1), np.concatenate([-sin, sin], 1)):
        out.append(np.ascontiguousarray(table.reshape(NT + 1, P, HD).transpose(1, 0, 2)).astype(np.float32))
    return out


def program(nc, in_arrays):
    A = {}
    for name, a in in_arrays.items():
        A[name] = nc.dram_tensor(f"in_{name}", a.shape, mybir.dt.from_np(a.dtype), kind="ExternalInput").ap()
    for name, (shape, _) in OUTPUTS.items():
        A[name] = nc.dram_tensor(f"out_{name}", shape, F32, kind="ExternalOutput").ap()
    for name in ("cv_t", "o_t"):
        A[name] = nc.dram_tensor(name, (D, ROWS), F32, kind="Internal").ap()
    A["x1"] = nc.dram_tensor("x1_rows", (SEQ + P, D), F32, kind="Internal").ap()
    build(nc, A)


def kernel(**inputs):
    import concourse.bacc as bacc
    from concourse.bass_utils import run_bass_kernel_spmd as run
    arrays = {name: np.ascontiguousarray(inputs[name]) for name in INPUTS}
    for name in ("cache_k", "cache_v"):
        arrays[name] = arrays[name].reshape(PAST, D)
    arrays["rope_cos"], arrays["rope_sin"] = rope_tables()
    nc = bacc.Bacc("TRN2", target_bir_lowering=False, num_devices=1)
    program(nc, arrays)
    r = run(nc, [{f"in_{k}": v for k, v in arrays.items()}], core_ids=[0])
    got = r.results[0]
    return tuple(np.asarray(got[f"out_{name}"]).reshape(shape) for name, (_, shape) in OUTPUTS.items())
```
